# Optimizing a Trainium2 kernel written in Bass

```python
import jax, jax.numpy as jnp
from jax import lax
import numpy as np

D_MODEL = 1024
BATCH = 1
SEQ = 128
DEPTH = 2
DEC_BATCH = 1
DEC_SEQ = 256
PAST_LEN = 128

GRID_W = 64
N_EVEN = (DEPTH + 1) // 2
N_ODD = DEPTH // 2
NA_HEADS = 8
NA_HD = 64
NA_W = NA_HEADS * NA_HD
NA_WIN_R = 8
NA_WIN_C = 16
FN_GROUPS = 4
FN_GW = 128
FN_W = FN_GROUPS * FN_GW
MIX0_IN = 3 * NA_W + FN_W
MIX0_OUT = NA_W + FN_W
HG_HEADS = 8
HG_DK = 128
HG_DV = 128
HG_KW = HG_HEADS * HG_DK
HG_VW = HG_HEADS * HG_DV
MIX1_IN = 3 * HG_KW + 2 * HG_VW
HG_CHUNK = 32
D_FF = 2816
N_SUB = 3
N_MOD = 3 * N_SUB
Q_BLOCK = 128
EPS = 1e-6

kernel_name = 'hybrid_natten_fnet_hgrn2_prefix_step'

def rms_norm(x, g):
    xf = x.astype(jnp.float32)
    y = xf * lax.rsqrt(jnp.mean(xf * xf, axis=-1, keepdims=True) + EPS)
    return (y * g.astype(jnp.float32)).astype(x.dtype)

def ada_params(cond, w, b):
    m = jax.nn.silu(cond) @ w + b
    return m.reshape(cond.shape[0], N_MOD, D_MODEL)

def modulated_norm(x, g, mod, j):
    shift = mod[:, 3 * j][:, None, :]
    scale = mod[:, 3 * j + 1][:, None, :]
    return rms_norm(x, g) * (1 + scale) + shift

def gate_of(mod, j):
    return mod[:, 3 * j + 2][:, None, :]

def swiglu(h, w1, w2):
    a, b = jnp.split(h @ w1, 2, axis=-1)
    return (jax.nn.silu(a) * b) @ w2

def half_ffn(x, mod, j, g, w1, w2):
    return x + 0.5 * gate_of(mod, j) * swiglu(modulated_norm(x, g, mod, j), w1, w2)

def context_attention(q, k, v):
    B, S, H, hd = q.shape
    nb = S // Q_BLOCK
    scale = hd ** -0.5
    qb = q.reshape(B, nb, Q_BLOCK, H, hd).transpose(1, 0, 2, 3, 4)

    def block(qi):
        s = jnp.einsum('bqhd,bkhd->bhqk', qi, k).astype(jnp.float32) * scale
        p = jax.nn.softmax(s, axis=-1).astype(v.dtype)
        return jnp.einsum('bhqk,bkhd->bqhd', p, v)

    o = lax.map(block, qb)
    return o.transpose(1, 0, 2, 3, 4).reshape(B, S, H * hd)

def neighbourhood_attention(q, k, v, ck, cv, rpb):
    B, T, H, hd = q.shape
    rows = T // GRID_W
    kr = min(NA_WIN_R, rows)
    kc = NA_WIN_C
    scale = hd ** -0.5
    qg = q.reshape(B, rows, GRID_W, H, hd)
    kg = k.reshape(B, rows, GRID_W, H, hd)
    vg = v.reshape(B, rows, GRID_W, H, hd)
    cols = jnp.arange(GRID_W)
    col_start = jnp.clip(cols - kc // 2, 0, GRID_W - kc)
    col_idx = col_start[:, None] + jnp.arange(kc)[None, :]
    col_bias_idx = col_idx - cols[:, None] + (NA_WIN_C - 1)

    def one_row(r):
        r0 = jnp.clip(r - kr // 2, 0, rows - kr)
        kb = lax.dynamic_slice_in_dim(kg, r0, kr, axis=1)
        vb = lax.dynamic_slice_in_dim(vg, r0, kr, axis=1)
        kw = kb[:, :, col_idx]
        vw = vb[:, :, col_idx]
        qr = lax.dynamic_index_in_dim(qg, r, axis=1, keepdims=False)
        row_bias_idx = r0 + jnp.arange(kr) - r + (NA_WIN_R - 1)
        bias = rpb[:, row_bias_idx[None, :, None], col_bias_idx[:, None, :]]
        s_loc = jnp.einsum('bwhd,brwkhd->bhwrk', qr, kw).astype(jnp.float32) * scale
        s_loc = (s_loc + bias[None].astype(jnp.float32)).reshape(B, H, GRID_W, kr * kc)
        s_ctx = jnp.einsum('bwhd,bphd->bhwp', qr, ck).astype(jnp.float32) * scale
        p = jax.nn.softmax(jnp.concatenate([s_loc, s_ctx], axis=-1), axis=-1).astype(v.dtype)
        p_loc = p[..., :kr * kc].reshape(B, H, GRID_W, kr, kc)
        p_ctx = p[..., kr * kc:]
        return (jnp.einsum('bhwrk,brwkhd->bwhd', p_loc, vw)
                + jnp.einsum('bhwp,bphd->bwhd', p_ctx, cv))

    o = lax.map(one_row, jnp.arange(rows))
    return o.transpose(1, 0, 2, 3, 4).reshape(B, T, H * hd)

def fourier_mix(u):
    B, T, _ = u.shape
    ug = u.reshape(B, T, FN_GROUPS, FN_GW).astype(jnp.float32)
    y = jnp.fft.fft2(ug, axes=(1, 3), norm='ortho').real
    return y.reshape(B, T, FN_W).astype(u.dtype)

def even_mixer(hp, hs, ck, cv, w_in, w_out, rpb):
    def split(u):
        B, T, _ = u.shape
        q, k, v, f = jnp.split(u, [NA_W, 2 * NA_W, 3 * NA_W], axis=-1)
        heads = lambda a: a.reshape(B, T, NA_HEADS, NA_HD)
        return heads(q), heads(k), heads(v), f

    qp, kp, vp, fp = split(hp @ w_in)
    qs, ks, vs, fs = split(hs @ w_in)
    yp = jnp.concatenate([context_attention(qp, kp, vp), fourier_mix(fp)], axis=-1) @ w_out
    ys = jnp.concatenate([neighbourhood_attention(qs, ks, vs, ck, cv, rpb), fourier_mix(fs)], axis=-1) @ w_out
    return yp, ys, kp, vp

def hgrn2_gates(z, lb):
    z = z.astype(jnp.float32)
    log_f = jnp.logaddexp(jnp.log(lb), jnp.log1p(-lb) + jax.nn.log_sigmoid(z))
    k = (1.0 - lb) * jax.nn.sigmoid(-z)
    return k, log_f

def gla_chunk_scan(q, k, v, log_f, s0):
    B, T, H, DK = q.shape
    C = HG_CHUNK
    n = T // C
    to_chunks = lambda a: a.reshape(B, n, C, H, a.shape[-1]).transpose(1, 0, 3, 2, 4)
    mask = jnp.tril(jnp.ones((C, C), dtype=bool))[:, :, None]

    def step(S, inp):
        qi, ki, vi, gi = inp
        b = jnp.cumsum(gi, axis=2)
        o_inter = jnp.einsum('bhck,bhkv->bhcv', qi * jnp.exp(b), S)
        diff = b[:, :, :, None, :] - b[:, :, None, :, :]
        decay = jnp.exp(jnp.where(mask, diff, -jnp.inf))
        A = jnp.einsum('bhtk,bhsk,bhtsk->bhts', qi, ki, decay)
        o_intra = jnp.einsum('bhts,bhsv->bhtv', A, vi)
        b_last = b[:, :, -1:, :]
        S_new = (S * jnp.exp(b_last[:, :, 0, :, None])
                 + jnp.einsum('bhsk,bhsv->bhkv', ki * jnp.exp(b_last - b), vi))
        return S_new, o_inter + o_intra

    S_fin, o = lax.scan(step, s0.astype(jnp.float32),
                        (to_chunks(q), to_chunks(k), to_chunks(v), to_chunks(log_f)))
    o = o.transpose(1, 0, 3, 2, 4).reshape(B, T, H, v.shape[-1])
    return o, S_fin

def hgrn2_bidir(u, lb_l, s0, norm_g):
    B, T, _ = u.shape
    q, zf, zb, v, g = jnp.split(u, [HG_KW, 2 * HG_KW, 3 * HG_KW, 3 * HG_KW + HG_VW], axis=-1)
    heads_k = lambda a: a.reshape(B, T, HG_HEADS, HG_DK)
    q = heads_k(q).astype(jnp.float32)
    v = v.reshape(B, T, HG_HEADS, HG_DV).astype(jnp.float32)
    kf, gf = hgrn2_gates(heads_k(zf), lb_l[0].reshape(HG_HEADS, HG_DK))
    kb, gb = hgrn2_gates(heads_k(zb), lb_l[1].reshape(HG_HEADS, HG_DK))
    rev = lambda a: jnp.flip(a, axis=1)
    o_f, s_f = gla_chunk_scan(q, kf, v, gf, s0[:, 0])
    o_b, s_b = gla_chunk_scan(rev(q), rev(kb), rev(v), rev(gb), s0[:, 1])
    o = o_f + rev(o_b)
    o = rms_norm(o, norm_g) * jax.nn.silu(g.reshape(B, T, HG_HEADS, HG_DV).astype(jnp.float32))
    return o.reshape(B, T, HG_VW).astype(u.dtype), jnp.stack([s_f, s_b], axis=1)

def setup_inputs(seed: int = 0) -> dict:
    key = jax.random.key(seed)
    ks = jax.random.split(key, 20)
    nrm = lambda k, shape, s: jax.random.normal(k, shape, jnp.float32) * s
    return {
        'x_prompt': nrm(ks[0], (BATCH, SEQ, D_MODEL), 1.0),
        'x_sample': nrm(ks[1], (DEC_BATCH, DEC_SEQ, D_MODEL), 1.0),
        'cache_k': nrm(ks[2], (DEC_BATCH, N_EVEN, PAST_LEN, NA_HEADS, NA_HD), 1.0),
        'cache_v': nrm(ks[3], (DEC_BATCH, N_EVEN, PAST_LEN, NA_HEADS, NA_HD), 1.0),
        'state_hgrn': nrm(ks[4], (DEC_BATCH, N_ODD, 2, HG_HEADS, HG_DK, HG_DV), 0.5),
        'c': nrm(ks[5], (DEC_BATCH, D_MODEL), 1.0),
        'c_ctx': nrm(ks[6], (D_MODEL,), 1.0),
        'ada_w': nrm(ks[7], (DEPTH, D_MODEL, N_MOD * D_MODEL), 0.5 * D_MODEL ** -0.5),
        'ada_b': nrm(ks[8], (DEPTH, N_MOD * D_MODEL), 0.01),
        'norm_g': 1.0 + nrm(ks[9], (DEPTH, N_SUB, D_MODEL), 0.01),
        'ffn_w1': nrm(ks[10], (DEPTH, 2, D_MODEL, 2 * D_FF), D_MODEL ** -0.5),
        'ffn_w2': nrm(ks[11], (DEPTH, 2, D_FF, D_MODEL), D_FF ** -0.5),
        'mix0_w_in': nrm(ks[12], (N_EVEN, D_MODEL, MIX0_IN), D_MODEL ** -0.5),
        'mix0_w_out': nrm(ks[13], (N_EVEN, MIX0_OUT, D_MODEL), MIX0_OUT ** -0.5),
        'na_rpb': nrm(ks[14], (N_EVEN, NA_HEADS, 2 * NA_WIN_R - 1, 2 * NA_WIN_C - 1), 0.02),
        'mix1_w_in': nrm(ks[15], (N_ODD, D_MODEL, MIX1_IN), D_MODEL ** -0.5),
        'mix1_w_out': nrm(ks[16], (N_ODD, HG_VW, D_MODEL), HG_VW ** -0.5),
        'hg_lb_logits': nrm(ks[17], (DEPTH, 2, HG_KW), 1.0),
        'hg_norm_g': 1.0 + nrm(ks[18], (N_ODD, HG_DV), 0.01),
        'norm_f': 1.0 + nrm(ks[19], (D_MODEL,), 0.01),
    }

def reference(x_prompt, x_sample, cache_k, cache_v, state_hgrn, c, c_ctx, ada_w, ada_b, norm_g,
              ffn_w1, ffn_w2, mix0_w_in, mix0_w_out, na_rpb, mix1_w_in, mix1_w_out,
              hg_lb_logits, hg_norm_g, norm_f):
    xp, xs = x_prompt, x_sample
    bp = xp.shape[0]
    sm = jax.nn.softmax(hg_lb_logits.astype(jnp.float32), axis=0)
    lb_all = jnp.cumsum(sm, axis=0) - sm[0]
    new_k, new_v, new_s = [], [], []
    for l in range(DEPTH):
        mp = ada_params(c_ctx[None, :], ada_w[l], ada_b[l])
        ms = ada_params(c, ada_w[l], ada_b[l])
        xp = half_ffn(xp, mp, 0, norm_g[l, 0], ffn_w1[l, 0], ffn_w2[l, 0])
        xs = half_ffn(xs, ms, 0, norm_g[l, 0], ffn_w1[l, 0], ffn_w2[l, 0])
        hp = modulated_norm(xp, norm_g[l, 1], mp, 1)
        hs = modulated_norm(xs, norm_g[l, 1], ms, 1)
        if l % 2 == 0:
            e = l // 2
            yp, ys, kp, vp = even_mixer(hp, hs, cache_k[:, e], cache_v[:, e],
                                        mix0_w_in[e], mix0_w_out[e], na_rpb[e])
            new_k.append(kp)
            new_v.append(vp)
        else:
            o = l // 2
            zero = jnp.zeros((bp, 2, HG_HEADS, HG_DK, HG_DV), jnp.float32)
            yp, sp = hgrn2_bidir(hp @ mix1_w_in[o], lb_all[l], zero, hg_norm_g[o])
            ys, _ = hgrn2_bidir(hs @ mix1_w_in[o], lb_all[l], state_hgrn[:, o], hg_norm_g[o])
            yp = yp @ mix1_w_out[o]
            ys = ys @ mix1_w_out[o]
            new_s.append(sp.astype(x_prompt.dtype))
        xp = xp + gate_of(mp, 1) * yp
        xs = xs + gate_of(ms, 1) * ys
        xp = half_ffn(xp, mp, 2, norm_g[l, 2], ffn_w1[l, 1], ffn_w2[l, 1])
        xs = half_ffn(xs, ms, 2, norm_g[l, 2], ffn_w1[l, 1], ffn_w2[l, 1])
    y_prompt = rms_norm(xp, norm_f)
    y_sample = rms_norm(xs, norm_f)
    new_cache_k = jnp.stack(new_k, axis=1)
    new_cache_v = jnp.stack(new_v, axis=1)
    new_state_hgrn = jnp.stack(new_s, axis=1)
    return (y_prompt, y_sample, new_cache_k, new_cache_v, new_state_hgrn)


_drawn_inputs = setup_inputs


def setup_inputs(seed=0):
    import zlib

    import numpy as np

    out = dict(_drawn_inputs(seed))
    spreads = {}
    factors = {'cache_k': 3.006, 'norm_g': 5.409, 'na_rpb': 21.652, 'hg_norm_g': 54.905, 'norm_f': 31.187}
    for name, (base, spread) in spreads.items():
        noise = np.random.default_rng([zlib.crc32(name.encode()), seed]).standard_normal(out[name].shape)
        drawn = base * np.exp(spread * noise) if base else spread * noise
        out[name] = __import__('jax').numpy.asarray(drawn.astype(out[name].dtype))
    for name, factor in factors.items():
        out[name] = (out[name] * factor).astype(out[name].dtype)
    return out
```

```python
from contextlib import ExitStack

import numpy as np

import concourse.bass as bass
from concourse import mybir

F32 = mybir.dt.float32
F32R = mybir.dt.float32r
ALU = mybir.AluOpType
ACT = mybir.ActivationFunctionType
AX = mybir.AxisListType.X

P = 128
D = 1024
KT = D // P
NP_, NS_ = 128, 256
T = NP_ + NS_
TB = T // P
DEPTH = 2
DFF = 2816
FT = DFF // P
HALF = FT // 2
NMOD = 9
GRID_W, ROWS = 64, 4
HEADS, HD = 8, 64
NAW = HEADS * HD
RPB_R, RPB_C = 15, 31
WIN_C = 16
SLOTS = 6
HG_HEADS = 8
LEVELS = 7
EPS = 1e-6
NEG = -1e30
GROUPS = ((0, 0, NP_), (1, NP_, T))

V_ADAB = 0
V_NG = V_ADAB + DEPTH * NMOD * KT
V_NF = V_NG + DEPTH * 3 * KT
V_LB = V_NF + KT
V_HG = V_LB + DEPTH * 2 * HG_HEADS
V_C = V_HG + 1
V_END = V_C + 2 * KT

C_ID = 0
C_ANTI = C_ID + P
C_MEAN = C_ANTI + P
C_MEANH = C_MEAN + P
C_MASK = C_MEANH + P
C_DG = C_MASK + 2 * LEVELS * 64
C_DT256 = C_DG + 2 * P
C_DT128 = C_DT256 + 4 * NS_
C_END = C_DT128 + 2 * NP_


def shape_constants():
    c = np.zeros((P, C_END), np.float64)
    c[:, C_ID:C_ID + P] = np.eye(P)
    c[:, C_ANTI:C_ANTI + P] = np.eye(P)[::-1]
    c[:, C_MEAN:C_MEAN + P] = 1.0 / D
    c[:, C_MEANH:C_MEANH + P] = 1.0 / P
    s = np.arange(P)[:, None]
    j = np.arange(64)[None, :]
    for back in range(2):
        for lv in range(LEVELS):
            w = 1 << lv
            m = (s // (2 * w) == j // w) & (((s % (2 * w)) >= w) == bool(back))
            at = C_MASK + (back * LEVELS + lv) * 64
            c[:, at:at + 64] = m
    n = np.arange(P)
    ang = 2 * np.pi * ((n[:, None] * n[None, :]) % P) / P
    c[:, C_DG:C_DG + P] = np.cos(ang)
    c[:, C_DG + P:C_DG + 2 * P] = np.sin(ang)
    c[:, C_DT128:C_DT128 + P] = np.cos(ang) / np.sqrt(NP_ * P)
    c[:, C_DT128 + P:C_DT128 + 2 * P] = -np.sin(ang) / np.sqrt(NP_ * P)
    k = np.arange(NS_)
    for tt in range(2):
        a = 2 * np.pi * (((tt * P + n)[:, None] * k[None, :]) % NS_) / NS_
        at = C_DT256 + tt * 2 * NS_
        c[:, at:at + NS_] = np.cos(a) / np.sqrt(NS_ * P)
        c[:, at + NS_:at + 2 * NS_] = -np.sin(a) / np.sqrt(NS_ * P)
    return c.astype(np.float32)


STAGES = [("ffn", 0, 0), ("mix0", 0, 1), ("ffn", 0, 2), ("ffn", 1, 0), ("mix1", 1, 1), ("ffn", 1, 2)]
N_CHUNKS = {"ffn": FT + 2 * KT, "mix0": 12, "mix1": 24}
BASE = [sum(N_CHUNKS[k] for k, _, _ in STAGES[:s]) for s in range(len(STAGES) + 1)]


def chunk_size(n):
    for s, (kind, _, _) in enumerate(STAGES):
        if BASE[s] <= n < BASE[s + 1]:
            return HALF * P if kind == "ffn" and n - BASE[s] >= FT else KT * 256
    return 0


def build(nc, x_prompt, x_sample, cache_k, cache_v, state_hgrn, c, c_ctx, ada_w, ada_b, norm_g,
          ffn_w1, ffn_w2, mix0_w_in, mix0_w_out, na_rpb, mix1_w_in, mix1_w_out,
          hg_lb_logits, hg_norm_g, norm_f, consts,
          y_prompt, y_sample, new_k, new_v, new_state):
    n_stages = len(STAGES)
    total_chunks = BASE[n_stages]
    with ExitStack() as ctx:
        def sb(name, shape, dt=F32, stack=ctx):
            return stack.enter_context(nc.sbuf_tensor(name, shape, dt))

        def sem(name):
            return ctx.enter_context(nc.semaphore(name))

        ps = [ctx.enter_context(nc.psum_tensor(f"bank{i}", [P, 512], F32)) for i in range(8)]

        w_raw = [sb(f"w_raw{i}", [P, KT * 256]) for i in range(2)]
        w_hi = [sb(f"w_hi{i}", [P, KT * 256], F32R) for i in range(2)]
        w_lo = [sb(f"w_lo{i}", [P, KT * 256], F32R) for i in range(2)]
        x = sb("x", [P, KT, T])
        xh = sb("xh", [P, KT, T], F32R)
        xl = sb("xl", [P, KT, T], F32R)
        xf = sb("xf", [P, KT, T])
        ada = [sb(f"ada{i}", [P, KT, P]) for i in range(2)]
        cst = sb("cst", [P, C_END])
        vrow = sb("vrow", [P, 2, P])
        vt = sb("vt", [P, 2 * P])
        cond = sb("cond", [P, KT, 2])
        prm = sb("prm", [P, DEPTH * NMOD * KT, 2])
        mod_a = sb("mod_a", [P, KT, 2])
        hgate = sb("hgate", [P, KT, 2])
        rr = sb("rr", [P, T])
        lb = sb("lb", [P, 6, 2 * HG_HEADS])
        gg_base = nc.sbuf_base
        gg = sb("gg", [P, FT, 2, T], F32R)
        ident = cst[:, C_ID:C_ID + P]
        anti = cst[:, C_ANTI:C_ANTI + P]

        silu_a = [sb(f"silu_a{i}", [P, T]) for i in range(2)]
        g_raw = [sb(f"g_raw{i}", [P, T]) for i in range(2)]

        arena = [gg_base + KT * 2 * T * 4]

        def at(name, shape, dt=F32):
            t = nc.alloc_sbuf_tensor_at(name, shape, dt, offset=arena[0])
            arena[0] += int(np.prod(shape[1:])) * 4
            return t

        start = arena[0]
        qT = at("qT", [P, 4, T])
        kT = at("kT", [P, 4, T])
        vtok = at("vtok", [P, TB, NAW])
        fT = at("fT", [P, 4, T])
        bias = at("bias", [P, HEADS, SLOTS, GRID_W])
        ck = at("ck", [P, NAW])
        ckT = at("ckT", [P, 4, P])
        cv = at("cv", [P, NAW])
        nk = at("nk", [P, NAW])
        prob = [at(f"prob{i}", [P, T]) for i in range(2)]
        probT = [at(f"probT{i}", [P, T]) for i in range(2)]
        smax = at("smax", [P, 24])
        ssum = at("ssum", [P, 24])
        srec = at("srec", [P, 24])
        ab = xf[:, :, :].rearrange("p k t -> p (k t)").rearrange("p (b g c) -> p b g c", b=TB, g=4)
        arena[0] = start
        hq = at("hq", [P, 2, T])
        hp_ = [at(f"hp{d}", [P, 2, T]) for d in range(2)]
        hk = [at(f"hk{d}", [P, 2, T]) for d in range(2)]
        hr = [at(f"hr{d}", [P, T]) for d in range(2)]
        sg = at("sg", [P, 2, T])
        hv = at("hv", [P, TB, 2 * P])
        hm = [at(f"hm{i}", [P, LEVELS, T]) for i in range(2)]
        gm = [at(f"gm{i}", [P, LEVELS * 64]) for i in range(2)]
        gd = at("gd", [P, T])
        ktok = at("ktok", [P, 2, P])
        st0 = at("st0", [P, 2, 2, P])
        st1 = at("st1", [P, P])
        sfin = at("sfin", [P, 4, P])
        osq = at("osq", [P, T])
        orr = at("orr", [P, T])
        oy = at("oy", [P, T])
        qi = [xf[:, 2 * i, :] for i in range(2)]
        ki = [xf[:, 2 * i + 1, :] for i in range(2)]

        s_cst = sem("cst_loaded")
        s_vrow = sem("vrow_loaded")
        s_xin = sem("x_loaded")
        s_kv = sem("cache_loaded")
        s_rpb = sem("rpb_loaded")
        s_raw = [sem(f"w_loaded{i}") for i in range(2)]
        s_hi = sem("w_hi_done")
        s_lo = sem("w_lo_done")
        s_used = sem("w_used")
        s_adaw = [sem(f"ada_loaded{i}") for i in range(2)]
        s_adamm = sem("ada_summed")
        s_ada = sem("ada_done")
        s_vT = sem("vectors_turned")
        s_vt = sem("vectors_ready")
        s_cond = sem("cond_ready")
        s_lbe = sem("lb_exp")
        s_xT = sem("x_turned")
        s_x = sem("x_ready")
        s_sq = sem("squares_ready")
        s_ms = sem("mean_ready")
        s_rs = sem("root_ready")
        s_mod = sem("mod_ready")
        s_xr = sem("x_scaled")
        s_xh = sem("xh_ready")
        s_xl = sem("xl_ready")
        s_sa = sem("silu_ready")
        s_gm = sem("g_ready")
        s_gh = sem("gh_ready")
        s_gl = sem("gl_ready")
        s_pj = sem("projection_copied")
        s_bias = sem("bias_ready")
        s_ckT = sem("ck_turned")
        s_ckv = sem("ck_ready")
        s_nkT = sem("nk_turned")
        s_nk = sem("nk_ready")
        s_fo = sem("fourier_summed")
        s_foe = sem("fourier_copied")
        s_foh = sem("fourier_hi")
        s_sc = sem("scores_ready")
        s_mx = sem("max_ready")
        s_exp = sem("exp_ready")
        s_pn = sem("probs_ready")
        s_tr = sem("probs_turned")
        s_pt = sem("probsT_ready")
        s_pv = sem("attn_summed")
        s_ath = sem("attn_hi")
        s_at = sem("attn_copied")
        s_un = sem("unit_ready")
        s_ud = sem("unit_used")
        s_gb = sem("bank_filled")
        s_ge = sem("bank_copied")
        s_osq = sem("o_squared")
        s_ort = sem("o_root")
        s_oy = sem("o_ready")
        s_oh = sem("o_hi")
        s_yo = sem("o_done")
        s_st0 = sem("state_loaded")
        s_sf = sem("state_ready")
        s_dv = sem("vector_step")
        s_yT = sem("y_turned")
        s_yo2 = sem("y_copied")
        s_ol = sem("o_lo")
        s_sfo = [sem(f"state_stored{i}") for i in range(4)]
        s_out = sem("stored")
        s_cache_out = sem("new_cache_stored")

        norm_col = [V_NG + (layer * 3 + j) * KT for _, layer, j in STAGES] + [V_NF]

        def prm_tile(s, which):
            _, layer, j = STAGES[s]
            return (layer * NMOD + 3 * j + which) * KT

        PAIRS_FIRST, PAIRS = 8, 12
        first_pair = [PAIRS_FIRST + PAIRS * s for s in range(n_stages)]
        stage_pairs = [PAIRS] * (n_stages - 1) + [4]
        ffn_no = {s: i for i, s in enumerate([s for s in range(n_stages) if STAGES[s][0] == "ffn"])}
        pj0 = {1: 0, 4: 8}
        gh0 = {s: FT * i for s, i in ffn_no.items()}
        units = [(pair, h2, what) for pair in range(4) for h2 in range(2) for what in range(3)]

        def y_stage(tb):
            return w_raw[tb // 2][:, tb % 2 * D:(tb % 2 + 1) * D]

        def blk(ap, lv):
            return ap.rearrange("p (b two w) -> p b two w", two=2, w=1 << lv)

        block = ctx.enter_context(nc.Block())

        @block.sync
        def _(sp):
            xin = xf[:, :, :].rearrange("p k t -> p (k t)").rearrange("p (b d) -> p b d", b=TB)
            flat = ada_b.rearrange("l (r q) -> (l r) q", q=P)
            sp.dma_start(vrow[:, 0, :], flat[0:P, :]).then_inc(s_vrow, 16)
            sp.dma_start(vrow[0:16, 1, :], flat[P:P + 16, :]).then_inc(s_vrow, 16)
            sp.dma_start(vrow[16:64, 1, :], norm_g.rearrange("l j (k q) -> (l j k) q", q=P)).then_inc(s_vrow, 16)
            sp.dma_start(vrow[64:72, 1, :], norm_f.rearrange("(k q) -> k q", q=P)).then_inc(s_vrow, 16)
            sp.dma_start(vrow[72:104, 1, :], hg_lb_logits.rearrange("l e (k q) -> (l e k) q", q=P)).then_inc(s_vrow, 16)
            sp.dma_start(vrow[104:105, 1, :], hg_norm_g).then_inc(s_vrow, 16)
            sp.dma_start(vrow[105:113, 1, :], c_ctx.rearrange("(k q) -> k q", q=P)).then_inc(s_vrow, 16)
            sp.dma_start(vrow[113:121, 1, :], c.rearrange("a (k q) -> (a k) q", q=P)).then_inc(s_vrow, 16)
            sp.dma_start(cst[:, :], consts).then_inc(s_cst, 16)
            sp.dma_start(xin[:, 0, :], x_prompt[0]).then_inc(s_xin, 16)
            sp.dma_start(xin[:, 1:3, :], x_sample[0].rearrange("(b p) d -> p b d", p=P)).then_inc(s_xin, 16)

            def load(n, parts):
                if not (isinstance(n, int) and n < 2):
                    sp.wait_ge(s_lo, n - 1)
                for dst, src in parts:
                    sp.dma_start(dst, src).then_inc(s_raw[dst_slot[0]], 16)

            dst_slot = [0]

            def load_w1(n, slot, w, col):
                dst_slot[0] = slot
                raw = w_raw[slot][:, :].rearrange("p (h k n) -> p h k n", h=2, k=KT)
                src = w.rearrange("(k p) n -> p k n", p=P)
                load(n, [(raw[:, h], src[:, :, bass.ds(h * DFF + col, P)]) for h in range(2)])

            def load_w2(n, slot, w, half, col):
                dst_slot[0] = slot
                raw = w_raw[slot][:, 0:HALF * P].rearrange("p (k n) -> p k n", k=HALF)
                src = w.rearrange("(k p) n -> p k n", p=P)
                load(n, [(raw[:, a:b], src[:, half * HALF + a:half * HALF + b, bass.ds(col, P)])
                         for a, b in ((0, 6), (6, HALF))])

            def load_square(n, slot, w, col):
                dst_slot[0] = slot
                raw = w_raw[slot][:, :].rearrange("p (k n) -> p k n", k=KT)
                src = w.rearrange("(k p) n -> p k n", p=P)
                load(n, [(raw[:, a:a + 4], src[:, a:a + 4, bass.ds(col, 256)]) for a in (0, 4)])

            for s, (kind, layer, j) in enumerate(STAGES):
                n0 = BASE[s]
                if kind == "ffn":
                    w1, w2 = ffn_w1[layer, j // 2], ffn_w2[layer, j // 2]
                    first = 0
                    if s == 0:
                        for slot in range(2):
                            load_w1(slot, slot, w1, slot * P)
                        first = 1
                    with sp.Fori(first, FT // 2) as i:
                        for slot in range(2):
                            load_w1(n0 + 2 * i + slot, slot, w1, (2 * i + slot) * P)
                    with sp.Fori(0, KT) as i:
                        for half in range(2):
                            load_w2(n0 + FT + 2 * i + half, half, w2, half, i * P)
                else:
                    w_in, w_out = (mix0_w_in, mix0_w_out) if kind == "mix0" else (mix1_w_in, mix1_w_out)
                    n_in = N_CHUNKS[kind] - 4
                    if kind == "mix0":
                        cols = [256 * i for i in range(n_in)]
                    else:
                        cols = [part * D + pair * 256 for pair in range(4) for part in range(5)]
                    for i, col in enumerate(cols):
                        load_square(n0 + i, i % 2, w_in[0], col)
                    for i in range(4):
                        load_square(n0 + n_in + i, i % 2, w_out[0], 256 * i)
            for tb in range(TB):
                sp.wait_ge(s_yo2, 2 * (tb + 1))
                dst = y_prompt[0] if tb == 0 else y_sample[0, (tb - 1) * P:tb * P, :]
                sp.dma_start(dst, y_stage(tb)).then_inc(s_out, 16)
            sp.wait_ge(s_out, 16 * TB)
            sp.wait_ge(s_cache_out, 32)
            for slot in s_sfo:
                sp.wait_ge(slot, 16 * 4)

        @block.gpsimd
        def _(pool):
            def load_ada(u, slot, layer, col):
                if not (isinstance(u, int) and u < 2):
                    pool.wait_ge(s_adamm, u - 1)
                src = ada_w[layer].rearrange("(k p) n -> p k n", p=P)
                pool.dma_start(ada[slot][:, :, :], src[:, :, bass.ds(col, P)]).then_inc(s_adaw[slot], 16)

            def load_pairs(first, end):
                layer = first * 2 // (NMOD * KT)
                with pool.Fori(first, end) as i:
                    for slot in range(2):
                        load_ada(2 * i + slot, slot, layer, (2 * i + slot - layer * NMOD * KT) * P)

            load_ada(0, 0, 0, 0)
            load_ada(1, 1, 0, P)
            load_pairs(1, first_pair[1] + 1)
            pool.wait_ge(s_used, BASE[1])
            pool.dma_start(ck[:, :], cache_k[0, 0].rearrange("t h d -> t (h d)")).then_inc(s_kv, 16)
            pool.dma_start(cv[:, :], cache_v[0, 0].rearrange("t h d -> t (h d)")).then_inc(s_kv, 16)
            for half in range(2):
                for head in range(HEADS):
                    row = head * RPB_R + ROWS + half
                    src = bass.AP(tensor=na_rpb.tensor, offset=row * RPB_C + WIN_C - 1 - (GRID_W - 1),
                                  ap=[[1, GRID_W], [RPB_C, SLOTS], [1, GRID_W]])
                    pool.dma_start(bias[half * GRID_W:(half + 1) * GRID_W, head, :, :], src).then_inc(s_rpb, 16)
            pool.wait_ge(s_rpb, 16 * 2 * HEADS)
            n_sel = 0
            for half in range(2):
                for lo_, hi_, base, sign in ((0, GRID_W - WIN_C, WIN_C // 2 - (GRID_W - 1), 1),
                                             (WIN_C, GRID_W, GRID_W - 1 + WIN_C // 2 - 1 - WIN_C, -1)):
                    b = bias[half * GRID_W:(half + 1) * GRID_W, :, :, lo_:hi_].rearrange("p h r c -> p (h r) c")
                    if n_sel % 2:
                        pool.wait_ge(s_bias, n_sel)
                    nc.gpsimd.affine_select(out=b, in_=b, compare_op=ALU.is_ge, fill=NEG, base=base,
                                            pattern=[[0, HEADS * SLOTS], [sign, hi_ - lo_]],
                                            channel_multiplier=sign).then_inc(s_bias, 1)
                    n_sel += 1
            load_pairs(first_pair[1] + 1, NMOD * KT // 2)
            load_pairs(NMOD * KT // 2, NMOD * KT)

        @block.scalar
        def _(act):
            def split_hi(n, half_n, slot, size):
                act.wait_ge(s_raw[slot], 32 * half_n + 32)
                nc.scalar.activation(w_hi[slot][:, 0:size], w_raw[slot][:, 0:size], ACT.Copy).then_inc(s_hi, 1)

            act.wait_ge(s_vt, 1)
            nc.scalar.activation(cond[:, :, :].rearrange("p k c -> p c k"),
                                 vt[:, V_C:V_END].rearrange("p (c k) -> p c k", c=2), ACT.Silu).then_inc(s_cond, 1)
            for i in range(2):
                split_hi(i, 0, i, chunk_size(i))
            act.wait_ge(s_mod, 1)
            nc.scalar.activation(lb[:, 1:3, :], lb[:, 1:3, :], ACT.Exp).then_inc(s_lbe, 1)

            def norm(m):
                for k in range(KT):
                    act.wait_ge(s_x, 8 * m + k + 1 if m else KT)
                    nc.scalar.activation(xf[:, k, :], x[:, k, :], ACT.Square).then_inc(s_sq, 1)
                act.wait_ge(s_ms, m + 1)
                nc.scalar.activation(rr[:, :], ps[6][:, 0:T], ACT.Sqrt, bias=lb[:, 5, 0:1]).then_inc(s_rs, 1)
                if m == n_stages:
                    return
                act.wait_ge(s_mod, m + 2)
                for k in range(KT):
                    act.wait_ge(s_xr, 8 * m + k + 1)
                    for cnd, a, b in GROUPS:
                        last = nc.scalar.activation(xh[:, k, a:b], xf[:, k, a:b], ACT.Identity,
                                                    scale=mod_a[:, k, cnd:cnd + 1],
                                                    bias=prm[:, prm_tile(m, 0) + k, cnd:cnd + 1])
                    last.then_inc(s_xh, 1)

            def ffn(s):
                n0, g0 = BASE[s], gh0[s]

                def w1_tile(cc, slot, cbase, size):
                    n = n0 + cc
                    act.wait_ge(s_used, n + 1)
                    nc.scalar.activation(silu_a[slot][:, :], ps[2 * slot][:, 0:T], ACT.Silu).then_inc(s_sa, 1)
                    split_hi(n + 2, n0 // 2 + cbase + 1, slot, size)
                    act.wait_ge(s_gm, g0 + cc + 1)
                    nc.scalar.activation(gg[:, bass.ds(cc, 1), 0, :].rearrange("p a t -> p (a t)"),
                                         g_raw[slot][:, :], ACT.Copy).then_inc(s_gh, 1)

                with act.Fori(0, FT // 2 - 1) as i:
                    for slot in range(2):
                        w1_tile(2 * i + slot, slot, i, KT * 256)
                for slot in range(2):
                    w1_tile(FT - 2 + slot, slot, FT // 2 - 1, HALF * P)

                def w2_tile(d, size):
                    for half in range(2):
                        n = n0 + FT + 2 * d + half
                        act.wait_ge(s_used, n + 1)
                        if size:
                            split_hi(n + 2, (n0 + FT) // 2 + d + 1, half, size)

                with act.Fori(0, KT - 1) as d:
                    w2_tile(d, HALF * P)
                w2_tile(KT - 1, chunk_size(BASE[s + 1]))

            def next_hi(n):
                if chunk_size(n + 2):
                    split_hi(n + 2, n // 2 + 1, n % 2, chunk_size(n + 2))

            def mix0(s):
                n0 = BASE[s]
                for i in range(8):
                    n = n0 + i
                    slot = i % 2
                    act.wait_ge(s_used, n + 1)
                    b0, b1 = ps[2 * slot], ps[2 * slot + 1]
                    part, half = i // 2, i % 2
                    if part == 2:
                        nc.scalar.activation(vtok[:, 0:2, half * 256:half * 256 + 256],
                                             b0[:, :].rearrange("p (b n) -> p b n", b=2), ACT.Copy)
                        last = nc.scalar.activation(vtok[:, 2, half * 256:half * 256 + 256], b1[:, 0:256], ACT.Copy)
                    else:
                        dst = (qT, kT, None, fT)[part]
                        scale = HD ** -0.5 if part == 0 else 1.0
                        nc.scalar.activation(dst[:, 2 * half, :], b0[:, 0:T], ACT.Copy, scale=scale)
                        last = nc.scalar.activation(dst[:, 2 * half + 1, :], b1[:, 0:T], ACT.Copy, scale=scale)
                    last.then_inc(s_pj, 1)
                    next_hi(n)
                act.wait_ge(s_pj, pj0[s] + 8)
                act.dma_start(new_v[0, 0].rearrange("t h d -> t (h d)"), vtok[:, 0, :]).then_inc(s_cache_out, 16)
                act.wait_ge(s_nk, 1)
                act.dma_start(new_k[0, 0].rearrange("t h d -> t (h d)"), nk[:, :]).then_inc(s_cache_out, 16)
                for g in range(4):
                    act.wait_ge(s_fo, 6 + g + 1)
                    nc.scalar.activation(gg[:, 4 + g, 0, :], ps[(6 + g) % 4][:, 0:T], ACT.Copy).then_inc(s_foh, 1)

                def attn_hi(pair):
                    act.wait_ge(s_pv, 6 * pair + 6)
                    nc.scalar.activation(gg[:, pair, 0, :], ps[4 + pair % 2][:, 0:T], ACT.Copy).then_inc(s_ath, 1)

                def exps(u):
                    width = NP_ if units[u][2] == 0 else T
                    act.wait_ge(s_mx, u + 1)
                    if u >= 2:
                        act.wait_ge(s_tr, u - 1)
                    nc.scalar.activation(prob[u % 2][:, 0:width], ps[u % 2][:, 0:width], ACT.Exp,
                                         bias=smax[:, u:u + 1], accum_out=ssum[:, u:u + 1]).then_inc(s_exp, 1)

                def copy_probs(u):
                    width = NP_ if units[u][2] == 0 else T
                    act.wait_ge(s_tr, u + 1)
                    if u >= 2:
                        act.wait_ge(s_pv, u - 1)
                    nc.scalar.activation(probT[u % 2][:, 0:width], ps[2 + u % 2][:, 0:width],
                                         ACT.Copy).then_inc(s_pt, 1)

                exps(0)
                for u in range(24):
                    if u + 1 < 24:
                        exps(u + 1)
                    copy_probs(u)
                    if u % 6 == 1 and u > 6:
                        attn_hi(u // 6 - 1)
                attn_hi(3)
                act.wait_ge(s_cache_out, 32)
                for i in range(4):
                    act.wait_ge(s_used, n0 + 8 + i + 1)
                    next_hi(n0 + 8 + i)

            def mix1(s):
                n0 = BASE[s]
                for pair in range(4):
                    for part in range(5):
                        i = pair * 5 + part
                        n = n0 + i
                        slot = i % 2
                        b = (ps[2 * slot], ps[2 * slot + 1])
                        act.wait_ge(s_used, n + 1)
                        for h2 in range(2):
                            bank = b[h2][:, 0:T]
                            if part == 0:
                                last = nc.scalar.activation(hq[:, h2, :], bank, ACT.Copy)
                            elif part in (1, 2):
                                nc.scalar.activation(hp_[part - 1][:, h2, :], bank, ACT.Sigmoid)
                                last = nc.scalar.activation(hk[part - 1][:, h2, :], bank, ACT.Sigmoid, scale=-1.0)
                            elif part == 3 and h2 == 0:
                                nc.scalar.activation(hv[:, 0:2, :], b[0][:, :].rearrange("p (b n) -> p b n", b=2), ACT.Copy)
                                last = nc.scalar.activation(hv[:, 2, :], b[1][:, 0:256], ACT.Copy)
                            elif part == 4:
                                last = nc.scalar.activation(sg[:, h2, :], bank, ACT.Silu)
                        last.then_inc(s_pj, 1)
                        if part == 0:
                            for d in range(2):
                                act.dma_start(st0[:, d, :, :],
                                              state_hgrn[0, 0, d, 2 * pair:2 * pair + 2].rearrange("h k v -> k h v")
                                              ).then_inc(s_st0, 16)
                        next_hi(n)
                    for h2 in range(2):
                        head = 2 * pair + h2
                        for d in range(2):
                            u = 4 * pair + 2 * h2 + d
                            act.wait_ge(s_sf, u + 1)
                            act.dma_start(new_state[0, 0, d, head], sfin[:, 2 * h2 + d, :]).then_inc(s_sfo[2 * h2 + d], 16)
                        act.wait_ge(s_ud, 2 * head + 2)
                        if head:
                            act.wait_ge(s_ge, 12 * head)
                        nc.scalar.activation(osq[:, :], ps[6][:, 0:T], ACT.Square).then_inc(s_osq, 1)
                        act.wait_ge(s_ge, 12 * head + 12)
                        nc.scalar.activation(orr[:, :], orr[:, :], ACT.Sqrt).then_inc(s_ort, 1)
                        act.wait_ge(s_oy, head + 1)
                        nc.scalar.activation(gg[:, head, 0, :], oy[:, :], ACT.Copy).then_inc(s_oh, 1)
                for slot in s_sfo:
                    act.wait_ge(slot, 16 * 4)
                for i in range(4):
                    act.wait_ge(s_used, n0 + 20 + i + 1)
                    next_hi(n0 + 20 + i)

            for s, (kind, _, _) in enumerate(STAGES):
                norm(s)
                {"ffn": ffn, "mix0": mix0, "mix1": mix1}[kind](s)
            norm(n_stages)

        @block.vector
        def _(dve):
            steps = [0]

            def link(ins):
                steps[0] += 1
                ins.then_inc(s_dv, 1)
                dve.wait_ge(s_dv, steps[0])

            def split_lo(n, slot, size):
                dve.wait_ge(s_hi, n + 1)
                nc.vector.tensor_tensor(w_lo[slot][:, 0:size], w_raw[slot][:, 0:size],
                                        w_hi[slot][:, 0:size].bitcast(F32), ALU.subtract).then_inc(s_lo, 1)

            def ada_evac(p, p_static=True):
                dve.wait_ge(s_adamm, 2 * p + 2)
                nc.vector.tensor_tensor(prm[:, bass.ds(2 * p, 2), :],
                                        ps[7][:, 0:4].rearrange("p (a b) -> p a b", a=2),
                                        vt[:, bass.ds(V_ADAB + 2 * p, 2)].unsqueeze(2).broadcast_to([P, 2, 2]),
                                        ALU.add).then_inc(s_ada, 1)

            dve.wait_ge(s_vT, 1)
            nc.vector.tensor_copy(vt[:, 0:V_END], ps[6][:, 0:V_END]).then_inc(s_vt, 1)
            dve.wait_ge(s_vt, 1)
            lg = vt[:, V_LB:V_LB + 4 * HG_HEADS].rearrange("p (l e) -> p l e", l=2)
            link(nc.vector.tensor_tensor(lb[:, 0, :], lg[:, 0, :], lg[:, 1, :], ALU.max))
            link(nc.vector.memset(lb[:, 5, 0:1], EPS))
            link(nc.vector.tensor_tensor(lb[:, 1, :], lg[:, 0, :], lb[:, 0, :], ALU.subtract))
            nc.vector.tensor_tensor(lb[:, 2, :], lg[:, 1, :], lb[:, 0, :], ALU.subtract).then_inc(s_mod, 1)
            for k in range(KT):
                dve.wait_ge(s_xT, k + 1)
                nc.vector.tensor_copy(x[:, k, :], ps[k % 4][:, 0:T]).then_inc(s_x, 1)
            for i in range(2):
                split_lo(i, i, chunk_size(i))
            with dve.Fori(0, PAIRS_FIRST) as i:
                ada_evac(i)
            dve.wait_ge(s_lbe, 1)
            link(nc.vector.tensor_tensor(lb[:, 0, :], lb[:, 1, :], lb[:, 2, :], ALU.add))
            link(nc.vector.reciprocal(lb[:, 0, :], lb[:, 0, :]))
            link(nc.vector.tensor_tensor(lb[:, 1, :], lb[:, 1, :], lb[:, 0, :], ALU.mult))
            link(nc.vector.tensor_tensor(lb[:, 2, :], lb[:, 2, :], lb[:, 0, :], ALU.mult))
            link(nc.vector.tensor_tensor(lb[:, 3, :], lb[:, 1, :], lb[:, 2, :], ALU.add))
            link(nc.vector.tensor_tensor(lb[:, 3, :], lb[:, 3, :], lb[:, 1, :], ALU.subtract))
            link(nc.vector.tensor_scalar(lb[:, 4, :], lb[:, 3, :], -1.0, 1.0, ALU.mult, ALU.add))

            def ada_all(s, lo, hi_):
                with dve.Fori(first_pair[s] + lo, first_pair[s] + hi_) as i:
                    ada_evac(i)

            def norm(m):
                if m < n_stages:
                    dve.wait_ge(s_ada, first_pair[m])
                    sc = prm_tile(m, 1)
                    ng = vt[:, norm_col[m]:norm_col[m] + KT].unsqueeze(2).broadcast_to([P, KT, 2])
                    nc.vector.scalar_tensor_tensor(mod_a[:, :, :], prm[:, sc:sc + KT, :], 1.0, ng,
                                                   ALU.add, ALU.mult).then_inc(s_mod, 1)
                dve.wait_ge(s_rs, m + 1)
                link(nc.vector.reciprocal(rr[:, :], rr[:, :]))

                def scaled(k):
                    nc.vector.tensor_tensor(xf[:, k, :], x[:, k, :], rr[:, :], ALU.mult).then_inc(s_xr, 1)

                if m == n_stages:
                    for k in range(KT):
                        nc.vector.scalar_tensor_tensor(xf[:, k, :], x[:, k, :], vt[:, V_NF + k:V_NF + k + 1],
                                                       rr[:, :], ALU.mult, ALU.mult).then_inc(s_xr, 1)
                    return
                scaled(0)
                scaled(1)
                for k in range(KT):
                    dve.wait_ge(s_xh, 8 * m + k + 1)
                    for cnd, a, b in GROUPS:
                        last = nc.vector.tensor_scalar(xf[:, k, a:b], xf[:, k, a:b], mod_a[:, k, cnd:cnd + 1],
                                                       prm[:, prm_tile(m, 0) + k, cnd:cnd + 1], ALU.mult, ALU.add)
                    steps[0] += 1
                    last.then_inc(s_dv, 1)
                    if k + 2 < KT:
                        scaled(k + 2)
                    dve.wait_ge(s_dv, steps[0])
                    nc.vector.tensor_tensor(xl[:, k, :], xf[:, k, :], xh[:, k, :].bitcast(F32),
                                            ALU.subtract).then_inc(s_xl, 1)

            def gates(s):
                dve.wait_ge(s_ada, first_pair[s] + 4)
                g = prm_tile(s, 2)
                link(nc.vector.tensor_scalar(hgate[:, :, :], prm[:, g:g + KT, :],
                                             0.5 if STAGES[s][0] == "ffn" else 1.0, None, ALU.mult))

            def residual(k, bank):
                for cnd, a, b in GROUPS:
                    last = nc.vector.scalar_tensor_tensor(
                        x[:, bass.ds(k, 1), a:b].rearrange("p a t -> p (a t)"), bank[:, a:b],
                        hgate[:, bass.ds(k, 1), cnd], x[:, bass.ds(k, 1), a:b].rearrange("p a t -> p (a t)"),
                        ALU.mult, ALU.add)
                last.then_inc(s_x, 1)

            def ffn(s):
                n0, g0 = BASE[s], gh0[s]
                looped = stage_pairs[s] == PAIRS
                if not looped:
                    ada_all(s, 0, stage_pairs[s])

                def w1_tile(cc, slot, size):
                    n = n0 + cc
                    dve.wait_ge(s_sa, g0 + cc + 1)
                    nc.vector.tensor_tensor(g_raw[slot][:, :], silu_a[slot][:, :], ps[2 * slot + 1][:, 0:T],
                                            ALU.mult).then_inc(s_gm, 1)
                    split_lo(n + 2, slot, size)
                    dve.wait_ge(s_gh, g0 + cc + 1)
                    nc.vector.tensor_tensor(gg[:, bass.ds(cc, 1), 1, :].rearrange("p a t -> p (a t)"),
                                            g_raw[slot][:, :],
                                            gg[:, bass.ds(cc, 1), 0, :].rearrange("p a t -> p (a t)").bitcast(F32),
                                            ALU.subtract).then_inc(s_gl, 1)

                with dve.Fori(0, FT // 2 - 1) as i:
                    for slot in range(2):
                        w1_tile(2 * i + slot, slot, KT * 256)
                    if looped:
                        ada_evac(first_pair[s] + i)
                for slot in range(2):
                    w1_tile(FT - 2 + slot, slot, HALF * P)
                if looped:
                    ada_all(s, FT // 2 - 1, PAIRS)
                gates(s)

                def w2_tile(d, bank, size):
                    n = n0 + FT + 2 * d
                    if size:
                        split_lo(n + 2, 0, size)
                    dve.wait_ge(s_used, n + 2)
                    residual(d, bank)
                    if size:
                        split_lo(n + 3, 1, size)

                with dve.Fori(0, KT // 2 - 1) as i:
                    for e in range(2):
                        w2_tile(2 * i + e, ps[4 + e], HALF * P)
                w2_tile(KT - 2, ps[4], HALF * P)
                w2_tile(KT - 1, ps[5], chunk_size(BASE[s + 1]))

            def next_lo(n):
                if chunk_size(n + 2):
                    split_lo(n + 2, n % 2, chunk_size(n + 2))

            def out_projection(s, n):
                gates(s)
                for i in range(4):
                    dve.wait_ge(s_used, n + i + 1)
                    for e in range(2):
                        residual(2 * i + e, ps[2 * (i % 2) + e])
                    next_lo(n + i)

            def mix0(s):
                n0 = BASE[s]
                for i in range(8):
                    next_lo(n0 + i)
                    ada_evac(first_pair[s] + i)
                ada_all(s, 8, PAIRS)
                dve.wait_ge(s_ckT, 1)
                nc.vector.tensor_copy(ckT[:, :, :].rearrange("p a t -> p (a t)"), ps[6][:, :]).then_inc(s_ckv, 1)
                dve.wait_ge(s_nkT, 1)
                nc.vector.tensor_copy(nk[:, :], ps[6][:, :]).then_inc(s_nk, 1)
                for f in range(6):
                    dve.wait_ge(s_fo, f + 1)
                    tb, gp = f // 2, f % 2
                    nc.vector.tensor_copy(ab[:, tb, 2 * gp:2 * gp + 2, :],
                                          ps[f % 4][:, :].rearrange("p (g c) -> p g c", g=2)).then_inc(s_foe, 1)
                for g in range(4):
                    dve.wait_ge(s_foh, g + 1)
                    nc.vector.tensor_tensor(gg[:, 4 + g, 1, :], ps[(6 + g) % 4][:, 0:T],
                                            gg[:, 4 + g, 0, :].bitcast(F32), ALU.subtract).then_inc(s_foe, 1)

                def maxes(u):
                    width = NP_ if units[u][2] == 0 else T
                    dve.wait_ge(s_sc, u + 1)
                    link(nc.vector.reduce_max(smax[:, u:u + 1], ps[u % 2][:, 0:width], AX))
                    nc.vector.tensor_scalar(smax[:, u:u + 1], smax[:, u:u + 1], -1.0, None, ALU.mult).then_inc(s_mx, 1)

                def attn_lo(pair):
                    dve.wait_ge(s_ath, pair + 1)
                    nc.vector.tensor_tensor(gg[:, pair, 1, :], ps[4 + pair % 2][:, 0:T],
                                            gg[:, pair, 0, :].bitcast(F32), ALU.subtract).then_inc(s_at, 1)

                maxes(0)
                for u in range(24):
                    if u + 1 < 24:
                        maxes(u + 1)
                    width = NP_ if units[u][2] == 0 else T
                    dve.wait_ge(s_exp, u + 1)
                    link(nc.vector.reciprocal(srec[:, u:u + 1], ssum[:, u:u + 1]))
                    nc.vector.tensor_scalar(prob[u % 2][:, 0:width], prob[u % 2][:, 0:width],
                                            srec[:, u:u + 1], None, ALU.mult).then_inc(s_pn, 1)
                    if u % 6 == 2 and u > 6:
                        attn_lo(u // 6 - 1)
                attn_lo(3)
                out_projection(s, n0 + 8)

            def mix1(s):
                n0 = BASE[s]

                def level(u, lv):
                    pair, h2, d = u // 4, u // 2 % 2, u % 2
                    if lv == 0 and u >= 2:
                        dve.wait_ge(s_ud, u - 1)
                    tq, ks = 1 - d, d
                    q, pr, k, r, m = (blk(a, lv) for a in (hq[:, h2, :], hp_[d][:, h2, :], hk[d][:, h2, :],
                                                           hr[u % 2][:, :], hm[u % 2][:, lv, :]))
                    w = 1 << lv
                    end = w - 1 if d == 0 else 0
                    nc.vector.tensor_tensor(m[:, :, tq, :], q[:, :, tq, :], pr[:, :, tq, :], ALU.mult)
                    whole = [P, T // (2 * w), w]
                    if lv == 0:
                        nc.vector.tensor_copy(m[:, :, ks, :], k[:, :, ks, :])
                        nc.vector.memset(r[:, :, tq, :], 1.0)
                        link(nc.vector.tensor_copy(r[:, :, ks, :], pr[:, :, tq, :]))
                    else:
                        nc.vector.tensor_tensor(m[:, :, ks, :], k[:, :, ks, :], r[:, :, ks, :], ALU.mult)
                        link(nc.vector.tensor_tensor(r[:, :, ks, :], r[:, :, ks, :],
                                                     pr[:, :, tq, end:end + 1].broadcast_to(whole), ALU.mult))
                    link(nc.vector.tensor_tensor(pr[:, :, tq, :], pr[:, :, tq, :],
                                                 pr[:, :, ks, end:end + 1].broadcast_to(whole), ALU.mult))
                    if lv == LEVELS - 1:
                        nc.vector.tensor_tensor(qi[u % 2], hq[:, h2, :], hp_[d][:, h2, :], ALU.mult)
                        nc.vector.tensor_tensor(ki[u % 2], hk[d][:, h2, :], hr[u % 2][:, :],
                                                ALU.mult).then_inc(s_un, 1)

                def copies(u):
                    kinds = ["diag"] * (u % 2 == 0) + ["level"] * 3 + ["turn", "state"] + ["mean"] * (u % 2)
                    return [(kind, 6 * u + e) for e, kind in enumerate(kinds)]

                def evac(u, what):
                    pair, h2, d = u // 4, u // 2 % 2, u % 2
                    head = 2 * pair + h2
                    kind, g = what
                    bank = ps[4 + g % 2]
                    dve.wait_ge(s_gb, g + 1)
                    if kind == "diag":
                        nc.vector.tensor_tensor(gd[:, :].rearrange("p (c t) -> p c t", c=3),
                                                bank[:, 0:T].rearrange("p (c t) -> p c t", c=3),
                                                ident.unsqueeze(1).broadcast_to([P, 3, P]), ALU.mult).then_inc(s_ge, 1)
                    elif kind == "level":
                        mask = cst[:, C_MASK + d * LEVELS * 64:C_MASK + (d + 1) * LEVELS * 64]
                        nc.vector.tensor_tensor(gm[g % 2][:, :], bank[:, 0:LEVELS * 64], mask, ALU.mult).then_inc(s_ge, 1)
                    elif kind == "turn":
                        nc.vector.tensor_copy(ktok[:, :, :], bank[:, 0:256].rearrange("p (a k) -> p a k", a=2)).then_inc(s_ge, 1)
                    elif kind == "state":
                        first = 1 if d == 0 else 2
                        col = first * P + (P - 1 if d == 0 else 0)
                        if pair:
                            dve.wait_ge(s_sfo[2 * h2 + d], 16 * pair)
                        nc.vector.tensor_copy(sfin[:, 2 * h2 + d, :], bank[:, 0:P]).then_inc(s_sf, 1)
                        dve.wait_ge(s_st0, 32 * (pair + 1))
                        nc.vector.scalar_tensor_tensor(st1[:, :], st0[:, d, h2, :], hp_[d][:, h2, col:col + 1],
                                                       bank[:, P:2 * P], ALU.mult, ALU.add).then_inc(s_ge, 1)
                    else:
                        nc.vector.tensor_scalar(orr[:, :], bank[:, 0:T], EPS, None, ALU.add).then_inc(s_ge, 1)

                def finish(head):
                    h2 = head % 2
                    nc.vector.scalar_tensor_tensor(oy[:, :], ps[6][:, 0:T], vt[:, V_HG:V_HG + 1], sg[:, h2, :],
                                                   ALU.mult, ALU.mult).then_inc(s_yo, 1)
                    dve.wait_ge(s_ort, head + 1)
                    link(nc.vector.reciprocal(orr[:, :], orr[:, :]))
                    nc.vector.tensor_tensor(oy[:, :], oy[:, :], orr[:, :], ALU.mult).then_inc(s_oy, 1)
                    dve.wait_ge(s_oh, head + 1)
                    nc.vector.tensor_tensor(gg[:, head, 1, :], oy[:, :], gg[:, head, 0, :].bitcast(F32),
                                            ALU.subtract).then_inc(s_ol, 1)

                for pair in range(4):
                    for part in range(5):
                        i = 5 * pair + part
                        next_lo(n0 + i)
                        if i < PAIRS:
                            ada_evac(first_pair[s] + i)
                        if part in (1, 2):
                            d = part - 1
                            dve.wait_ge(s_pj, pj0[s] + i + 1)
                            for h2 in range(2):
                                cc = d * HG_HEADS + 2 * pair + h2
                                nc.vector.tensor_scalar(hp_[d][:, h2, :], hp_[d][:, h2, :], lb[:, 4, cc:cc + 1],
                                                        lb[:, 3, cc:cc + 1], ALU.mult, ALU.add)
                                last = nc.vector.tensor_scalar(hk[d][:, h2, :], hk[d][:, h2, :], lb[:, 4, cc:cc + 1],
                                                               None, ALU.mult)
                            link(last)
                    for lv in range(LEVELS):
                        level(4 * pair, lv)
                    for e in range(4):
                        u = 4 * pair + e
                        todo = list(copies(u))
                        for lv in range(LEVELS):
                            if e < 3:
                                level(u + 1, lv)
                            if lv < len(todo):
                                evac(u, todo[lv])
                        if e % 2:
                            finish(2 * pair + e // 2)
                out_projection(s, n0 + 20)

            for s, (kind, _, _) in enumerate(STAGES):
                norm(s)
                {"ffn": ffn, "mix0": mix0, "mix1": mix1}[kind](s)
            norm(n_stages)
            for f in range(2 * TB):
                tb, half = f // 2, f % 2
                dve.wait_ge(s_yT, f + 1)
                nc.vector.tensor_copy(y_stage(tb)[:, half * 512:half * 512 + 512], ps[f % 2][:, :]).then_inc(s_yo2, 1)

        @block.tensor
        def _(pe):
            def mm3(out, a, b, first, last):
                (ah, al), (bh, bl) = a, b
                nc.tensor.matmul(out, ah, bh, start=first, stop=False)
                nc.tensor.matmul(out, ah, bl, start=False, stop=False)
                return nc.tensor.matmul(out, al, bh, start=False, stop=last)

            def hidden(k, a=0, b=T):
                return gg[:, k, 0, a:b], gg[:, k, 1, a:b]

            def normed(k, a=0, b=T):
                return xh[:, k, a:b], xl[:, k, a:b]

            def wtile(slot, k, width, a, b):
                return (w_hi[slot][:, k * width + a:k * width + b], w_lo[slot][:, k * width + a:k * width + b])

            def ada_pair(p):
                if not (isinstance(p, int) and p == 0):
                    pe.wait_ge(s_ada, p)
                for slot in range(2):
                    pe.wait_ge(s_adaw[slot], 16 * p + 16)
                    for k in range(KT):
                        last = nc.tensor.matmul(ps[7][:, 2 * slot:2 * slot + 2], ada[slot][:, k, :], cond[:, k, :],
                                                start=(k == 0), stop=(k == KT - 1))
                    last.then_inc(s_adamm, 1)

            def ada_all(s, lo, hi_):
                with pe.Fori(first_pair[s] + lo, first_pair[s] + hi_) as i:
                    ada_pair(i)

            pe.wait_ge(s_cst, 16)
            pe.wait_ge(s_vrow, 16 * 8)
            nc.tensor.transpose(ps[6][:, 0:P], vrow[:, 0, :], ident)
            nc.tensor.transpose(ps[6][:, P:V_END], vrow[0:V_END - P, 1, :],
                                cst[0:V_END - P, C_ID:C_ID + V_END - P]).then_inc(s_vT, 1)
            pe.wait_ge(s_xin, 32)
            xin = xf[:, :, :].rearrange("p k t -> p (k t)").rearrange("p (b d) -> p b d", b=TB)
            for k in range(KT):
                if k >= 4:
                    pe.wait_ge(s_x, k - 3)
                for tb in range(TB):
                    last = nc.tensor.transpose(ps[k % 4][:, tb * P:(tb + 1) * P], xin[:, tb, k * P:(k + 1) * P], ident)
                last.then_inc(s_xT, 1)
            pe.wait_ge(s_cond, 1)
            ada_pair(0)
            with pe.Fori(1, PAIRS_FIRST) as i:
                ada_pair(i)

            def norm(m):
                for k in range(KT):
                    pe.wait_ge(s_sq, 8 * m + k + 1)
                    last = nc.tensor.matmul(ps[6][:, 0:T], cst[:, C_MEAN:C_MEAN + P], xf[:, k, :],
                                            start=(k == 0), stop=(k == KT - 1))
                last.then_inc(s_ms, 1)

            def features(m, n, slot, first, width=256):
                pe.wait_ge(s_lo, n + 1)
                for k in range(KT):
                    if first:
                        pe.wait_ge(s_xl, 8 * m + k + 1)
                    for e in range(2):
                        last = mm3(ps[2 * slot + e][:, 0:T], wtile(slot, k, 256, e * P, (e + 1) * P), normed(k),
                                   k == 0, k == KT - 1)
                last.then_inc(s_used, 1)

            def tokens(n, slot):
                pe.wait_ge(s_lo, n + 1)
                for tb in range(TB):
                    out = ps[2 * slot + tb // 2][:, tb % 2 * 256:tb % 2 * 256 + 256]
                    for k in range(KT):
                        last = mm3(out, normed(k, tb * P, (tb + 1) * P), wtile(slot, k, 256, 0, 256),
                                   k == 0, k == KT - 1)
                last.then_inc(s_used, 1)

            def out_projection(s, n):
                for i in range(4):
                    slot = i % 2
                    pe.wait_ge(s_lo, n + i + 1)
                    if i >= 2:
                        pe.wait_ge(s_x, 8 * (s + 1) + 2 * (i - 1))
                    for k in range(KT):
                        for e in range(2):
                            last = mm3(ps[2 * slot + e][:, 0:T], wtile(slot, k, 256, e * P, (e + 1) * P), hidden(k),
                                       k == 0, k == KT - 1)
                    last.then_inc(s_used, 1)

            def ffn(s):
                n0, g0 = BASE[s], gh0[s]
                looped = stage_pairs[s] == PAIRS
                if not looped:
                    ada_all(s, 0, stage_pairs[s])

                def w1_tile(cc, slot, first, guard):
                    if guard:
                        pe.wait_ge(s_gm, g0 + cc - 1)
                    pe.wait_ge(s_lo, n0 + cc + 1)
                    for k in range(KT):
                        if first:
                            pe.wait_ge(s_xl, 8 * s + k + 1)
                        for e in range(2):
                            at_ = (e * KT + k) * P
                            last = mm3(ps[2 * slot + e][:, 0:T],
                                       (w_hi[slot][:, at_:at_ + P], w_lo[slot][:, at_:at_ + P]), normed(k),
                                       k == 0, k == KT - 1)
                    last.then_inc(s_used, 1)

                w1_tile(0, 0, True, False)
                w1_tile(1, 1, False, False)
                if looped:
                    ada_pair(first_pair[s])
                with pe.Fori(1, FT // 2) as i:
                    for slot in range(2):
                        w1_tile(2 * i + slot, slot, False, True)
                    if looped:
                        ada_pair(first_pair[s] + i)
                if looped:
                    ada_all(s, FT // 2, PAIRS)

                def w2_tile(d, bank, guard):
                    if guard:
                        pe.wait_ge(s_x, 8 * (s + 1) + d - 1)
                    for half in range(2):
                        pe.wait_ge(s_lo, n0 + FT + 2 * d + half + 1)
                        pe.wait_ge(s_gl, g0 + HALF * (half + 1))
                        for kk in range(HALF):
                            last = mm3(bank[:, 0:T], wtile(half, kk, P, 0, P), hidden(half * HALF + kk),
                                       half == 0 and kk == 0, half == 1 and kk == HALF - 1)
                        last.then_inc(s_used, 1)

                w2_tile(0, ps[4], False)
                w2_tile(1, ps[5], False)
                with pe.Fori(1, KT // 2) as i:
                    for e in range(2):
                        w2_tile(2 * i + e, ps[4 + e], True)

            def mix0(s):
                n0 = BASE[s]
                for i in range(8):
                    slot = i % 2
                    if i >= 2:
                        pe.wait_ge(s_pj, pj0[s] + i - 1)
                    if i // 2 == 2:
                        tokens(n0 + i, slot)
                    else:
                        features(s, n0 + i, slot, i == 0)
                    ada_pair(first_pair[s] + i)
                ada_all(s, 8, PAIRS)
                pe.wait_ge(s_kv, 32)
                pe.wait_ge(s_rs, s + 1)
                for e in range(4):
                    last = nc.tensor.transpose(ps[6][:, e * P:(e + 1) * P], ck[:, e * P:(e + 1) * P], ident)
                last.then_inc(s_ckT, 1)
                pe.wait_ge(s_pj, pj0[s] + 8)
                pe.wait_ge(s_ckv, 1)
                for e in range(4):
                    last = nc.tensor.transpose(ps[6][:, e * P:(e + 1) * P], kT[:, e, 0:P], ident)
                last.then_inc(s_nkT, 1)
                for f in range(6):
                    tb, gp = f // 2, f % 2
                    if f >= 4:
                        pe.wait_ge(s_foe, f - 3)
                    for e in range(2):
                        g = 2 * gp + e
                        last = nc.tensor.matmul(ps[f % 4][:, e * 256:e * 256 + 256], fT[:, g, tb * P:(tb + 1) * P],
                                                cst[:, C_DG:C_DG + 256], start=True, stop=True)
                    last.then_inc(s_fo, 1)
                pe.wait_ge(s_foe, 6)
                for g in range(4):
                    if g >= 2:
                        pe.wait_ge(s_foe, 6 + g - 1)
                    bank = ps[(6 + g) % 4]
                    for e in range(2):
                        nc.tensor.matmul(bank[:, 0:P], ab[:, 0, g, e * P:(e + 1) * P],
                                         cst[:, C_DT128 + e * P:C_DT128 + (e + 1) * P], start=(e == 0), stop=(e == 1))
                    for tt in range(2):
                        for e in range(2):
                            at_ = C_DT256 + (2 * tt + e) * NS_
                            last = nc.tensor.matmul(bank[:, NP_:T], ab[:, 1 + tt, g, e * P:(e + 1) * P],
                                                    cst[:, at_:at_ + NS_], start=(tt == 0 and e == 0),
                                                    stop=(tt == 1 and e == 1))
                    last.then_inc(s_fo, 1)
                pe.wait_ge(s_foe, 10)
                pe.wait_ge(s_bias, 4)

                def scores(u):
                    pair, h2, what = units[u]
                    rows = slice(HD * h2, HD * h2 + HD)
                    bank = ps[u % 2]
                    if u >= 2:
                        pe.wait_ge(s_exp, u - 1)
                    if what == 0:
                        nc.tensor.matmul(bank[:, 0:P], qT[rows, pair, 0:P], kT[rows, pair, 0:P],
                                         start=True, stop=True).then_inc(s_sc, 1)
                        return
                    b = what - 1
                    q = qT[rows, pair, NP_ + b * P:NP_ + (b + 1) * P]
                    nc.tensor.matmul(bank[:, 0:NS_], q, kT[rows, pair, NP_:T], start=True, stop=False)
                    tab = bias[:, 2 * pair + h2, 2 - 2 * b:6 - 2 * b, :].rearrange("p r c -> p (r c)")
                    nc.tensor.matmul(bank[:, 0:NS_], anti, tab, start=False, stop=True)
                    nc.tensor.matmul(bank[:, NS_:T], q, ckT[rows, pair, :], start=True, stop=True).then_inc(s_sc, 1)

                def turn(u):
                    n = 1 if units[u][2] == 0 else 3
                    pe.wait_ge(s_pn, u + 1)
                    if u >= 2:
                        pe.wait_ge(s_pt, u - 1)
                    for e in range(n):
                        last = nc.tensor.transpose(ps[2 + u % 2][:, e * P:(e + 1) * P], prob[u % 2][:, e * P:(e + 1) * P], ident)
                    last.then_inc(s_tr, 1)

                def values(u):
                    pair, h2, what = units[u]
                    head = 2 * pair + h2
                    cols = slice(head * HD, head * HD + HD)
                    if u % 6 == 0 and pair >= 2:
                        pe.wait_ge(s_at, pair - 1)
                    pe.wait_ge(s_pt, u + 1)
                    out = ps[4 + pair % 2][HD * h2:HD * h2 + HD, what * P:(what + 1) * P]
                    vals = [vtok[:, 0, cols]] if what == 0 else [vtok[:, 1, cols], vtok[:, 2, cols], cv[:, cols]]
                    for e, v in enumerate(vals):
                        last = nc.tensor.matmul(out, v, probT[u % 2][:, e * P:(e + 1) * P],
                                                start=(e == 0), stop=(e == len(vals) - 1))
                    last.then_inc(s_pv, 1)

                scores(0)
                scores(1)
                for u in range(24):
                    turn(u)
                    if u + 2 < 24:
                        scores(u + 2)
                    if u:
                        values(u - 1)
                values(23)
                pe.wait_ge(s_at, 4)
                out_projection(s, n0 + 8)

            def mix1(s):
                n0 = BASE[s]

                def wait_bank(g):
                    if g >= 2:
                        pe.wait_ge(s_ge, g - 1)
                    return ps[4 + g % 2]

                def unit(u):
                    pair, h2, d = u // 4, u // 2 % 2, u % 2
                    head = 2 * pair + h2
                    o = ps[6]
                    m = hm[u % 2]
                    g = 6 * u
                    tq = 1 - d
                    vcols = slice(h2 * P, (h2 + 1) * P)

                    def level_sums(cc, g):
                        bank = wait_bank(g)
                        for lv in range(LEVELS):
                            rhs = blk(m[:, lv, cc * P:(cc + 1) * P], lv)[:, :, tq, :]
                            last = nc.tensor.matmul(bank[:, lv * 64:(lv + 1) * 64], m[:, lv, cc * P:(cc + 1) * P],
                                                    rhs, start=True, stop=True)
                        last.then_inc(s_gb, 1)

                    def level_values(cc, g):
                        pe.wait_ge(s_ge, g + 1)
                        for lv in range(LEVELS):
                            out = blk(o[:, cc * P:(cc + 1) * P], lv)[:, :, tq, :]
                            masked = gm[g % 2][:, lv * 64:(lv + 1) * 64].rearrange("p (b w) -> p b w", w=1 << lv)
                            last = nc.tensor.matmul(out, hv[:, cc, vcols], masked,
                                                    start=False, stop=False, skip_group_check=True)
                        return last

                    pe.wait_ge(s_un, u + 1)
                    if d == 0:
                        bank = wait_bank(g)
                        for cc in range(3):
                            for e in range(2):
                                last = nc.tensor.matmul(bank[:, cc * P:(cc + 1) * P], hk[e][:, h2, cc * P:(cc + 1) * P],
                                                        hq[:, h2, cc * P:(cc + 1) * P], start=(e == 0), stop=(e == 1))
                        last.then_inc(s_gb, 1)
                        g += 1
                    level_sums(0, g)
                    if d == 0:
                        pe.wait_ge(s_ge, g)
                        if head:
                            pe.wait_ge(s_yo, head)
                        for cc in range(3):
                            nc.tensor.matmul(o[:, cc * P:(cc + 1) * P], hv[:, cc, vcols], gd[:, cc * P:(cc + 1) * P],
                                             start=(cc == 0), stop=False, skip_group_check=True)
                    level_sums(1, g + 1)
                    level_values(0, g)
                    level_sums(2, g + 2)
                    level_values(1, g + 1)
                    first = 1 if d == 0 else 2
                    second = 3 - first
                    bank = wait_bank(g + 3)
                    nc.tensor.transpose(bank[:, 0:P], ki[u % 2][:, 0:P], ident)
                    nc.tensor.transpose(bank[:, P:2 * P], ki[u % 2][:, first * P:(first + 1) * P], ident).then_inc(s_gb, 1)
                    level_values(2, g + 2)
                    pe.wait_ge(s_ge, g + 4)
                    bank = wait_bank(g + 4)
                    nc.tensor.matmul(bank[:, 0:P], ktok[:, 0, :], hv[:, 0, vcols], start=True, stop=True)
                    nc.tensor.matmul(bank[:, P:2 * P], ktok[:, 1, :], hv[:, first, vcols],
                                     start=True, stop=True).then_inc(s_gb, 1)
                    pe.wait_ge(s_st0, 32 * (pair + 1))
                    nc.tensor.matmul(o[:, first * P:(first + 1) * P], st0[:, d, h2, :],
                                     qi[u % 2][:, first * P:(first + 1) * P], start=False, stop=False, skip_group_check=True)
                    pe.wait_ge(s_ge, g + 5)
                    nc.tensor.matmul(o[:, second * P:(second + 1) * P], st1[:, :],
                                     qi[u % 2][:, second * P:(second + 1) * P], start=False, stop=True,
                                     skip_group_check=True).then_inc(s_ud, 1)
                    if d == 1:
                        pe.wait_ge(s_osq, head + 1)
                        bank = wait_bank(g + 5)
                        nc.tensor.matmul(bank[:, 0:T], cst[:, C_MEANH:C_MEANH + P], osq[:, :],
                                         start=True, stop=True).then_inc(s_gb, 1)

                for pair in range(4):
                    for part in range(5):
                        i = 5 * pair + part
                        slot = i % 2
                        if i >= 2:
                            pe.wait_ge(s_pj, pj0[s] + i - 1)
                        if part == 3:
                            tokens(n0 + i, slot)
                        else:
                            features(s, n0 + i, slot, i == 0)
                        if i < PAIRS:
                            ada_pair(first_pair[s] + i)
                    pe.wait_ge(s_pj, pj0[s] + 5 * pair + 5)
                    for e in range(4):
                        unit(4 * pair + e)
                pe.wait_ge(s_ol, HG_HEADS)
                out_projection(s, n0 + 20)

            for s, (kind, _, _) in enumerate(STAGES):
                norm(s)
                {"ffn": ffn, "mix0": mix0, "mix1": mix1}[kind](s)
            norm(n_stages)
            for f in range(2 * TB):
                tb, half = f // 2, f % 2
                pe.wait_ge(s_xr, 8 * n_stages + 8)
                if f >= 2:
                    pe.wait_ge(s_yo2, f - 1)
                for e in range(4):
                    last = nc.tensor.transpose(ps[f % 2][:, e * P:(e + 1) * P],
                                               xf[:, 4 * half + e, tb * P:(tb + 1) * P], ident)
                last.then_inc(s_yT, 1)


_INS = ['x_prompt', 'x_sample', 'cache_k', 'cache_v', 'state_hgrn', 'c', 'c_ctx', 'ada_w', 'ada_b', 'norm_g',
        'ffn_w1', 'ffn_w2', 'mix0_w_in', 'mix0_w_out', 'na_rpb', 'mix1_w_in', 'mix1_w_out',
        'hg_lb_logits', 'hg_norm_g', 'norm_f']
_OUTS = [(1, NP_, D), (1, NS_, D), (1, 1, NP_, HEADS, HD), (1, 1, NP_, HEADS, HD), (1, 1, 2, HG_HEADS, P, P)]


def kernel(**inputs):
    import concourse.bacc as bacc
    from concourse.bass_utils import run_bass_kernel_spmd as run

    nc = bacc.Bacc("TRN2", target_bir_lowering=False, num_devices=1)
    arrays, args = {}, []
    given = {name: np.ascontiguousarray(inputs[name]) for name in _INS}
    given["consts"] = shape_constants()
    for name, a in given.items():
        arrays[f"in_{name}"] = a
        args.append(nc.dram_tensor(f"in_{name}", a.shape, mybir.dt.from_np(a.dtype), kind="ExternalInput").ap())
    for i, shape in enumerate(_OUTS):
        args.append(nc.dram_tensor(f"out_{i}", shape, F32, kind="ExternalOutput").ap())
    build(nc, *args)
    r = run(nc, [arrays], core_ids=[0])
    return tuple(r.results[0][f"out_{i}"] for i in range(len(_OUTS)))
```

```python
from contextlib import ExitStack

import numpy as np

import concourse.bass as bass
from concourse import mybir

F32 = mybir.dt.float32
F32R = mybir.dt.float32r
ALU = mybir.AluOpType
ACT = mybir.ActivationFunctionType
AX = mybir.AxisListType.X

P = 128
D = 1024
KT = D // P
NP_, NS_ = 128, 256
T = NP_ + NS_
TB = T // P
DEPTH = 2
DFF = 2816
FT = DFF // P
HALF = FT // 2
NMOD = 9
GRID_W, ROWS = 64, 4
HEADS, HD = 8, 64
NAW = HEADS * HD
RPB_R, RPB_C = 15, 31
WIN_C = 16
SLOTS = 6
HG_HEADS = 8
LEVELS = 7
EPS = 1e-6
SBUF_END = 229344
NEG = -1e30
GROUPS = ((0, 0, NP_), (1, NP_, T))

V_ADAB = 0
V_NG = V_ADAB + DEPTH * NMOD * KT
V_NF = V_NG + DEPTH * 3 * KT
V_LB = V_NF + KT
V_HG = V_LB + DEPTH * 2 * HG_HEADS
V_C = V_HG + 1
V_END = V_C + 2 * KT

C_ID = 0
C_ANTI = C_ID + P
C_MEAN = C_ANTI + P
C_MEANH = C_MEAN + P
C_MASK = C_MEANH + P
C_KEEP = C_MASK + 2 * LEVELS * 64
C_DG = C_KEEP
C_DT256 = C_DG + 2 * P
C_DT128 = C_DT256 + 4 * NS_
C_END = C_DT128 + 2 * NP_


def shape_constants():
    c = np.zeros((P, C_END), np.float64)
    c[:, C_ID:C_ID + P] = np.eye(P)
    c[:, C_ANTI:C_ANTI + P] = np.eye(P)[::-1]
    c[:, C_MEAN:C_MEAN + P] = 1.0 / D
    c[:, C_MEANH:C_MEANH + P] = 1.0 / P
    s = np.arange(P)[:, None]
    j = np.arange(64)[None, :]
    for back in range(2):
        for lv in range(LEVELS):
            w = 1 << lv
            m = (s // (2 * w) == j // w) & (((s % (2 * w)) >= w) == bool(back))
            at = C_MASK + (back * LEVELS + lv) * 64
            c[:, at:at + 64] = m
    n = np.arange(P)
    ang = 2 * np.pi * ((n[:, None] * n[None, :]) % P) / P
    c[:, C_DG:C_DG + P] = np.cos(ang)
    c[:, C_DG + P:C_DG + 2 * P] = np.sin(ang)
    c[:, C_DT128:C_DT128 + P] = np.cos(ang) / np.sqrt(NP_ * P)
    c[:, C_DT128 + P:C_DT128 + 2 * P] = -np.sin(ang) / np.sqrt(NP_ * P)
    k = np.arange(NS_)
    for tt in range(2):
        a = 2 * np.pi * (((tt * P + n)[:, None] * k[None, :]) % NS_) / NS_
        at = C_DT256 + tt * 2 * NS_
        c[:, at:at + NS_] = np.cos(a) / np.sqrt(NS_ * P)
        c[:, at + NS_:at + 2 * NS_] = -np.sin(a) / np.sqrt(NS_ * P)
    return c.astype(np.float32)


STAGES = [("ffn", 0, 0), ("mix0", 0, 1), ("ffn", 0, 2), ("ffn", 1, 0), ("mix1", 1, 1), ("ffn", 1, 2)]
N_CHUNKS = {"ffn": FT + 2 * KT, "mix0": 12, "mix1": 24}
BASE = [sum(N_CHUNKS[k] for k, _, _ in STAGES[:s]) for s in range(len(STAGES) + 1)]


def chunk_size(n):
    for s, (kind, _, _) in enumerate(STAGES):
        if BASE[s] <= n < BASE[s + 1]:
            return HALF * P if kind == "ffn" and n - BASE[s] >= FT else KT * 256
    return 0


def build(nc, x_prompt, x_sample, cache_k, cache_v, state_hgrn, c, c_ctx, ada_w, ada_b, norm_g,
          ffn_w1, ffn_w2, mix0_w_in, mix0_w_out, na_rpb, mix1_w_in, mix1_w_out,
          hg_lb_logits, hg_norm_g, norm_f, consts,
          y_prompt, y_sample, new_k, new_v, new_state):
    n_stages = len(STAGES)
    total_chunks = BASE[n_stages]
    with ExitStack() as ctx:
        def sb(name, shape, dt=F32, stack=ctx):
            return stack.enter_context(nc.sbuf_tensor(name, shape, dt))

        def sem(name):
            return ctx.enter_context(nc.semaphore(name))

        ps = [ctx.enter_context(nc.psum_tensor(f"bank{i}", [P, 512], F32)) for i in range(8)]

        w_raw = [sb(f"w_raw{i}", [P, KT * 256]) for i in range(2)]
        w_hi = [sb(f"w_hi{i}", [P, KT * 256], F32R) for i in range(2)]
        w_lo = [sb(f"w_lo{i}", [P, KT * 256], F32R) for i in range(2)]
        x = sb("x", [P, KT, T])
        xh = sb("xh", [P, KT, T], F32R)
        xl = sb("xl", [P, KT, T], F32R)
        xf = sb("xf", [P, KT, T])
        ada = [sb(f"ada{i}", [P, KT // 2, 256]) for i in range(2)]
        acc = sb("acc", [P, 2, 256])
        asum = sb("asum", [P, 4])
        cst = sb("cst", [P, C_KEEP])
        vrow = sb("vrow", [P, 2, P])
        vt = sb("vt", [P, 2 * P])
        cond = sb("cond", [P, KT, 2])
        prm = sb("prm", [P, DEPTH * NMOD * KT, 2])
        mod_a = sb("mod_a", [P, KT, 2])
        hgate = sb("hgate", [P, KT, 2])
        rr = sb("rr", [P, T])
        warm = sb("warm", [P, 1])
        lb = sb("lb", [P, 6, 2 * HG_HEADS])
        gg_base = nc.sbuf_base
        gg = sb("gg", [P, FT, 2, T], F32R)
        ident = cst[:, C_ID:C_ID + P]
        anti = cst[:, C_ANTI:C_ANTI + P]

        silu_a = [sb(f"silu_a{i}", [P, T]) for i in range(2)]
        g_raw = [sb(f"g_raw{i}", [P, T]) for i in range(2)]

        arena = [gg_base + KT * 2 * T * 4]

        def at(name, shape, dt=F32):
            t = nc.alloc_sbuf_tensor_at(name, shape, dt, offset=arena[0])
            arena[0] += int(np.prod(shape[1:])) * 4
            return t

        start = arena[0]
        qT = at("qT", [P, 4, T])
        kT = at("kT", [P, 4, T])
        vtok = at("vtok", [P, TB, NAW])
        fT = at("fT", [P, 4, T])
        bias = at("bias", [P, HEADS, SLOTS, GRID_W])
        ck = at("ck", [P, NAW])
        ckT = at("ckT", [P, 4, P])
        cv = at("cv", [P, NAW])
        dft = at("dft", [P, C_END - C_KEEP])
        nk = at("nk", [P, NAW])
        prob = [at(f"prob{i}", [P, T]) for i in range(2)]
        probT = [at(f"probT{i}", [P, T]) for i in range(2)]
        smax = at("smax", [P, 24])
        ssum = at("ssum", [P, 24])
        srec = at("srec", [P, 24])
        ab = xf[:, :, :].rearrange("p k t -> p (k t)").rearrange("p (b g c) -> p b g c", b=TB, g=4)
        QUADS = 4
        arena[0] = gg_base
        first_ada = [at(f"first_ada{q}", [P, KT, 512]) for q in range(QUADS)]
        arena[0] = SBUF_END - QUADS * 512 * 4
        assert arena[0] >= nc.sbuf_base
        first_rows = at("first_rows", [2, QUADS * 512])
        arena[0] = gg_base
        y_all = at("y_all", [P, HG_HEADS, T])
        hq = [at(f"hq{i}", [P, 2, T]) for i in range(2)]
        hp_ = [[at(f"hp{i}{d}", [P, 2, T]) for d in range(2)] for i in range(2)]
        hk = [[at(f"hk{i}{d}", [P, 2, T]) for d in range(2)] for i in range(2)]
        hv = [at(f"hv{i}", [P, TB, 2 * P]) for i in range(2)]
        hr = [at(f"hr{d}", [P, T]) for d in range(2)]
        hm = [at(f"hm{i}", [P, LEVELS, T]) for i in range(2)]
        gm = [at(f"gm{i}", [P, LEVELS * 64]) for i in range(TB)]
        gd = at("gd", [P, T])
        ktok = at("ktok", [P, 2, P])
        st0 = [at(f"st0{i}", [P, 2, 2, P]) for i in range(2)]
        st1 = at("st1", [P, P])
        sfin = at("sfin", [P, 4, P])
        osq = at("osq", [P, T])
        orr = at("orr", [P, T])
        assert arena[0] <= SBUF_END
        qi = [xf[:, 2 * i, :] for i in range(2)]
        ki = [xf[:, 2 * i + 1, :] for i in range(2)]
        sg = [xf[:, 4 + 2 * i:6 + 2 * i, :] for i in range(2)]

        s_cst = sem("cst_loaded")
        s_vrow = sem("vrow_loaded")
        s_xin = sem("x_loaded")
        s_kv = sem("cache_loaded")
        s_rpb = sem("rpb_loaded")
        s_raw = [sem(f"w_loaded{i}") for i in range(2)]
        s_hi = sem("w_hi_done")
        s_lo = sem("w_lo_done")
        s_used = sem("w_used")
        s_adaw = [sem(f"ada_loaded{i}") for i in range(2)]
        s_adaT = sem("ada_turned")
        s_asum = sem("ada_row_sums")
        s_adaP = sem("ada_first_summed")
        s_adaR = sem("ada_first_rows")
        s_first = [sem(f"ada_first_loaded{q}") for q in range(QUADS)]
        s_mac = sem("ada_products_added")
        s_ada = sem("ada_done")
        s_vT = sem("vectors_turned")
        s_vt = sem("vectors_ready")
        s_cond = sem("cond_ready")
        s_lbe = sem("lb_exp")
        s_xT = sem("x_turned")
        s_x = sem("x_ready")
        s_sq = sem("squares_ready")
        s_ms = sem("mean_ready")
        s_rs = sem("root_ready")
        s_mod = sem("mod_ready")
        s_xr = sem("x_scaled")
        s_xh = sem("xh_ready")
        s_xl = sem("xl_ready")
        s_sa = sem("silu_ready")
        s_gm = sem("g_ready")
        s_gh = sem("gh_ready")
        s_gl = sem("gl_ready")
        s_pj = sem("projection_copied")
        s_bias = sem("bias_ready")
        s_ckT = sem("ck_turned")
        s_ckv = sem("ck_ready")
        s_nkT = sem("nk_turned")
        s_nk = sem("nk_ready")
        s_fo = sem("fourier_summed")
        s_foe = sem("fourier_copied")
        s_foh = sem("fourier_hi")
        s_sc = sem("scores_ready")
        s_mx = sem("max_ready")
        s_exp = sem("exp_ready")
        s_pn = sem("probs_ready")
        s_tr = sem("probs_turned")
        s_pt = sem("probsT_ready")
        s_pv = sem("attn_summed")
        s_ath = sem("attn_hi")
        s_at = sem("attn_copied")
        s_un = sem("unit_ready")
        s_ud = sem("unit_used")
        s_gb = sem("bank_filled")
        s_ge = sem("bank_copied")
        s_osq = sem("o_squared")
        s_ort = sem("o_root")
        s_oy = sem("o_ready")
        s_oh = sem("o_hi")
        s_yo = sem("o_done")
        s_st0 = [sem(f"state_loaded{i}") for i in range(2)]
        s_sf = sem("state_ready")
        s_dv = sem("vector_step")
        s_yT = sem("y_turned")
        s_yo2 = sem("y_copied")
        s_ol = sem("o_lo")
        s_sfo = [sem(f"state_stored{i}") for i in range(4)]
        s_out = sem("stored")
        s_cache_out = sem("new_cache_stored")

        norm_col = [V_NG + (layer * 3 + j) * KT for _, layer, j in STAGES] + [V_NF]

        def prm_tile(s, which):
            _, layer, j = STAGES[s]
            return (layer * NMOD + 3 * j + which) * KT

        PAIRS_FIRST = 2 * QUADS
        n_pairs = [15, 11, 15, 15, 5, 3]
        pair_at = [PAIRS_FIRST + sum(n_pairs[:s]) for s in range(n_stages)]
        n_all = PAIRS_FIRST + sum(n_pairs)
        assert 2 * n_all == DEPTH * NMOD * KT
        norm_pairs = [PAIRS_FIRST + 12 * s for s in range(n_stages)]
        for s in range(1, n_stages):
            assert norm_pairs[s] < pair_at[s]
        ffn_no = {s: i for i, s in enumerate([s for s in range(n_stages) if STAGES[s][0] == "ffn"])}
        pj0 = {1: 0, 4: 8}
        gh0 = {s: FT * i for s, i in ffn_no.items()}
        units = [(pair, h2, what) for pair in range(4) for h2 in range(2) for what in range(3)]

        fills = []
        for u in range(4 * 4):
            fills += [(u, kind) for kind in ["diag"] * (u % 2 == 0) + ["level0", "level1", "level2", "turn"]
                      + ["mean"] * (u % 2 == 0 and u > 0) + ["state"]]
        fills.append((16, "mean"))
        fill_no = {fill: g for g, fill in enumerate(fills)}

        def fill_bank(g):
            return ps[(4, 5, 7)[g % 3]]

        def y_stage(tb):
            return w_raw[tb // 2][:, tb % 2 * D:(tb % 2 + 1) * D]

        def blk(ap, lv):
            return ap.rearrange("p (b two w) -> p b two w", two=2, w=1 << lv)

        block = ctx.enter_context(nc.Block())

        @block.sync
        def _(sp):
            xin = xf[:, :, :].rearrange("p k t -> p (k t)").rearrange("p (b d) -> p b d", b=TB)
            flat = ada_b.rearrange("l (r q) -> (l r) q", q=P)
            sp.dma_start(vrow[:, 0, :], flat[0:P, :]).then_inc(s_vrow, 16)
            sp.dma_start(vrow[0:16, 1, :], flat[P:P + 16, :]).then_inc(s_vrow, 16)
            sp.dma_start(vrow[16:64, 1, :], norm_g.rearrange("l j (k q) -> (l j k) q", q=P)).then_inc(s_vrow, 16)
            sp.dma_start(vrow[64:72, 1, :], norm_f.rearrange("(k q) -> k q", q=P)).then_inc(s_vrow, 16)
            sp.dma_start(vrow[72:104, 1, :], hg_lb_logits.rearrange("l e (k q) -> (l e k) q", q=P)).then_inc(s_vrow, 16)
            sp.dma_start(vrow[104:105, 1, :], hg_norm_g).then_inc(s_vrow, 16)
            sp.dma_start(vrow[105:113, 1, :], c_ctx.rearrange("(k q) -> k q", q=P)).then_inc(s_vrow, 16)
            sp.dma_start(vrow[113:121, 1, :], c.rearrange("a (k q) -> (a k) q", q=P)).then_inc(s_vrow, 16)
            sp.dma_start(cst[:, :], consts[:, 0:C_KEEP]).then_inc(s_cst, 16)
            sp.dma_start(xin[:, 0, :], x_prompt[0]).then_inc(s_xin, 16)
            sp.dma_start(xin[:, 1:3, :], x_sample[0].rearrange("(b p) d -> p b d", p=P)).then_inc(s_xin, 16)
            src = ada_w[0].rearrange("(k p) n -> p k n", p=P)
            for q in range(QUADS):
                for a in (0, 4):
                    sp.dma_start(first_ada[q][:, a:a + 4, :],
                                  src[:, a:a + 4, 512 * q:512 * q + 512]).then_inc(s_first[q], 16)

            def load(n, parts):
                if not (isinstance(n, int) and n < 2):
                    sp.wait_ge(s_lo, n - 1)
                for dst, src in parts:
                    sp.dma_start(dst, src).then_inc(s_raw[dst_slot[0]], 16)

            dst_slot = [0]

            def load_w1(n, slot, w, col):
                dst_slot[0] = slot
                raw = w_raw[slot][:, :].rearrange("p (h k n) -> p h k n", h=2, k=KT)
                src = w.rearrange("(k p) n -> p k n", p=P)
                load(n, [(raw[:, h], src[:, :, bass.ds(h * DFF + col, P)]) for h in range(2)])

            def load_w2(n, slot, w, half, col):
                dst_slot[0] = slot
                raw = w_raw[slot][:, 0:HALF * P].rearrange("p (k n) -> p k n", k=HALF)
                src = w.rearrange("(k p) n -> p k n", p=P)
                load(n, [(raw[:, a:b], src[:, half * HALF + a:half * HALF + b, bass.ds(col, P)])
                         for a, b in ((0, 6), (6, HALF))])

            def load_square(n, slot, w, col):
                dst_slot[0] = slot
                raw = w_raw[slot][:, :].rearrange("p (k n) -> p k n", k=KT)
                src = w.rearrange("(k p) n -> p k n", p=P)
                load(n, [(raw[:, a:a + 4], src[:, a:a + 4, bass.ds(col, 256)]) for a in (0, 4)])

            for s, (kind, layer, j) in enumerate(STAGES):
                n0 = BASE[s]
                if kind == "ffn":
                    w1, w2 = ffn_w1[layer, j // 2], ffn_w2[layer, j // 2]
                    first = 0
                    if s == 0:
                        for slot in range(2):
                            load_w1(slot, slot, w1, slot * P)
                        first = 1
                    with sp.Fori(first, FT // 2) as i:
                        for slot in range(2):
                            load_w1(n0 + 2 * i + slot, slot, w1, (2 * i + slot) * P)
                    with sp.Fori(0, KT) as i:
                        for half in range(2):
                            load_w2(n0 + FT + 2 * i + half, half, w2, half, i * P)
                else:
                    w_in, w_out = (mix0_w_in, mix0_w_out) if kind == "mix0" else (mix1_w_in, mix1_w_out)
                    n_in = N_CHUNKS[kind] - 4
                    if kind == "mix0":
                        cols = [256 * i for i in range(n_in)]
                    else:
                        cols = [part * D + pair * 256 for pair in range(4) for part in range(5)]
                    for i, col in enumerate(cols):
                        load_square(n0 + i, i % 2, w_in[0], col)
                    for i in range(4):
                        load_square(n0 + n_in + i, i % 2, w_out[0], 256 * i)
            for tb in range(TB):
                sp.wait_ge(s_yo2, 2 * (tb + 1))
                dst = y_prompt[0] if tb == 0 else y_sample[0, (tb - 1) * P:tb * P, :]
                sp.dma_start(dst, y_stage(tb)).then_inc(s_out, 16)
            sp.wait_ge(s_out, 16 * TB)
            sp.wait_ge(s_cache_out, 32)
            for slot in s_sfo:
                sp.wait_ge(slot, 16 * 4)

        @block.gpsimd
        def _(pool):
            def load_pair(p, layer, col):
                src = ada_w[layer].rearrange("(k p) n -> p k n", p=P)
                for half in range(2):
                    if not (isinstance(p, int) and p == PAIRS_FIRST):
                        pool.wait_ge(s_mac, 8 * (p - PAIRS_FIRST - 1) + 4 * half + 4)
                    pool.dma_start(ada[half][:, :, :],
                                   src[:, half * 4:half * 4 + 4, bass.ds(col, 256)]).then_inc(s_adaw[half], 16)

            per_layer = NMOD * KT // 2

            def load_pairs(first, end):
                layer = first // per_layer
                with pool.Fori(first, end) as p:
                    load_pair(p, layer, (p - layer * per_layer) * 256)

            load_pair(PAIRS_FIRST, 0, PAIRS_FIRST * 256)
            load_pairs(PAIRS_FIRST + 1, pair_at[1] + 1)
            pool.wait_ge(s_used, BASE[1])
            pool.dma_start(ck[:, :], cache_k[0, 0].rearrange("t h d -> t (h d)")).then_inc(s_kv, 16)
            pool.dma_start(cv[:, :], cache_v[0, 0].rearrange("t h d -> t (h d)")).then_inc(s_kv, 16)
            pool.dma_start(dft[:, :], consts[:, C_KEEP:C_END]).then_inc(s_kv, 16)
            for half in range(2):
                for head in range(HEADS):
                    row = head * RPB_R + ROWS + half
                    src = bass.AP(tensor=na_rpb.tensor, offset=row * RPB_C + WIN_C - 1 - (GRID_W - 1),
                                  ap=[[1, GRID_W], [RPB_C, SLOTS], [1, GRID_W]])
                    pool.dma_start(bias[half * GRID_W:(half + 1) * GRID_W, head, :, :], src).then_inc(s_rpb, 16)
            pool.wait_ge(s_rpb, 16 * 2 * HEADS)
            n_sel = 0
            for half in range(2):
                for lo_, hi_, base, sign in ((0, GRID_W - WIN_C, WIN_C // 2 - (GRID_W - 1), 1),
                                             (WIN_C, GRID_W, GRID_W - 1 + WIN_C // 2 - 1 - WIN_C, -1)):
                    b = bias[half * GRID_W:(half + 1) * GRID_W, :, :, lo_:hi_].rearrange("p h r c -> p (h r) c")
                    if n_sel % 2:
                        pool.wait_ge(s_bias, n_sel)
                    nc.gpsimd.affine_select(out=b, in_=b, compare_op=ALU.is_ge, fill=NEG, base=base,
                                            pattern=[[0, HEADS * SLOTS], [sign, hi_ - lo_]],
                                            channel_multiplier=sign).then_inc(s_bias, 1)
                    n_sel += 1
            load_pairs(pair_at[1] + 1, per_layer)
            load_pairs(per_layer, n_all)

        @block.scalar
        def _(act):
            def split_hi(n, half_n, slot, size):
                act.wait_ge(s_raw[slot], 32 * half_n + 32)
                nc.scalar.activation(w_hi[slot][:, 0:size], w_raw[slot][:, 0:size], ACT.Copy).then_inc(s_hi, 1)

            act.wait_ge(s_vt, 1)
            nc.scalar.activation(cond[:, :, :].rearrange("p k c -> p c k"),
                                 vt[:, V_C:V_END].rearrange("p (c k) -> p c k", c=2), ACT.Silu).then_inc(s_cond, 1)
            for i in range(2):
                split_hi(i, 0, i, chunk_size(i))
            act.wait_ge(s_mod, 1)
            nc.scalar.activation(lb[:, 1:3, :], lb[:, 1:3, :], ACT.Exp).then_inc(s_lbe, 1)

            def norm(m):
                for k in range(KT):
                    act.wait_ge(s_x, 8 * m + k + 1 if m else KT)
                    nc.scalar.activation(xf[:, k, :], x[:, k, :], ACT.Square).then_inc(s_sq, 1)
                nc.scalar.activation(warm[:, 0:1], lb[:, 5, 0:1], ACT.Sqrt)
                act.wait_ge(s_ms, m + 1)
                nc.scalar.activation(rr[:, :], ps[6][:, 0:T], ACT.Sqrt, bias=lb[:, 5, 0:1]).then_inc(s_rs, 1)
                if m == n_stages:
                    return
                for k in range(KT):
                    act.wait_ge(s_xr, 8 * m + k + 1)
                    for cnd, a, b in GROUPS:
                        last = nc.scalar.activation(xh[:, k, a:b], xf[:, k, a:b], ACT.Identity,
                                                    bias=prm[:, prm_tile(m, 0) + k, cnd:cnd + 1])
                    last.then_inc(s_xh, 1)

            def ffn(s):
                n0, g0 = BASE[s], gh0[s]

                def w1_tile(cc, slot, cbase, size):
                    n = n0 + cc
                    act.wait_ge(s_used, n + 1)
                    nc.scalar.activation(silu_a[slot][:, :], ps[2 * slot][:, 0:T], ACT.Silu).then_inc(s_sa, 1)
                    split_hi(n + 2, n0 // 2 + cbase + 1, slot, size)
                    act.wait_ge(s_gm, g0 + cc + 1)
                    nc.scalar.activation(gg[:, bass.ds(cc, 1), 0, :].rearrange("p a t -> p (a t)"),
                                         g_raw[slot][:, :], ACT.Copy).then_inc(s_gh, 1)

                with act.Fori(0, FT // 2 - 1) as i:
                    for slot in range(2):
                        w1_tile(2 * i + slot, slot, i, KT * 256)
                for slot in range(2):
                    w1_tile(FT - 2 + slot, slot, FT // 2 - 1, HALF * P)

                def w2_tile(d, size):
                    for half in range(2):
                        n = n0 + FT + 2 * d + half
                        act.wait_ge(s_used, n + 1)
                        if size:
                            split_hi(n + 2, (n0 + FT) // 2 + d + 1, half, size)

                with act.Fori(0, KT - 1) as d:
                    w2_tile(d, HALF * P)
                w2_tile(KT - 1, chunk_size(BASE[s + 1]))

            def next_hi(n):
                if chunk_size(n + 2):
                    split_hi(n + 2, n // 2 + 1, n % 2, chunk_size(n + 2))

            def mix0(s):
                n0 = BASE[s]
                for i in range(8):
                    n = n0 + i
                    slot = i % 2
                    act.wait_ge(s_used, n + 1)
                    b0, b1 = ps[2 * slot], ps[2 * slot + 1]
                    part, half = i // 2, i % 2
                    if part == 2:
                        nc.scalar.activation(vtok[:, 0:2, half * 256:half * 256 + 256],
                                             b0[:, :].rearrange("p (b n) -> p b n", b=2), ACT.Copy)
                        last = nc.scalar.activation(vtok[:, 2, half * 256:half * 256 + 256], b1[:, 0:256], ACT.Copy)
                    else:
                        dst = (qT, kT, None, fT)[part]
                        scale = HD ** -0.5 if part == 0 else 1.0
                        nc.scalar.activation(dst[:, 2 * half, :], b0[:, 0:T], ACT.Copy, scale=scale)
                        last = nc.scalar.activation(dst[:, 2 * half + 1, :], b1[:, 0:T], ACT.Copy, scale=scale)
                    last.then_inc(s_pj, 1)
                    next_hi(n)
                act.wait_ge(s_pj, pj0[s] + 8)
                act.dma_start(new_v[0, 0].rearrange("t h d -> t (h d)"), vtok[:, 0, :]).then_inc(s_cache_out, 16)
                act.wait_ge(s_nk, 1)
                act.dma_start(new_k[0, 0].rearrange("t h d -> t (h d)"), nk[:, :]).then_inc(s_cache_out, 16)
                for g in range(4):
                    act.wait_ge(s_fo, 6 + g + 1)
                    nc.scalar.activation(gg[:, 4 + g, 0, :], ps[(6 + g) % 4][:, 0:T], ACT.Copy).then_inc(s_foh, 1)

                def attn_hi(pair):
                    act.wait_ge(s_pv, 6 * pair + 6)
                    nc.scalar.activation(gg[:, pair, 0, :], ps[4 + pair % 2][:, 0:T], ACT.Copy).then_inc(s_ath, 1)

                def exps(u):
                    width = NP_ if units[u][2] == 0 else T
                    act.wait_ge(s_mx, u + 1)
                    if u >= 2:
                        act.wait_ge(s_tr, u - 1)
                    nc.scalar.activation(prob[u % 2][:, 0:width], ps[u % 2][:, 0:width], ACT.Exp,
                                         bias=smax[:, u:u + 1], accum_out=ssum[:, u:u + 1]).then_inc(s_exp, 1)

                def copy_probs(u):
                    width = NP_ if units[u][2] == 0 else T
                    act.wait_ge(s_tr, u + 1)
                    if u >= 2:
                        act.wait_ge(s_pv, u - 1)
                    nc.scalar.activation(probT[u % 2][:, 0:width], ps[2 + u % 2][:, 0:width],
                                         ACT.Copy).then_inc(s_pt, 1)

                exps(0)
                for u in range(24):
                    if u + 1 < 24:
                        exps(u + 1)
                    copy_probs(u)
                    if u % 6 == 1 and u > 6:
                        attn_hi(u // 6 - 1)
                attn_hi(3)
                act.wait_ge(s_cache_out, 32)
                for i in range(4):
                    act.wait_ge(s_used, n0 + 8 + i + 1)
                    next_hi(n0 + 8 + i)

            def mix1(s):
                n0 = BASE[s]

                def copy_chunk(pair, part):
                    n = n0 + 5 * pair + part
                    bank = [ps[2 * (n % 2)], ps[2 * (n % 2) + 1]]
                    b = pair % 2
                    act.wait_ge(s_used, n + 1)
                    if part == 3:
                        nc.scalar.activation(hv[b][:, 0:2, :], bank[0][:, :].rearrange("p (b n) -> p b n", b=2), ACT.Copy)
                        last = nc.scalar.activation(hv[b][:, 2, :], bank[1][:, 0:256], ACT.Copy)
                    else:
                        for h2 in range(2):
                            z = bank[h2][:, 0:T]
                            if part == 0:
                                last = nc.scalar.activation(hq[b][:, h2, :], z, ACT.Copy)
                            elif part == 4:
                                last = nc.scalar.activation(sg[b][:, h2, :], z, ACT.Silu)
                            else:
                                nc.scalar.activation(hp_[b][part - 1][:, h2, :], z, ACT.Sigmoid)
                                last = nc.scalar.activation(hk[b][part - 1][:, h2, :], z, ACT.Sigmoid, scale=-1.0)
                    last.then_inc(s_pj, 1)
                    if part == 0:
                        for d in range(2):
                            act.dma_start(st0[b][:, d, :, :],
                                          state_hgrn[0, 0, d, 2 * pair:2 * pair + 2].rearrange("h k v -> k h v")
                                          ).then_inc(s_st0[b], 16)
                    next_hi(n)

                def after_unit(u):
                    h2, d, head = u // 2 % 2, u % 2, u // 2
                    act.wait_ge(s_sf, u + 1)
                    act.dma_start(new_state[0, 0, d, head], sfin[:, 2 * h2 + d, :]).then_inc(s_sfo[2 * h2 + d], 16)
                    if d == 1:
                        act.wait_ge(s_ud, 2 * head + 2)
                        nc.scalar.activation(osq[:, :], ps[6][:, 0:T], ACT.Square).then_inc(s_osq, 1)

                def root(head):
                    act.wait_ge(s_ge, fill_no[2 * head + 2, "mean"] + 1)
                    nc.scalar.activation(orr[:, :], orr[:, :], ACT.Sqrt).then_inc(s_ort, 1)

                def y_hi(head):
                    act.wait_ge(s_oy, head + 1)
                    nc.scalar.activation(xh[:, head, :], y_all[:, head, :], ACT.Copy).then_inc(s_oh, 1)

                for pair in range(5):
                    for part in range(5):
                        u = 4 * (pair - 1) + part
                        if pair and part in (0, 2) and u:
                            root(u // 2 - 1)
                        if pair < 4:
                            copy_chunk(pair, part)
                        elif part == 0:
                            for head in range(6):
                                y_hi(head)
                        elif part == 2:
                            y_hi(6)
                        if pair and part < 4:
                            after_unit(u)
                root(7)
                y_hi(7)
                for slot in s_sfo:
                    act.wait_ge(slot, 16 * 4)
                for i in range(4):
                    act.wait_ge(s_used, n0 + 20 + i + 1)
                    next_hi(n0 + 20 + i)

            for s, (kind, _, _) in enumerate(STAGES):
                norm(s)
                {"ffn": ffn, "mix0": mix0, "mix1": mix1}[kind](s)
            norm(n_stages)

        @block.vector
        def _(dve):
            steps = [0]

            def link(ins):
                steps[0] += 1
                ins.then_inc(s_dv, 1)
                dve.wait_ge(s_dv, steps[0])

            def split_lo(n, slot, size):
                dve.wait_ge(s_hi, n + 1)
                nc.vector.tensor_tensor(w_lo[slot][:, 0:size], w_raw[slot][:, 0:size],
                                        w_hi[slot][:, 0:size].bitcast(F32), ALU.subtract).then_inc(s_lo, 1)

            def add_bias(p, n, sums):
                nc.vector.tensor_tensor(prm[:, bass.ds(2 * p, 2 * n), :], sums,
                                        vt[:, bass.ds(V_ADAB + 2 * p, 2 * n)].unsqueeze(2).broadcast_to([P, 2 * n, 2]),
                                        ALU.add).then_inc(s_ada, n)

            def ada_half(p, half):
                if half == 0 and not (isinstance(p, int) and p == PAIRS_FIRST):
                    dve.wait_ge(s_adaT, p - PAIRS_FIRST)
                dve.wait_ge(s_adaw[half], 16 * (p - PAIRS_FIRST) + 16)
                base = 8 * (p - PAIRS_FIRST)
                for k in range(KT // 2):
                    at_k = 4 * half + k
                    if at_k:
                        dve.wait_ge(s_mac, base + at_k)
                    for cnd in range(2):
                        scalar = cond[:, at_k, cnd:cnd + 1]
                        if at_k == 0:
                            ins = nc.vector.tensor_scalar(acc[:, cnd, :], ada[half][:, k, :], scalar, None, ALU.mult)
                        else:
                            ins = nc.vector.scalar_tensor_tensor(acc[:, cnd, :], ada[half][:, k, :], scalar,
                                                                 acc[:, cnd, :], ALU.mult, ALU.add)
                    ins.then_inc(s_mac, 1)

            def ada_sum(p):
                dve.wait_ge(s_adaT, p - PAIRS_FIRST + 1)
                nc.vector.reduce_sum(asum[:, :], ps[7][:, :].rearrange("p (a q) -> p a q", a=4), AX).then_inc(s_asum, 1)
                dve.wait_ge(s_asum, p - PAIRS_FIRST + 1)
                add_bias(p, 1, asum[:, :].rearrange("p (c a) -> p a c", c=2))

            dve.wait_ge(s_vT, 1)
            nc.vector.tensor_copy(vt[:, 0:V_END], ps[6][:, 0:V_END]).then_inc(s_vt, 1)
            dve.wait_ge(s_vt, 1)
            lg = vt[:, V_LB:V_LB + 4 * HG_HEADS].rearrange("p (l e) -> p l e", l=2)
            link(nc.vector.tensor_tensor(lb[:, 0, :], lg[:, 0, :], lg[:, 1, :], ALU.max))
            link(nc.vector.memset(lb[:, 5, 0:1], EPS))
            link(nc.vector.tensor_tensor(lb[:, 1, :], lg[:, 0, :], lb[:, 0, :], ALU.subtract))
            nc.vector.tensor_tensor(lb[:, 2, :], lg[:, 1, :], lb[:, 0, :], ALU.subtract).then_inc(s_mod, 1)
            for k in range(KT):
                dve.wait_ge(s_xT, k + 1)
                nc.vector.tensor_copy(x[:, k, :], ps[k % 4][:, 0:T]).then_inc(s_x, 1)
            for i in range(2):
                split_lo(i, i, chunk_size(i))
            dve.wait_ge(s_lbe, 1)
            link(nc.vector.tensor_tensor(lb[:, 0, :], lb[:, 1, :], lb[:, 2, :], ALU.add))
            link(nc.vector.reciprocal(lb[:, 0, :], lb[:, 0, :]))
            link(nc.vector.tensor_tensor(lb[:, 1, :], lb[:, 1, :], lb[:, 0, :], ALU.mult))
            link(nc.vector.tensor_tensor(lb[:, 2, :], lb[:, 2, :], lb[:, 0, :], ALU.mult))
            link(nc.vector.tensor_tensor(lb[:, 3, :], lb[:, 1, :], lb[:, 2, :], ALU.add))
            link(nc.vector.tensor_tensor(lb[:, 3, :], lb[:, 3, :], lb[:, 1, :], ALU.subtract))
            link(nc.vector.tensor_scalar(lb[:, 4, :], lb[:, 3, :], -1.0, 1.0, ALU.mult, ALU.add))
            for q in range(QUADS):
                dve.wait_ge(s_adaP, q + 1)
                nc.vector.tensor_copy(first_rows[:, 512 * q:512 * q + 512], ps[4 + q][0:2, :]).then_inc(s_adaR, 1)
            dve.wait_ge(s_adaP, QUADS + 1)
            add_bias(0, PAIRS_FIRST, ps[4][:, 0:4 * PAIRS_FIRST].rearrange("p (a b) -> p a b", b=2))

            def norm(m):
                if m < n_stages:
                    dve.wait_ge(s_ada, norm_pairs[m])
                    sc = prm_tile(m, 1)
                    ng = vt[:, norm_col[m]:norm_col[m] + KT].unsqueeze(2).broadcast_to([P, KT, 2])
                    nc.vector.scalar_tensor_tensor(mod_a[:, :, :], prm[:, sc:sc + KT, :], 1.0, ng,
                                                   ALU.add, ALU.mult).then_inc(s_mod, 1)
                    dve.wait_ge(s_mod, m + 2)
                dve.wait_ge(s_rs, m + 1)
                link(nc.vector.reciprocal(rr[:, :], rr[:, :]))

                if m == n_stages:
                    for k in range(KT):
                        nc.vector.scalar_tensor_tensor(xf[:, k, :], x[:, k, :], vt[:, V_NF + k:V_NF + k + 1],
                                                       rr[:, :], ALU.mult, ALU.mult).then_inc(s_xr, 1)
                    return
                def scaled(k):
                    for cnd, a, b in GROUPS:
                        last = nc.vector.scalar_tensor_tensor(xf[:, k, a:b], x[:, k, a:b], mod_a[:, k, cnd:cnd + 1],
                                                              rr[:, a:b], ALU.mult, ALU.mult)
                    last.then_inc(s_xr, 1)

                def low(k):
                    dve.wait_ge(s_xh, 8 * m + k + 1)
                    for cnd, a, b in GROUPS:
                        last = nc.vector.scalar_tensor_tensor(xl[:, k, a:b], xf[:, k, a:b],
                                                              prm[:, prm_tile(m, 0) + k, cnd:cnd + 1],
                                                              xh[:, k, a:b].bitcast(F32), ALU.add, ALU.subtract)
                    last.then_inc(s_xl, 1)

                scaled(0)
                scaled(1)
                for k in range(KT):
                    if k + 2 < KT:
                        scaled(k + 2)
                    low(k)

            def gates(s):
                dve.wait_ge(s_ada, norm_pairs[s] + 4)
                g = prm_tile(s, 2)
                link(nc.vector.tensor_scalar(hgate[:, :, :], prm[:, g:g + KT, :],
                                             0.5 if STAGES[s][0] == "ffn" else 1.0, None, ALU.mult))

            def residual(k, bank):
                for cnd, a, b in GROUPS:
                    last = nc.vector.scalar_tensor_tensor(
                        x[:, bass.ds(k, 1), a:b].rearrange("p a t -> p (a t)"), bank[:, a:b],
                        hgate[:, bass.ds(k, 1), cnd], x[:, bass.ds(k, 1), a:b].rearrange("p a t -> p (a t)"),
                        ALU.mult, ALU.add)
                last.then_inc(s_x, 1)

            def ffn(s):
                n0, g0 = BASE[s], gh0[s]
                pa = pair_at[s]
                n_w1 = min(n_pairs[s], FT // 2)
                fresh = s == 0

                def w1_tile(cc, slot, size, p, first=False):
                    n = n0 + cc
                    split_lo(n + 2, slot, size)
                    dve.wait_ge(s_sa, g0 + cc + 1)
                    nc.vector.tensor_tensor(g_raw[slot][:, :], silu_a[slot][:, :], ps[2 * slot + 1][:, 0:T],
                                            ALU.mult).then_inc(s_gm, 1)
                    if p is not None:
                        if slot == 0 and not first:
                            ada_sum(p - 1)
                        ada_half(p, slot)
                    dve.wait_ge(s_gh, g0 + cc + 1)
                    nc.vector.tensor_tensor(gg[:, bass.ds(cc, 1), 1, :].rearrange("p a t -> p (a t)"),
                                            g_raw[slot][:, :],
                                            gg[:, bass.ds(cc, 1), 0, :].rearrange("p a t -> p (a t)").bitcast(F32),
                                            ALU.subtract).then_inc(s_gl, 1)

                for slot in range(2):
                    w1_tile(slot, slot, KT * 256, pa, fresh)
                with dve.Fori(1, min(n_w1, FT // 2 - 1)) as i:
                    for slot in range(2):
                        w1_tile(2 * i + slot, slot, KT * 256, pa + i)
                if n_w1 < FT // 2 - 1:
                    ada_sum(n_all - 1)
                    with dve.Fori(n_w1, FT // 2 - 1) as i:
                        for slot in range(2):
                            w1_tile(2 * i + slot, slot, KT * 256, None)
                for slot in range(2):
                    w1_tile(FT - 2 + slot, slot, HALF * P, pa + n_w1 - 1 if n_w1 == FT // 2 else None)
                gates(s)

                def w2_tile(d, e, size, p):
                    n = n0 + FT + 2 * d
                    if size:
                        split_lo(n + 2, 0, size)
                    if p is not None:
                        if e == 0:
                            ada_sum(p - 1)
                        ada_half(p, e)
                    if size:
                        split_lo(n + 3, 1, size)
                    dve.wait_ge(s_used, n + 2)
                    residual(d, ps[4 + e])

                looped = n_pairs[s] > n_w1
                with dve.Fori(0, KT // 2 - 1) as i:
                    for e in range(2):
                        w2_tile(2 * i + e, e, HALF * P, pa + n_w1 + i if looped else None)
                for e in range(2):
                    w2_tile(KT - 2 + e, e, chunk_size(BASE[s + 1]) if e else HALF * P,
                            pa + n_w1 + KT // 2 - 1 if looped else None)

            def next_lo(n):
                if chunk_size(n + 2):
                    split_lo(n + 2, n % 2, chunk_size(n + 2))

            def out_projection(s, n, pairs):
                gates(s)
                for i in range(4):
                    next_lo(n + i)
                    dve.wait_ge(s_used, n + i + 1)
                    for e in range(2):
                        residual(2 * i + e, ps[2 * (i % 2) + e])
                    if i < len(pairs):
                        ada_sum(pairs[i] - 1)
                        for half in range(2):
                            ada_half(pairs[i], half)

            def mix0(s):
                n0 = BASE[s]
                for i in range(8):
                    next_lo(n0 + i)
                    ada_sum(pair_at[s] + i - 1)
                    for half in range(2):
                        ada_half(pair_at[s] + i, half)
                dve.wait_ge(s_ckT, 1)
                nc.vector.tensor_copy(ckT[:, :, :].rearrange("p a t -> p (a t)"), ps[6][:, :]).then_inc(s_ckv, 1)
                dve.wait_ge(s_nkT, 1)
                nc.vector.tensor_copy(nk[:, :], ps[6][:, :]).then_inc(s_nk, 1)
                for f in range(6):
                    dve.wait_ge(s_fo, f + 1)
                    tb, gp = f // 2, f % 2
                    nc.vector.tensor_copy(ab[:, tb, 2 * gp:2 * gp + 2, :],
                                          ps[f % 4][:, :].rearrange("p (g c) -> p g c", g=2)).then_inc(s_foe, 1)
                for g in range(4):
                    dve.wait_ge(s_foh, g + 1)
                    nc.vector.tensor_tensor(gg[:, 4 + g, 1, :], ps[(6 + g) % 4][:, 0:T],
                                            gg[:, 4 + g, 0, :].bitcast(F32), ALU.subtract).then_inc(s_foe, 1)

                def maxes(u):
                    width = NP_ if units[u][2] == 0 else T
                    dve.wait_ge(s_sc, u + 1)
                    link(nc.vector.reduce_max(smax[:, u:u + 1], ps[u % 2][:, 0:width], AX))
                    nc.vector.tensor_scalar(smax[:, u:u + 1], smax[:, u:u + 1], -1.0, None, ALU.mult).then_inc(s_mx, 1)

                def attn_lo(pair):
                    dve.wait_ge(s_ath, pair + 1)
                    nc.vector.tensor_tensor(gg[:, pair, 1, :], ps[4 + pair % 2][:, 0:T],
                                            gg[:, pair, 0, :].bitcast(F32), ALU.subtract).then_inc(s_at, 1)

                maxes(0)
                for u in range(24):
                    if u + 1 < 24:
                        maxes(u + 1)
                    width = NP_ if units[u][2] == 0 else T
                    dve.wait_ge(s_exp, u + 1)
                    link(nc.vector.reciprocal(srec[:, u:u + 1], ssum[:, u:u + 1]))
                    nc.vector.tensor_scalar(prob[u % 2][:, 0:width], prob[u % 2][:, 0:width],
                                            srec[:, u:u + 1], None, ALU.mult).then_inc(s_pn, 1)
                    if u % 6 == 2 and u > 6:
                        attn_lo(u // 6 - 1)
                attn_lo(3)
                out_projection(s, n0 + 8, [pair_at[s] + 8 + i for i in range(3)])

            def mix1(s):
                n0 = BASE[s]

                def level(u, lv):
                    pair, h2, d = u // 4, u // 2 % 2, u % 2
                    if lv == 0 and u >= 2:
                        dve.wait_ge(s_ud, u - 1)
                    tq, ks, b = 1 - d, d, pair % 2
                    q, pr, k, r, m = (blk(a, lv) for a in (hq[b][:, h2, :], hp_[b][d][:, h2, :], hk[b][d][:, h2, :],
                                                           hr[u % 2][:, :], hm[u % 2][:, lv, :]))
                    w = 1 << lv
                    end = w - 1 if d == 0 else 0
                    nc.vector.tensor_tensor(m[:, :, tq, :], q[:, :, tq, :], pr[:, :, tq, :], ALU.mult)
                    whole = [P, T // (2 * w), w]
                    if lv == 0:
                        nc.vector.tensor_copy(m[:, :, ks, :], k[:, :, ks, :])
                        nc.vector.memset(r[:, :, tq, :], 1.0)
                        link(nc.vector.tensor_copy(r[:, :, ks, :], pr[:, :, tq, :]))
                    else:
                        nc.vector.tensor_tensor(m[:, :, ks, :], k[:, :, ks, :], r[:, :, ks, :], ALU.mult)
                        link(nc.vector.tensor_tensor(r[:, :, ks, :], r[:, :, ks, :],
                                                     pr[:, :, tq, end:end + 1].broadcast_to(whole), ALU.mult))
                    link(nc.vector.tensor_tensor(pr[:, :, tq, :], pr[:, :, tq, :],
                                                 pr[:, :, ks, end:end + 1].broadcast_to(whole), ALU.mult))
                    if lv == LEVELS - 1:
                        nc.vector.tensor_tensor(qi[u % 2], hq[b][:, h2, :], hp_[b][d][:, h2, :], ALU.mult)
                        nc.vector.tensor_tensor(ki[u % 2], hk[b][d][:, h2, :], hr[u % 2][:, :],
                                                ALU.mult).then_inc(s_un, 1)

                def evac(u, kind):
                    pair, h2, d = u // 4, u // 2 % 2, u % 2
                    g = fill_no[u, kind]
                    bank = fill_bank(g)
                    dve.wait_ge(s_gb, g + 1)
                    if kind == "diag":
                        nc.vector.tensor_tensor(gd[:, :].rearrange("p (c t) -> p c t", c=3),
                                                bank[:, 0:T].rearrange("p (c t) -> p c t", c=3),
                                                ident.unsqueeze(1).broadcast_to([P, 3, P]), ALU.mult).then_inc(s_ge, 1)
                    elif kind[:5] == "level":
                        mask = cst[:, C_MASK + d * LEVELS * 64:C_MASK + (d + 1) * LEVELS * 64]
                        nc.vector.tensor_tensor(gm[int(kind[5])][:, :], bank[:, 0:LEVELS * 64], mask, ALU.mult).then_inc(s_ge, 1)
                    elif kind == "turn":
                        nc.vector.tensor_copy(ktok[:, :, :], bank[:, 0:256].rearrange("p (a k) -> p a k", a=2)).then_inc(s_ge, 1)
                    elif kind == "state":
                        first = 1 if d == 0 else 2
                        col = first * P + (P - 1 if d == 0 else 0)
                        if pair:
                            dve.wait_ge(s_sfo[2 * h2 + d], 16 * pair)
                        nc.vector.tensor_copy(sfin[:, 2 * h2 + d, :], bank[:, 0:P]).then_inc(s_sf, 1)
                        dve.wait_ge(s_st0[pair % 2], 32 * (pair // 2 + 1))
                        nc.vector.scalar_tensor_tensor(st1[:, :], st0[pair % 2][:, d, h2, :],
                                                       hp_[pair % 2][d][:, h2, col:col + 1],
                                                       bank[:, P:2 * P], ALU.mult, ALU.add).then_inc(s_ge, 1)
                    else:
                        nc.vector.tensor_scalar(orr[:, :], bank[:, 0:T], EPS, None, ALU.add).then_inc(s_ge, 1)

                def finish(head):
                    evac(2 * head + 2, "mean")
                    nc.vector.scalar_tensor_tensor(y_all[:, head, :], ps[6][:, 0:T], vt[:, V_HG:V_HG + 1],
                                                   sg[head // 2 % 2][:, head % 2, :], ALU.mult, ALU.mult).then_inc(s_yo, 1)

                def scale_y(head):
                    y = y_all[:, head, :]
                    dve.wait_ge(s_yo, head + 1)
                    dve.wait_ge(s_ort, head + 1)
                    link(nc.vector.reciprocal(orr[:, :], orr[:, :]))
                    nc.vector.tensor_tensor(y, y, orr[:, :], ALU.mult).then_inc(s_oy, 1)

                def y_lo(head):
                    dve.wait_ge(s_oh, head + 1)
                    nc.vector.tensor_tensor(xl[:, head, :], y_all[:, head, :], xh[:, head, :].bitcast(F32),
                                            ALU.subtract).then_inc(s_ol, 1)

                def decays(pair, d):
                    dve.wait_ge(s_pj, pj0[s] + 5 * pair + d + 2)
                    for h2 in range(2):
                        cc = d * HG_HEADS + 2 * pair + h2
                        f, k = hp_[pair % 2][d][:, h2, :], hk[pair % 2][d][:, h2, :]
                        nc.vector.tensor_scalar(f, f, lb[:, 4, cc:cc + 1], lb[:, 3, cc:cc + 1], ALU.mult, ALU.add)
                        last = nc.vector.tensor_scalar(k, k, lb[:, 4, cc:cc + 1], None, ALU.mult)
                    link(last)

                for pair in range(5):
                    for part in range(5):
                        u = 4 * (pair - 1) + part
                        has_unit = pair > 0 and part < 4
                        new_head = has_unit and u % 2 == 0 and u > 0
                        if has_unit:
                            for kind in ["diag"] * (u % 2 == 0) + ["level0", "level1", "level2", "turn"]:
                                evac(u, kind)
                        if new_head:
                            finish(u // 2 - 1)
                        if pair < 4 and part in (2, 3):
                            decays(pair, part - 2)
                        nxt = u + 1 if pair and part < 3 else 4 * pair if part == 4 and pair < 4 else None
                        if nxt is not None:
                            for lv in range(LEVELS):
                                level(nxt, lv)
                        if new_head:
                            scale_y(u // 2 - 1)
                        if has_unit:
                            evac(u, "state")
                        if pair < 4:
                            next_lo(n0 + 5 * pair + part)
                        elif part == 0:
                            for head in range(6):
                                y_lo(head)
                        elif part == 2:
                            y_lo(6)
                        if pair == 0:
                            ada_sum(pair_at[s] + part - 1)
                            for half in range(2):
                                ada_half(pair_at[s] + part, half)
                finish(7)
                scale_y(7)
                y_lo(7)
                out_projection(s, n0 + 20, [])

            for s, (kind, _, _) in enumerate(STAGES):
                norm(s)
                {"ffn": ffn, "mix0": mix0, "mix1": mix1}[kind](s)
            norm(n_stages)
            for f in range(2 * TB):
                tb, half = f // 2, f % 2
                dve.wait_ge(s_yT, f + 1)
                nc.vector.tensor_copy(y_stage(tb)[:, half * 512:half * 512 + 512], ps[f % 2][:, :]).then_inc(s_yo2, 1)

        @block.tensor
        def _(pe):
            def mm3(out, a, b, first, last):
                (ah, al), (bh, bl) = a, b
                nc.tensor.matmul(out, ah, bh, start=first, stop=False)
                nc.tensor.matmul(out, ah, bl, start=False, stop=False)
                return nc.tensor.matmul(out, al, bh, start=False, stop=last)

            def hidden(k, a=0, b=T):
                return gg[:, k, 0, a:b], gg[:, k, 1, a:b]

            def normed(k, a=0, b=T):
                return xh[:, k, a:b], xl[:, k, a:b]

            def wtile(slot, k, width, a, b):
                return (w_hi[slot][:, k * width + a:k * width + b], w_lo[slot][:, k * width + a:k * width + b])

            def ada_turn(p):
                pe.wait_ge(s_mac, 8 * (p - PAIRS_FIRST) + 8)
                pe.wait_ge(s_ada, p)
                for e in range(4):
                    last = nc.tensor.transpose(ps[7][:, e * P:(e + 1) * P],
                                               acc[:, e // 2, e % 2 * P:(e % 2 + 1) * P], ident)
                last.then_inc(s_adaT, 1)

            pe.wait_ge(s_cst, 16)
            pe.wait_ge(s_vrow, 16 * 8)
            nc.tensor.transpose(ps[6][:, 0:P], vrow[:, 0, :], ident)
            nc.tensor.transpose(ps[6][:, P:V_END], vrow[0:V_END - P, 1, :],
                                cst[0:V_END - P, C_ID:C_ID + V_END - P]).then_inc(s_vT, 1)
            pe.wait_ge(s_xin, 32)
            xin = xf[:, :, :].rearrange("p k t -> p (k t)").rearrange("p (b d) -> p b d", b=TB)
            for k in range(KT):
                if k >= 4:
                    pe.wait_ge(s_x, k - 3)
                for tb in range(TB):
                    last = nc.tensor.transpose(ps[k % 4][:, tb * P:(tb + 1) * P], xin[:, tb, k * P:(k + 1) * P], ident)
                last.then_inc(s_xT, 1)
            pe.wait_ge(s_cond, 1)
            for q in range(QUADS):
                pe.wait_ge(s_first[q], 32)
                for k in range(KT):
                    last = nc.tensor.matmul(ps[4 + q][0:2, :], cond[:, k, :], first_ada[q][:, k, :],
                                            start=(k == 0), stop=(k == KT - 1))
                last.then_inc(s_adaP, 1)
            pe.wait_ge(s_adaR, QUADS)
            for e in range(2 * PAIRS_FIRST):
                last = nc.tensor.transpose(ps[4][:, 2 * e:2 * e + 2], first_rows[:, e * P:(e + 1) * P],
                                           cst[0:2, C_ID:C_ID + 2])
            last.then_inc(s_adaP, 1)

            def norm(m):
                for k in range(KT):
                    pe.wait_ge(s_sq, 8 * m + k + 1)
                    last = nc.tensor.matmul(ps[6][:, 0:T], cst[:, C_MEAN:C_MEAN + P], xf[:, k, :],
                                            start=(k == 0), stop=(k == KT - 1))
                last.then_inc(s_ms, 1)

            def first_products(m, outs, ws):
                for k in range(KT):
                    pe.wait_ge(s_xh, 8 * m + k + 1)
                    for e, out in enumerate(outs):
                        for w in ws[2 * k + e]:
                            nc.tensor.matmul(out, w, xh[:, k, :], start=(k == 0 and w is ws[e][0]), stop=False)
                for k in range(KT):
                    pe.wait_ge(s_xl, 8 * m + k + 1)
                    for e, out in enumerate(outs):
                        last = nc.tensor.matmul(out, ws[2 * k + e][0], xl[:, k, :], start=False, stop=(k == KT - 1))
                return last

            def features(m, n, slot, first):
                pe.wait_ge(s_lo, n + 1)
                outs = [ps[2 * slot + e][:, 0:T] for e in range(2)]
                ws = [wtile(slot, k, 256, e * P, (e + 1) * P) for k in range(KT) for e in range(2)]
                if first:
                    last = first_products(m, outs, ws)
                else:
                    for k in range(KT):
                        for e in range(2):
                            last = mm3(outs[e], ws[2 * k + e], normed(k), k == 0, k == KT - 1)
                last.then_inc(s_used, 1)

            def tokens(n, slot):
                pe.wait_ge(s_lo, n + 1)
                for tb in range(TB):
                    out = ps[2 * slot + tb // 2][:, tb % 2 * 256:tb % 2 * 256 + 256]
                    for k in range(KT):
                        last = mm3(out, normed(k, tb * P, (tb + 1) * P), wtile(slot, k, 256, 0, 256),
                                   k == 0, k == KT - 1)
                last.then_inc(s_used, 1)

            def out_products(i, parts, k0, k1):
                slot = i % 2
                for k in range(k0, k1):
                    for e in range(2):
                        last = mm3(ps[2 * slot + e][:, 0:T], wtile(slot, k, 256, e * P, (e + 1) * P), parts(k),
                                   k == 0, k == KT - 1)
                if k1 == KT:
                    last.then_inc(s_used, 1)

            def out_projection(s, n, parts, pairs, ahead=0):
                for i in range(4):
                    if i < len(pairs):
                        ada_turn(pairs[i] - 1)
                    pe.wait_ge(s_lo, n + i + 1)
                    if i >= 2:
                        pe.wait_ge(s_x, 8 * (s + 1) + 2 * (i - 1))
                    out_products(i, parts, ahead if i < 2 else 0, KT)

            def ffn(s):
                n0, g0 = BASE[s], gh0[s]
                pa = pair_at[s]
                n_w1 = min(n_pairs[s], FT // 2)

                def w1_tile(cc, slot, first, guard):
                    if guard:
                        pe.wait_ge(s_gm, g0 + cc - 1)
                    pe.wait_ge(s_lo, n0 + cc + 1)
                    outs = [ps[2 * slot + e][:, 0:T] for e in range(2)]
                    ws = [[(w[slot][:, (e * KT + k) * P:(e * KT + k + 1) * P]) for w in (w_hi, w_lo)]
                          for k in range(KT) for e in range(2)]
                    if first:
                        last = first_products(s, outs, ws)
                    else:
                        for k in range(KT):
                            for e in range(2):
                                last = mm3(outs[e], ws[2 * k + e], normed(k), k == 0, k == KT - 1)
                    last.then_inc(s_used, 1)

                w1_tile(0, 0, True, False)
                if s:
                    ada_turn(pa - 1)
                w1_tile(1, 1, False, False)
                with pe.Fori(1, n_w1) as i:
                    w1_tile(2 * i, 0, False, True)
                    ada_turn(pa + i - 1)
                    w1_tile(2 * i + 1, 1, False, True)
                if n_w1 < FT // 2:
                    w1_tile(2 * n_w1, 0, False, True)
                    ada_turn(n_all - 1)
                    w1_tile(2 * n_w1 + 1, 1, False, True)
                    with pe.Fori(n_w1 + 1, FT // 2) as i:
                        for slot in range(2):
                            w1_tile(2 * i + slot, slot, False, True)

                def w2_tile(d, bank, guard):
                    if guard:
                        pe.wait_ge(s_x, 8 * (s + 1) + d - 1)
                    for half in range(2):
                        pe.wait_ge(s_lo, n0 + FT + 2 * d + half + 1)
                        pe.wait_ge(s_gl, g0 + HALF * (half + 1))
                        for kk in range(HALF):
                            last = mm3(bank[:, 0:T], wtile(half, kk, P, 0, P), hidden(half * HALF + kk),
                                       half == 0 and kk == 0, half == 1 and kk == HALF - 1)
                        last.then_inc(s_used, 1)

                looped = n_pairs[s] > n_w1
                w2_tile(0, ps[4], False)
                if looped:
                    ada_turn(pa + n_w1 - 1)
                w2_tile(1, ps[5], False)
                with pe.Fori(1, KT // 2) as i:
                    w2_tile(2 * i, ps[4], True)
                    if looped:
                        ada_turn(pa + n_w1 + i - 1)
                    w2_tile(2 * i + 1, ps[5], True)

            def mix0(s):
                n0 = BASE[s]
                for i in range(8):
                    slot = i % 2
                    if i >= 2:
                        pe.wait_ge(s_pj, pj0[s] + i - 1)
                    if i // 2 == 2:
                        tokens(n0 + i, slot)
                    else:
                        features(s, n0 + i, slot, i == 0)
                    ada_turn(pair_at[s] + i - 1)
                pe.wait_ge(s_kv, 48)
                pe.wait_ge(s_rs, s + 1)
                for e in range(4):
                    last = nc.tensor.transpose(ps[6][:, e * P:(e + 1) * P], ck[:, e * P:(e + 1) * P], ident)
                last.then_inc(s_ckT, 1)
                pe.wait_ge(s_pj, pj0[s] + 8)
                pe.wait_ge(s_ckv, 1)
                for e in range(4):
                    last = nc.tensor.transpose(ps[6][:, e * P:(e + 1) * P], kT[:, e, 0:P], ident)
                last.then_inc(s_nkT, 1)
                for f in range(6):
                    tb, gp = f // 2, f % 2
                    if f >= 4:
                        pe.wait_ge(s_foe, f - 3)
                    for e in range(2):
                        g = 2 * gp + e
                        last = nc.tensor.matmul(ps[f % 4][:, e * 256:e * 256 + 256], fT[:, g, tb * P:(tb + 1) * P],
                                                dft[:, 0:2 * P], start=True, stop=True)
                    last.then_inc(s_fo, 1)
                pe.wait_ge(s_foe, 6)
                for g in range(4):
                    if g >= 2:
                        pe.wait_ge(s_foe, 6 + g - 1)
                    bank = ps[(6 + g) % 4]
                    for e in range(2):
                        nc.tensor.matmul(bank[:, 0:P], ab[:, 0, g, e * P:(e + 1) * P],
                                         dft[:, C_DT128 - C_KEEP + e * P:C_DT128 - C_KEEP + (e + 1) * P],
                                         start=(e == 0), stop=(e == 1))
                    for tt in range(2):
                        for e in range(2):
                            at_ = C_DT256 - C_KEEP + (2 * tt + e) * NS_
                            last = nc.tensor.matmul(bank[:, NP_:T], ab[:, 1 + tt, g, e * P:(e + 1) * P],
                                                    dft[:, at_:at_ + NS_], start=(tt == 0 and e == 0),
                                                    stop=(tt == 1 and e == 1))
                    last.then_inc(s_fo, 1)
                pe.wait_ge(s_foe, 10)
                pe.wait_ge(s_bias, 4)

                def scores(u):
                    pair, h2, what = units[u]
                    rows = slice(HD * h2, HD * h2 + HD)
                    bank = ps[u % 2]
                    if u >= 2:
                        pe.wait_ge(s_exp, u - 1)
                    if what == 0:
                        nc.tensor.matmul(bank[:, 0:P], qT[rows, pair, 0:P], kT[rows, pair, 0:P],
                                         start=True, stop=True).then_inc(s_sc, 1)
                        return
                    b = what - 1
                    q = qT[rows, pair, NP_ + b * P:NP_ + (b + 1) * P]
                    nc.tensor.matmul(bank[:, 0:NS_], q, kT[rows, pair, NP_:T], start=True, stop=False)
                    tab = bias[:, 2 * pair + h2, 2 - 2 * b:6 - 2 * b, :].rearrange("p r c -> p (r c)")
                    nc.tensor.matmul(bank[:, 0:NS_], anti, tab, start=False, stop=True)
                    nc.tensor.matmul(bank[:, NS_:T], q, ckT[rows, pair, :], start=True, stop=True).then_inc(s_sc, 1)

                def turn(u):
                    n = 1 if units[u][2] == 0 else 3
                    pe.wait_ge(s_pn, u + 1)
                    if u >= 2:
                        pe.wait_ge(s_pt, u - 1)
                    for e in range(n):
                        last = nc.tensor.transpose(ps[2 + u % 2][:, e * P:(e + 1) * P], prob[u % 2][:, e * P:(e + 1) * P], ident)
                    last.then_inc(s_tr, 1)

                def values(u):
                    pair, h2, what = units[u]
                    head = 2 * pair + h2
                    cols = slice(head * HD, head * HD + HD)
                    if u % 6 == 0 and pair >= 2:
                        pe.wait_ge(s_at, pair - 1)
                    pe.wait_ge(s_pt, u + 1)
                    out = ps[4 + pair % 2][HD * h2:HD * h2 + HD, what * P:(what + 1) * P]
                    vals = [vtok[:, 0, cols]] if what == 0 else [vtok[:, 1, cols], vtok[:, 2, cols], cv[:, cols]]
                    for e, v in enumerate(vals):
                        last = nc.tensor.matmul(out, v, probT[u % 2][:, e * P:(e + 1) * P],
                                                start=(e == 0), stop=(e == len(vals) - 1))
                    last.then_inc(s_pv, 1)

                scores(0)
                scores(1)
                for u in range(24):
                    turn(u)
                    if u + 2 < 24:
                        scores(u + 2)
                    if u:
                        values(u - 1)
                values(23)
                pe.wait_ge(s_at, 4)
                out_projection(s, n0 + 8, hidden, [pair_at[s] + 8 + i for i in range(3)])

            def mix1(s):
                n0 = BASE[s]

                def next_bank(u, kind):
                    g = fill_no[u, kind]
                    if g >= 3:
                        pe.wait_ge(s_ge, g - 2)
                    return fill_bank(g)

                def mean(head):
                    bank = next_bank(2 * head + 2, "mean")
                    pe.wait_ge(s_osq, head + 1)
                    nc.tensor.matmul(bank[:, 0:T], cst[:, C_MEANH:C_MEANH + P], osq[:, :],
                                     start=True, stop=True).then_inc(s_gb, 1)

                def unit_first(u):
                    h2, d, b = u // 2 % 2, u % 2, u // 4 % 2
                    m = hm[u % 2]
                    pe.wait_ge(s_un, u + 1)
                    if d == 0:
                        bank = next_bank(u, "diag")
                        for cc in range(3):
                            for e in range(2):
                                last = nc.tensor.matmul(bank[:, cc * P:(cc + 1) * P], hk[b][e][:, h2, cc * P:(cc + 1) * P],
                                                        hq[b][:, h2, cc * P:(cc + 1) * P], start=(e == 0), stop=(e == 1))
                        last.then_inc(s_gb, 1)
                    for cc in range(3):
                        bank = next_bank(u, f"level{cc}")
                        for lv in range(LEVELS):
                            rhs = blk(m[:, lv, cc * P:(cc + 1) * P], lv)[:, :, 1 - d, :]
                            last = nc.tensor.matmul(bank[:, lv * 64:(lv + 1) * 64], m[:, lv, cc * P:(cc + 1) * P],
                                                    rhs, start=True, stop=True)
                        last.then_inc(s_gb, 1)
                    first = 1 if d == 0 else 2
                    bank = next_bank(u, "turn")
                    nc.tensor.transpose(bank[:, 0:P], ki[u % 2][:, 0:P], ident)
                    nc.tensor.transpose(bank[:, P:2 * P], ki[u % 2][:, first * P:(first + 1) * P], ident).then_inc(s_gb, 1)

                def unit_second(u):
                    pair, h2, d, b = u // 4, u // 2 % 2, u % 2, u // 4 % 2
                    head = 2 * pair + h2
                    o = ps[6]
                    vcols = slice(h2 * P, (h2 + 1) * P)
                    first = 1 if d == 0 else 2
                    second = 3 - first
                    bank = next_bank(u, "state")
                    pe.wait_ge(s_ge, fill_no[u, "turn"] + 1)
                    nc.tensor.matmul(bank[:, 0:P], ktok[:, 0, :], hv[b][:, 0, vcols], start=True, stop=True)
                    nc.tensor.matmul(bank[:, P:2 * P], ktok[:, 1, :], hv[b][:, first, vcols],
                                     start=True, stop=True).then_inc(s_gb, 1)
                    if d == 0:
                        if head:
                            pe.wait_ge(s_yo, head)
                        for cc in range(3):
                            nc.tensor.matmul(o[:, cc * P:(cc + 1) * P], hv[b][:, cc, vcols], gd[:, cc * P:(cc + 1) * P],
                                             start=(cc == 0), stop=False, skip_group_check=True)
                    for cc in range(3):
                        for lv in range(LEVELS):
                            out = blk(o[:, cc * P:(cc + 1) * P], lv)[:, :, 1 - d, :]
                            masked = gm[cc][:, lv * 64:(lv + 1) * 64].rearrange("p (b w) -> p b w", w=1 << lv)
                            nc.tensor.matmul(out, hv[b][:, cc, vcols], masked,
                                             start=False, stop=False, skip_group_check=True)
                    pe.wait_ge(s_st0[b], 32 * (pair // 2 + 1))
                    nc.tensor.matmul(o[:, first * P:(first + 1) * P], st0[b][:, d, h2, :],
                                     qi[u % 2][:, first * P:(first + 1) * P], start=False, stop=False, skip_group_check=True)
                    pe.wait_ge(s_ge, fill_no[u, "state"] + 1)
                    nc.tensor.matmul(o[:, second * P:(second + 1) * P], st1[:, :],
                                     qi[u % 2][:, second * P:(second + 1) * P], start=False, stop=True,
                                     skip_group_check=True).then_inc(s_ud, 1)

                for pair in range(5):
                    for part in range(5):
                        u = 4 * (pair - 1) + part
                        has_unit = pair > 0 and part < 4
                        if has_unit:
                            unit_first(u)
                            if u % 2 == 0 and u:
                                mean(u // 2 - 1)
                        if pair < 4:
                            i = 5 * pair + part
                            if i >= 2:
                                pe.wait_ge(s_pj, pj0[s] + i - 1)
                            if part == 3:
                                tokens(n0 + i, i % 2)
                            else:
                                features(s, n0 + i, i % 2, i == 0)
                        elif part in (1, 2):
                            if part == 1:
                                pe.wait_ge(s_pj, pj0[s] + 20)
                                pe.wait_ge(s_ol, 6)
                            pe.wait_ge(s_lo, n0 + 20 + part)
                            out_products(part - 1, normed, 0, 6)
                        elif part == 3:
                            pe.wait_ge(s_ol, 7)
                            for i in range(2):
                                out_products(i, normed, 6, 7)
                        if has_unit:
                            unit_second(u)
                        if pair == 0:
                            ada_turn(pair_at[s] + part - 1)
                            if part == 4:
                                pe.wait_ge(s_ada, pair_at[s] + 4)
                mean(7)
                pe.wait_ge(s_ol, HG_HEADS)
                out_projection(s, n0 + 20, normed, [], 7)

            for s, (kind, _, _) in enumerate(STAGES):
                norm(s)
                {"ffn": ffn, "mix0": mix0, "mix1": mix1}[kind](s)
            norm(n_stages)
            for f in range(2 * TB):
                tb, half = f // 2, f % 2
                pe.wait_ge(s_xr, 8 * n_stages + 8)
                if f >= 2:
                    pe.wait_ge(s_yo2, f - 1)
                for e in range(4):
                    last = nc.tensor.transpose(ps[f % 2][:, e * P:(e + 1) * P],
                                               xf[:, 4 * half + e, tb * P:(tb + 1) * P], ident)
                last.then_inc(s_yT, 1)


_INS = ['x_prompt', 'x_sample', 'cache_k', 'cache_v', 'state_hgrn', 'c', 'c_ctx', 'ada_w', 'ada_b', 'norm_g',
        'ffn_w1', 'ffn_w2', 'mix0_w_in', 'mix0_w_out', 'na_rpb', 'mix1_w_in', 'mix1_w_out',
        'hg_lb_logits', 'hg_norm_g', 'norm_f']
_OUTS = [(1, NP_, D), (1, NS_, D), (1, 1, NP_, HEADS, HD), (1, 1, NP_, HEADS, HD), (1, 1, 2, HG_HEADS, P, P)]


def kernel(**inputs):
    import concourse.bacc as bacc
    from concourse.bass_utils import run_bass_kernel_spmd as run

    nc = bacc.Bacc("TRN2", target_bir_lowering=False, num_devices=1)
    arrays, args = {}, []
    given = {name: np.ascontiguousarray(inputs[name]) for name in _INS}
    given["consts"] = shape_constants()
    for name, a in given.items():
        arrays[f"in_{name}"] = a
        args.append(nc.dram_tensor(f"in_{name}", a.shape, mybir.dt.from_np(a.dtype), kind="ExternalInput").ap())
    for i, shape in enumerate(_OUTS):
        args.append(nc.dram_tensor(f"out_{i}", shape, F32, kind="ExternalOutput").ap())
    build(nc, *args)
    r = run(nc, [arrays], core_ids=[0])
    return tuple(r.results[0][f"out_{i}"] for i in range(len(_OUTS)))
```

```python
from contextlib import ExitStack

import numpy as np

import concourse.bass as bass
from concourse import mybir

F32 = mybir.dt.float32
F32R = mybir.dt.float32r
ALU = mybir.AluOpType
ACT = mybir.ActivationFunctionType
AX = mybir.AxisListType.X

P = 128
D = 1024
KT = D // P
NP_, NS_ = 128, 256
T = NP_ + NS_
TB = T // P
DEPTH = 2
DFF = 2816
FT = DFF // P
HALF = FT // 2
NMOD = 9
GRID_W, ROWS = 64, 4
HEADS, HD = 8, 64
NAW = HEADS * HD
RPB_R, RPB_C = 15, 31
WIN_C = 16
SLOTS = 6
HG_HEADS = 8
LEVELS = 7
EPS = 1e-6
SBUF_END = 229344
NEG = -1e30
GROUPS = ((0, 0, NP_), (1, NP_, T))

V_ADAB = 0
V_NG = V_ADAB + DEPTH * NMOD * KT
V_NF = V_NG + DEPTH * 3 * KT
V_LB = V_NF + KT
V_HG = V_LB + DEPTH * 2 * HG_HEADS
V_C = V_HG + 1
V_END = V_C + 2 * KT

C_ID = 0
C_ANTI = C_ID + P
C_MEAN = C_ANTI + P
C_MEANH = C_MEAN + P
C_MASK = C_MEANH + P
C_KEEP = C_MASK + 2 * LEVELS * 64
C_DG = C_KEEP
C_DT256 = C_DG + 2 * P
C_DT128 = C_DT256 + 4 * NS_
C_END = C_DT128 + 2 * NP_


def shape_constants():
    c = np.zeros((P, C_END), np.float64)
    c[:, C_ID:C_ID + P] = np.eye(P)
    c[:, C_ANTI:C_ANTI + P] = np.eye(P)[::-1]
    c[:, C_MEAN:C_MEAN + P] = 1.0 / D
    c[:, C_MEANH:C_MEANH + P] = 1.0 / P
    s = np.arange(P)[:, None]
    j = np.arange(64)[None, :]
    for back in range(2):
        for lv in range(LEVELS):
            w = 1 << lv
            m = (s // (2 * w) == j // w) & (((s % (2 * w)) >= w) == bool(back))
            at = C_MASK + (back * LEVELS + lv) * 64
            c[:, at:at + 64] = m
    n = np.arange(P)
    ang = 2 * np.pi * ((n[:, None] * n[None, :]) % P) / P
    c[:, C_DG:C_DG + P] = np.cos(ang)
    c[:, C_DG + P:C_DG + 2 * P] = np.sin(ang)
    c[:, C_DT128:C_DT128 + P] = np.cos(ang) / np.sqrt(NP_ * P)
    c[:, C_DT128 + P:C_DT128 + 2 * P] = -np.sin(ang) / np.sqrt(NP_ * P)
    k = np.arange(NS_)
    for tt in range(2):
        a = 2 * np.pi * (((tt * P + n)[:, None] * k[None, :]) % NS_) / NS_
        at = C_DT256 + tt * 2 * NS_
        c[:, at:at + NS_] = np.cos(a) / np.sqrt(NS_ * P)
        c[:, at + NS_:at + 2 * NS_] = -np.sin(a) / np.sqrt(NS_ * P)
    return c.astype(np.float32)


STAGES = [("ffn", 0, 0), ("mix0", 0, 1), ("ffn", 0, 2), ("ffn", 1, 0), ("mix1", 1, 1), ("ffn", 1, 2)]
N_CHUNKS = {"ffn": FT + 2 * KT, "mix0": 12, "mix1": 24}
BASE = [sum(N_CHUNKS[k] for k, _, _ in STAGES[:s]) for s in range(len(STAGES) + 1)]


def chunk_size(n):
    for s, (kind, _, _) in enumerate(STAGES):
        if BASE[s] <= n < BASE[s + 1]:
            return HALF * P if kind == "ffn" and n - BASE[s] >= FT else KT * 256
    return 0


def build(nc, x_prompt, x_sample, cache_k, cache_v, state_hgrn, c, c_ctx, ada_w, ada_b, norm_g,
          ffn_w1, ffn_w2, mix0_w_in, mix0_w_out, na_rpb, mix1_w_in, mix1_w_out,
          hg_lb_logits, hg_norm_g, norm_f, consts,
          y_prompt, y_sample, new_k, new_v, new_state):
    n_stages = len(STAGES)
    total_chunks = BASE[n_stages]
    with ExitStack() as ctx:
        def sb(name, shape, dt=F32, stack=ctx):
            return stack.enter_context(nc.sbuf_tensor(name, shape, dt))

        def sem(name):
            return ctx.enter_context(nc.semaphore(name))

        ps = [ctx.enter_context(nc.psum_tensor(f"bank{i}", [P, 512], F32)) for i in range(8)]

        w_raw = [sb(f"w_raw{i}", [P, KT * 256]) for i in range(2)]
        w_hi = [sb(f"w_hi{i}", [P, KT * 256], F32R) for i in range(2)]
        w_lo = [sb(f"w_lo{i}", [P, KT * 256], F32R) for i in range(2)]
        x = sb("x", [P, KT, T])
        xh = sb("xh", [P, KT, T], F32R)
        xl = sb("xl", [P, KT, T], F32R)
        xf = sb("xf", [P, KT, T])
        ada = [sb(f"ada{i}", [P, KT // 2, 256]) for i in range(2)]
        acc = sb("acc", [P, 2, 256])
        asum = sb("asum", [P, 4])
        cst = sb("cst", [P, C_KEEP])
        vrow = sb("vrow", [P, 2, P])
        vt = sb("vt", [P, 2 * P])
        cond = sb("cond", [P, KT, 2])
        prm = sb("prm", [P, DEPTH * NMOD * KT, 2])
        mod_a = sb("mod_a", [P, KT, 2])
        hgate = sb("hgate", [P, KT, 2])
        rr = sb("rr", [P, T])
        warm = sb("warm", [P, 1])
        lb = sb("lb", [P, 6, 2 * HG_HEADS])
        gg_base = nc.sbuf_base
        gg = sb("gg", [P, FT, 2, T], F32R)
        ident = cst[:, C_ID:C_ID + P]
        anti = cst[:, C_ANTI:C_ANTI + P]

        silu_a = [sb(f"silu_a{i}", [P, T]) for i in range(2)]
        g_raw = [sb(f"g_raw{i}", [P, T]) for i in range(2)]

        arena = [gg_base + KT * 2 * T * 4]

        def at(name, shape, dt=F32):
            t = nc.alloc_sbuf_tensor_at(name, shape, dt, offset=arena[0])
            arena[0] += int(np.prod(shape[1:])) * 4
            return t

        start = arena[0]
        qT = at("qT", [P, 4, T])
        kT = at("kT", [P, 4, T])
        vtok = at("vtok", [P, TB, NAW])
        fT = at("fT", [P, 4, T])
        bias = at("bias", [P, HEADS, SLOTS, GRID_W])
        ck = at("ck", [P, NAW])
        ckT = at("ckT", [P, 4, P])
        cv = at("cv", [P, NAW])
        dft = at("dft", [P, C_END - C_KEEP])
        nk = at("nk", [P, NAW])
        prob = [at(f"prob{i}", [P, T]) for i in range(3)]
        probT = [at(f"probT{i}", [P, T]) for i in range(2)]
        smax = at("smax", [P, 24])
        ssum = at("ssum", [P, 24])
        srec = at("srec", [P, 24])
        ab = xf[:, :, :].rearrange("p k t -> p (k t)").rearrange("p (b g c) -> p b g c", b=TB, g=4)
        QUADS = 4
        arena[0] = gg_base
        first_ada = [at(f"first_ada{q}", [P, KT, 512]) for q in range(QUADS)]
        arena[0] = SBUF_END - QUADS * 512 * 4
        assert arena[0] >= nc.sbuf_base
        first_rows = at("first_rows", [2, QUADS * 512])
        arena[0] = gg_base
        y_all = at("y_all", [P, HG_HEADS, T])
        hq = [at(f"hq{i}", [P, 2, T]) for i in range(2)]
        hp_ = [[at(f"hp{i}{d}", [P, 2, T]) for d in range(2)] for i in range(2)]
        hk = [[at(f"hk{i}{d}", [P, 2, T]) for d in range(2)] for i in range(2)]
        hv = [at(f"hv{i}", [P, TB, 2 * P]) for i in range(2)]
        hr = [at(f"hr{d}", [P, T]) for d in range(2)]
        hm = [at(f"hm{i}", [P, LEVELS, T]) for i in range(2)]
        gm = [at(f"gm{i}", [P, LEVELS * 64]) for i in range(TB)]
        gd = at("gd", [P, T])
        ktok = at("ktok", [P, 2, P])
        st0 = [at(f"st0{i}", [P, 2, 2, P]) for i in range(2)]
        st1 = at("st1", [P, P])
        sfin = at("sfin", [P, 4, P])
        osq = at("osq", [P, T])
        orr = at("orr", [P, T])
        assert arena[0] <= SBUF_END
        qi = [xf[:, 2 * i, :] for i in range(2)]
        ki = [xf[:, 2 * i + 1, :] for i in range(2)]
        sg = [xf[:, 4 + 2 * i:6 + 2 * i, :] for i in range(2)]

        s_cst = sem("cst_loaded")
        s_vrow = sem("vrow_loaded")
        s_xin = sem("x_loaded")
        s_kv = sem("cache_loaded")
        s_rpb = sem("rpb_loaded")
        s_raw = [sem(f"w_loaded{i}") for i in range(2)]
        s_hi = sem("w_hi_done")
        s_lo = sem("w_lo_done")
        s_used = sem("w_used")
        s_adaw = [sem(f"ada_loaded{i}") for i in range(2)]
        s_adaT = sem("ada_turned")
        s_asum = sem("ada_row_sums")
        s_rows = sem("ada_rows_summed")
        s_rowc = sem("ada_rows_copied")
        s_rowT = sem("ada_rows_turned")
        s_adaP = sem("ada_first_summed")
        s_adaR = sem("ada_first_rows")
        s_first = [sem(f"ada_first_loaded{q}") for q in range(QUADS)]
        s_mac = sem("ada_products_added")
        s_ada = sem("ada_done")
        s_vT = sem("vectors_turned")
        s_vt = sem("vectors_ready")
        s_cond = sem("cond_ready")
        s_lbe = sem("lb_exp")
        s_xT = sem("x_turned")
        s_x = sem("x_ready")
        s_sq = sem("squares_ready")
        s_sqs = sem("squares_summed")
        s_ms = sem("mean_ready")
        s_rs = sem("root_ready")
        s_mod = sem("mod_ready")
        s_xr = sem("x_scaled")
        s_xh = sem("xh_ready")
        s_xl = sem("xl_ready")
        s_sa = sem("silu_ready")
        s_gm = sem("g_ready")
        s_gh = sem("gh_ready")
        s_gl = sem("gl_ready")
        s_pj = sem("projection_copied")
        s_bias = sem("bias_ready")
        s_ckT = sem("ck_turned")
        s_ckv = sem("ck_ready")
        s_nkT = sem("nk_turned")
        s_nk = sem("nk_ready")
        s_fo = sem("fourier_summed")
        s_foe = sem("fourier_copied")
        s_foh = sem("fourier_hi")
        s_sc = sem("scores_ready")
        s_mx = sem("max_ready")
        s_exp = sem("exp_ready")
        s_pn = sem("probs_ready")
        s_tr = sem("probs_turned")
        s_pt = sem("probsT_ready")
        s_pv = sem("attn_summed")
        s_ath = sem("attn_hi")
        s_at = sem("attn_copied")
        s_dec = sem("decays_ready")
        s_un = sem("unit_ready")
        s_ud = sem("unit_used")
        s_gb = sem("bank_filled")
        s_ge = sem("bank_copied")
        s_osq = sem("o_squared")
        s_ort = sem("o_root")
        s_oy = sem("o_ready")
        s_oh = sem("o_hi")
        s_yo = sem("o_done")
        s_st0 = [sem(f"state_loaded{i}") for i in range(2)]
        s_sf = sem("state_ready")
        s_dv = sem("vector_step")
        s_yT = sem("y_turned")
        s_yo2 = sem("y_copied")
        s_ol = sem("o_lo")
        s_sfo = [sem(f"state_stored{i}") for i in range(4)]
        s_out = sem("stored")
        s_cache_out = sem("new_cache_stored")

        norm_col = [V_NG + (layer * 3 + j) * KT for _, layer, j in STAGES] + [V_NF]

        def prm_tile(s, which):
            _, layer, j = STAGES[s]
            return (layer * NMOD + 3 * j + which) * KT

        PAIRS_FIRST = 2 * QUADS
        n_pairs = [15, 11, 15, 15, 4, 4]
        pair_at = [PAIRS_FIRST + sum(n_pairs[:s]) for s in range(n_stages)]
        n_all = PAIRS_FIRST + sum(n_pairs)
        assert 2 * n_all == DEPTH * NMOD * KT
        norm_pairs = [PAIRS_FIRST + 12 * s for s in range(n_stages)]
        pending = [s > 0 and STAGES[s - 1][0] == "ffn" for s in range(n_stages)]
        rows_before = [sum(n_pairs[r] for r in range(s) if STAGES[r][0] != "ffn") for s in range(n_stages + 1)]
        for s in range(1, n_stages):
            assert norm_pairs[s] <= pair_at[s] - pending[s]
        ffn_no = {s: i for i, s in enumerate([s for s in range(n_stages) if STAGES[s][0] == "ffn"])}
        pj0 = {1: 0, 4: 8}
        gh0 = {s: FT * i for s, i in ffn_no.items()}
        units = [(pair, h2, what) for pair in range(4) for h2 in range(2) for what in range(3)]

        def unit_kinds(u):
            return ["diag"] * (u % 2 == 0) + ["turn", "level0", "level1", "level2", "state"]

        fills = []
        for u in range(4 * 4):
            fills += [(u, kind) for kind in unit_kinds(u) + ["mean"] * (u % 2 == 0 and u > 0)]
        fills.append((16, "mean"))
        fill_no = {fill: g for g, fill in enumerate(fills)}

        hg_steps = [(pair, part) for pair in range(4) for part in range(5)] + [(4, part) for part in range(3)]

        def unit_at(i):
            if i >= len(hg_steps):
                return None
            pair, part = hg_steps[i]
            return 4 * pair if part == 4 else 4 * (pair - 1) + part + 1 if pair and part < 3 else None

        def fill_bank(g):
            return ps[(4, 5, 7)[g % 3]]

        def score_bank(u):
            return ps[(0, 1, 6)[u % 3]]

        def y_stage(tb):
            return w_raw[tb // 2][:, tb % 2 * D:(tb % 2 + 1) * D]

        def blk(ap, lv):
            return ap.rearrange("p (b two w) -> p b two w", two=2, w=1 << lv)

        block = ctx.enter_context(nc.Block())

        @block.sync
        def _(sp):
            xin = xf[:, :, :].rearrange("p k t -> p (k t)").rearrange("p (b d) -> p b d", b=TB)
            flat = ada_b.rearrange("l (r q) -> (l r) q", q=P)
            sp.dma_start(vrow[:, 0, :], flat[0:P, :]).then_inc(s_vrow, 16)
            sp.dma_start(vrow[0:16, 1, :], flat[P:P + 16, :]).then_inc(s_vrow, 16)
            sp.dma_start(vrow[16:64, 1, :], norm_g.rearrange("l j (k q) -> (l j k) q", q=P)).then_inc(s_vrow, 16)
            sp.dma_start(vrow[64:72, 1, :], norm_f.rearrange("(k q) -> k q", q=P)).then_inc(s_vrow, 16)
            sp.dma_start(vrow[72:104, 1, :], hg_lb_logits.rearrange("l e (k q) -> (l e k) q", q=P)).then_inc(s_vrow, 16)
            sp.dma_start(vrow[104:105, 1, :], hg_norm_g).then_inc(s_vrow, 16)
            sp.dma_start(vrow[105:113, 1, :], c_ctx.rearrange("(k q) -> k q", q=P)).then_inc(s_vrow, 16)
            sp.dma_start(vrow[113:121, 1, :], c.rearrange("a (k q) -> (a k) q", q=P)).then_inc(s_vrow, 16)
            sp.dma_start(cst[:, :], consts[:, 0:C_KEEP]).then_inc(s_cst, 16)
            sp.dma_start(xin[:, 0, :], x_prompt[0]).then_inc(s_xin, 16)
            sp.dma_start(xin[:, 1:3, :], x_sample[0].rearrange("(b p) d -> p b d", p=P)).then_inc(s_xin, 16)
            src = ada_w[0].rearrange("(k p) n -> p k n", p=P)
            for q in range(QUADS):
                for a in (0, 4):
                    sp.dma_start(first_ada[q][:, a:a + 4, :],
                                  src[:, a:a + 4, 512 * q:512 * q + 512]).then_inc(s_first[q], 16)

            def load(n, parts):
                if not (isinstance(n, int) and n < 2):
                    sp.wait_ge(s_lo, n - 1)
                for dst, src in parts:
                    sp.dma_start(dst, src).then_inc(s_raw[dst_slot[0]], 16)

            dst_slot = [0]

            def load_w1(n, slot, w, col):
                dst_slot[0] = slot
                raw = w_raw[slot][:, :].rearrange("p (h k n) -> p h k n", h=2, k=KT)
                src = w.rearrange("(k p) n -> p k n", p=P)
                load(n, [(raw[:, h], src[:, :, bass.ds(h * DFF + col, P)]) for h in range(2)])

            def load_w2(n, slot, w, half, col):
                dst_slot[0] = slot
                raw = w_raw[slot][:, 0:HALF * P].rearrange("p (k n) -> p k n", k=HALF)
                src = w.rearrange("(k p) n -> p k n", p=P)
                load(n, [(raw[:, a:b], src[:, half * HALF + a:half * HALF + b, bass.ds(col, P)])
                         for a, b in ((0, 6), (6, HALF))])

            def load_square(n, slot, w, col):
                dst_slot[0] = slot
                raw = w_raw[slot][:, :].rearrange("p (k n) -> p k n", k=KT)
                src = w.rearrange("(k p) n -> p k n", p=P)
                load(n, [(raw[:, a:a + 4], src[:, a:a + 4, bass.ds(col, 256)]) for a in (0, 4)])

            def load_mix0():
                sp.wait_ge(s_used, BASE[1])
                sp.dma_start(ck[:, :], cache_k[0, 0].rearrange("t h d -> t (h d)")).then_inc(s_kv, 16)
                sp.dma_start(cv[:, :], cache_v[0, 0].rearrange("t h d -> t (h d)")).then_inc(s_kv, 16)
                sp.dma_start(dft[:, :], consts[:, C_KEEP:C_END]).then_inc(s_kv, 16)
                for half in range(2):
                    for head in range(HEADS):
                        row = head * RPB_R + ROWS + half
                        src = bass.AP(tensor=na_rpb.tensor, offset=row * RPB_C + WIN_C - 1 - (GRID_W - 1),
                                      ap=[[1, GRID_W], [RPB_C, SLOTS], [1, GRID_W]])
                        sp.dma_start(bias[half * GRID_W:(half + 1) * GRID_W, head, :, :], src).then_inc(s_rpb, 16)

            for s, (kind, layer, j) in enumerate(STAGES):
                n0 = BASE[s]
                if kind == "ffn":
                    w1, w2 = ffn_w1[layer, j // 2], ffn_w2[layer, j // 2]
                    first = 0
                    if s == 0:
                        for slot in range(2):
                            load_w1(slot, slot, w1, slot * P)
                        first = 1
                    with sp.Fori(first, FT // 2) as i:
                        for slot in range(2):
                            load_w1(n0 + 2 * i + slot, slot, w1, (2 * i + slot) * P)
                    with sp.Fori(0, KT) as i:
                        for half in range(2):
                            load_w2(n0 + FT + 2 * i + half, half, w2, half, i * P)
                else:
                    w_in, w_out = (mix0_w_in, mix0_w_out) if kind == "mix0" else (mix1_w_in, mix1_w_out)
                    n_in = N_CHUNKS[kind] - 4
                    if kind == "mix0":
                        cols = [256 * i for i in range(n_in)]
                    else:
                        cols = [part * D + pair * 256 for pair in range(4) for part in range(5)]
                    for i, col in enumerate(cols):
                        load_square(n0 + i, i % 2, w_in[0], col)
                        if kind == "mix0" and i == 3:
                            load_mix0()
                    for i in range(4):
                        load_square(n0 + n_in + i, i % 2, w_out[0], 256 * i)
            for tb in range(TB):
                sp.wait_ge(s_yo2, 2 * (tb + 1))
                dst = y_prompt[0] if tb == 0 else y_sample[0, (tb - 1) * P:tb * P, :]
                sp.dma_start(dst, y_stage(tb)).then_inc(s_out, 16)
            sp.wait_ge(s_out, 16 * TB)
            sp.wait_ge(s_cache_out, 32)
            for slot in s_sfo:
                sp.wait_ge(slot, 16 * 4)

        @block.gpsimd
        def _(pool):
            per_layer = NMOD * KT // 2

            def load_pair(p, layer, s):
                src = ada_w[layer].rearrange("(k p) n -> p k n", p=P)
                col = (p - layer * per_layer) * 256
                for half in range(2):
                    if s is None:
                        pass
                    elif STAGES[s][0] == "ffn":
                        pool.wait_ge(s_mac, 8 * (p - 1 - PAIRS_FIRST - rows_before[s]) + 4 * half + 4)
                    elif half == 0:
                        pool.wait_ge(s_rows, p - pair_at[s] + rows_before[s])
                    pool.dma_start(ada[half][:, :, :],
                                   src[:, half * 4:half * 4 + 4, bass.ds(col, 256)]).then_inc(s_adaw[half], 16)

            def load_pairs(s):
                first, end = pair_at[s] + 1, min(pair_at[s] + n_pairs[s] + 1, n_all)
                for a, b in ((first, min(end, per_layer)), (max(first, per_layer), end)):
                    if a < b:
                        with pool.Fori(a, b) as p:
                            load_pair(p, a // per_layer, s)

            load_pair(PAIRS_FIRST, 0, None)
            load_pairs(0)
            def window(n_sel):
                half = n_sel // 2
                lo_, hi_, base, sign = ((0, GRID_W - WIN_C, WIN_C // 2 - (GRID_W - 1), 1),
                                        (WIN_C, GRID_W, GRID_W - 1 + WIN_C // 2 - 1 - WIN_C, -1))[n_sel % 2]
                b = bias[half * GRID_W:(half + 1) * GRID_W, :, :, lo_:hi_].rearrange("p h r c -> p (h r) c")
                if n_sel % 2:
                    pool.wait_ge(s_bias, n_sel)
                nc.gpsimd.affine_select(out=b, in_=b, compare_op=ALU.is_ge, fill=NEG, base=base,
                                        pattern=[[0, HEADS * SLOTS], [sign, hi_ - lo_]],
                                        channel_multiplier=sign).then_inc(s_bias, 1)

            for i in range(n_pairs[1]):
                load_pair(pair_at[1] + i + 1, 0, 1)
                if i == 3:
                    pool.wait_ge(s_rpb, 16 * 2 * HEADS)
                if i in (3, 4, 5, 6):
                    window(i - 3)
            for s in range(2, n_stages):
                load_pairs(s)

        @block.scalar
        def _(act):
            def split_hi(n, half_n, slot, size):
                act.wait_ge(s_raw[slot], 32 * half_n + 32)
                nc.scalar.activation(w_hi[slot][:, 0:size], w_raw[slot][:, 0:size], ACT.Copy).then_inc(s_hi, 1)

            act.wait_ge(s_vt, 1)
            nc.scalar.activation(cond[:, :, :].rearrange("p k c -> p c k"),
                                 vt[:, V_C:V_END].rearrange("p (c k) -> p c k", c=2), ACT.Silu).then_inc(s_cond, 1)
            for i in range(2):
                split_hi(i, 0, i, chunk_size(i))
            act.wait_ge(s_mod, 1)
            nc.scalar.activation(lb[:, 1:3, :], lb[:, 1:3, :], ACT.Exp).then_inc(s_lbe, 1)

            def norm(m):
                for k in range(KT):
                    if k == KT - 2:
                        nc.scalar.activation(warm[:, 0:1], lb[:, 5, 0:1], ACT.Sqrt)
                    act.wait_ge(s_x, 8 * m + k + 1 if m else KT)
                    nc.scalar.activation(xf[:, k, :], x[:, k, :], ACT.Square).then_inc(s_sq, 1)
                act.wait_ge(s_ms, m + 1)
                nc.scalar.activation(rr[:, :], ps[6][:, 0:T], ACT.Sqrt, bias=lb[:, 5, 0:1]).then_inc(s_rs, 1)
                if m == n_stages:
                    return
                if m:
                    act.wait_ge(s_used, BASE[m])
                    n = BASE[m] + 1
                    split_hi(n, n // 2, n % 2, chunk_size(n))
                for k in range(KT):
                    act.wait_ge(s_xr, 8 * m + k + 1)
                    for cnd, a, b in GROUPS:
                        last = nc.scalar.activation(xh[:, k, a:b], xf[:, k, a:b], ACT.Identity,
                                                    bias=prm[:, prm_tile(m, 0) + k, cnd:cnd + 1])
                    last.then_inc(s_xh, 1)

            def ffn(s):
                n0, g0 = BASE[s], gh0[s]

                def w1_tile(cc, slot, cbase, size):
                    n = n0 + cc
                    act.wait_ge(s_used, n + 1)
                    nc.scalar.activation(silu_a[slot][:, :], ps[2 * slot][:, 0:T], ACT.Silu).then_inc(s_sa, 1)
                    split_hi(n + 2, n0 // 2 + cbase + 1, slot, size)
                    act.wait_ge(s_gm, g0 + cc + 1)
                    nc.scalar.activation(gg[:, bass.ds(cc, 1), 0, :].rearrange("p a t -> p (a t)"),
                                         g_raw[slot][:, :], ACT.Copy).then_inc(s_gh, 1)

                with act.Fori(0, FT // 2 - 1) as i:
                    for slot in range(2):
                        w1_tile(2 * i + slot, slot, i, KT * 256)
                for slot in range(2):
                    w1_tile(FT - 2 + slot, slot, FT // 2 - 1, HALF * P)

                with act.Fori(0, KT - 1) as d:
                    for half in range(2):
                        n = n0 + FT + 2 * d + half
                        act.wait_ge(s_used, n + 1)
                        split_hi(n + 2, (n0 + FT) // 2 + d + 1, half, HALF * P)
                if chunk_size(BASE[s + 1]):
                    act.wait_ge(s_used, BASE[s + 1] - 1)
                    next_hi(BASE[s + 1] - 2)

            def next_hi(n):
                if n + 1 not in BASE:
                    split_hi(n + 2, n // 2 + 1, n % 2, chunk_size(n + 2))

            def mix0(s):
                n0 = BASE[s]
                for i in range(8):
                    n = n0 + i
                    slot = i % 2
                    act.wait_ge(s_used, n + 1)
                    b0, b1 = ps[2 * slot], ps[2 * slot + 1]
                    part, half = i // 2, i % 2
                    if part == 2:
                        nc.scalar.activation(vtok[:, 0:2, half * 256:half * 256 + 256],
                                             b0[:, :].rearrange("p (b n) -> p b n", b=2), ACT.Copy)
                        last = nc.scalar.activation(vtok[:, 2, half * 256:half * 256 + 256], b1[:, 0:256], ACT.Copy)
                    else:
                        dst = (qT, kT, None, fT)[part]
                        scale = HD ** -0.5 if part == 0 else 1.0
                        nc.scalar.activation(dst[:, 2 * half, :], b0[:, 0:T], ACT.Copy, scale=scale)
                        last = nc.scalar.activation(dst[:, 2 * half + 1, :], b1[:, 0:T], ACT.Copy, scale=scale)
                    last.then_inc(s_pj, 1)
                    next_hi(n)
                act.wait_ge(s_pj, pj0[s] + 8)
                act.dma_start(new_v[0, 0].rearrange("t h d -> t (h d)"), vtok[:, 0, :]).then_inc(s_cache_out, 16)
                act.wait_ge(s_nk, 1)
                act.dma_start(new_k[0, 0].rearrange("t h d -> t (h d)"), nk[:, :]).then_inc(s_cache_out, 16)
                for g in range(4):
                    act.wait_ge(s_fo, 6 + g + 1)
                    nc.scalar.activation(gg[:, 4 + g, 0, :], ps[(6 + g) % 4][:, 0:T], ACT.Copy).then_inc(s_foh, 1)

                def attn_hi(pair):
                    act.wait_ge(s_pv, 6 * pair + 6)
                    nc.scalar.activation(gg[:, pair, 0, :], ps[4 + pair % 2][:, 0:T], ACT.Copy).then_inc(s_ath, 1)

                def exps(u):
                    width = NP_ if units[u][2] == 0 else T
                    act.wait_ge(s_mx, u + 1)
                    if u >= 3:
                        act.wait_ge(s_tr, u - 2)
                    nc.scalar.activation(prob[u % 3][:, 0:width], score_bank(u)[:, 0:width], ACT.Exp,
                                         bias=smax[:, u:u + 1], accum_out=ssum[:, u:u + 1]).then_inc(s_exp, 1)

                def copy_probs(u):
                    width = NP_ if units[u][2] == 0 else T
                    act.wait_ge(s_tr, u + 1)
                    if u >= 2:
                        act.wait_ge(s_pv, u - 1)
                    nc.scalar.activation(probT[u % 2][:, 0:width], ps[2 + u % 2][:, 0:width],
                                         ACT.Copy).then_inc(s_pt, 1)

                exps(0)
                exps(1)
                for u in range(24):
                    copy_probs(u)
                    if u + 2 < 24:
                        exps(u + 2)
                    if u % 6 == 1 and u > 6:
                        attn_hi(u // 6 - 1)
                attn_hi(3)
                act.wait_ge(s_cache_out, 32)
                for i in range(3):
                    act.wait_ge(s_used, n0 + 8 + i + 1)
                    next_hi(n0 + 8 + i)

            def mix1(s):
                n0 = BASE[s]

                def copy_chunk(pair, part):
                    n = n0 + 5 * pair + part
                    bank = [ps[2 * (n % 2)], ps[2 * (n % 2) + 1]]
                    b = pair % 2
                    act.wait_ge(s_used, n + 1)
                    if part == 3:
                        nc.scalar.activation(hv[b][:, 0:2, :], bank[0][:, :].rearrange("p (b n) -> p b n", b=2), ACT.Copy)
                        last = nc.scalar.activation(hv[b][:, 2, :], bank[1][:, 0:256], ACT.Copy)
                    else:
                        for h2 in range(2):
                            z = bank[h2][:, 0:T]
                            if part == 0:
                                last = nc.scalar.activation(hq[b][:, h2, :], z, ACT.Copy)
                            elif part == 4:
                                last = nc.scalar.activation(sg[b][:, h2, :], z, ACT.Silu)
                            else:
                                nc.scalar.activation(hp_[b][part - 1][:, h2, :], z, ACT.Sigmoid)
                                last = nc.scalar.activation(hk[b][part - 1][:, h2, :], z, ACT.Sigmoid, scale=-1.0)
                    last.then_inc(s_pj, 1)
                    if part == 0:
                        for d in range(2):
                            act.dma_start(st0[b][:, d, :, :],
                                          state_hgrn[0, 0, d, 2 * pair:2 * pair + 2].rearrange("h k v -> k h v")
                                          ).then_inc(s_st0[b], 16)
                    next_hi(n)

                def after_unit(u):
                    h2, d, head = u // 2 % 2, u % 2, u // 2
                    act.wait_ge(s_sf, u + 1)
                    act.dma_start(new_state[0, 0, d, head], sfin[:, 2 * h2 + d, :]).then_inc(s_sfo[2 * h2 + d], 16)
                    if d == 1:
                        act.wait_ge(s_ud, 2 * head + 2)
                        nc.scalar.activation(osq[:, :], ps[6][:, 0:T], ACT.Square).then_inc(s_osq, 1)

                def root(head):
                    act.wait_ge(s_ge, fill_no[2 * head + 2, "mean"] + 1)
                    nc.scalar.activation(orr[:, :], orr[:, :], ACT.Sqrt).then_inc(s_ort, 1)

                def y_hi(head):
                    act.wait_ge(s_oy, head + 1)
                    nc.scalar.activation(xh[:, head, :], y_all[:, head, :], ACT.Copy).then_inc(s_oh, 1)

                for i, (pair, part) in enumerate(hg_steps):
                    u = unit_at(i)
                    if u and u % 2 == 0:
                        root(u // 2 - 1)
                    if pair < 4:
                        copy_chunk(pair, part)
                    elif part == 0:
                        for head in range(6):
                            y_hi(head)
                    elif part == 2:
                        y_hi(6)
                    if u is not None:
                        after_unit(u)
                root(7)
                y_hi(7)
                for slot in s_sfo:
                    act.wait_ge(slot, 16 * 4)
                for i in range(3):
                    act.wait_ge(s_used, n0 + 20 + i + 1)
                    next_hi(n0 + 20 + i)

            for s, (kind, _, _) in enumerate(STAGES):
                norm(s)
                {"ffn": ffn, "mix0": mix0, "mix1": mix1}[kind](s)
            norm(n_stages)

        @block.vector
        def _(dve):
            steps = [0]

            def link(ins):
                steps[0] += 1
                ins.then_inc(s_dv, 1)
                dve.wait_ge(s_dv, steps[0])

            def split_lo(n, slot, size):
                dve.wait_ge(s_hi, n + 1)
                nc.vector.tensor_tensor(w_lo[slot][:, 0:size], w_raw[slot][:, 0:size],
                                        w_hi[slot][:, 0:size].bitcast(F32), ALU.subtract).then_inc(s_lo, 1)

            def add_bias(p, n, sums):
                nc.vector.tensor_tensor(prm[:, bass.ds(2 * p, 2 * n), :], sums,
                                        vt[:, bass.ds(V_ADAB + 2 * p, 2 * n)].unsqueeze(2).broadcast_to([P, 2 * n, 2]),
                                        ALU.add).then_inc(s_ada, n)

            def ada_half(p, half, s, first=False):
                at = p - PAIRS_FIRST - rows_before[s]
                if half == 0 and not first:
                    dve.wait_ge(s_adaT, at)
                dve.wait_ge(s_adaw[half], 16 * (p - PAIRS_FIRST) + 16)
                for k in range(KT // 2):
                    at_k = 4 * half + k
                    if at_k:
                        dve.wait_ge(s_mac, 8 * at + at_k)
                    for cnd in range(2):
                        scalar = cond[:, at_k, cnd:cnd + 1]
                        if at_k == 0:
                            ins = nc.vector.tensor_scalar(acc[:, cnd, :], ada[half][:, k, :], scalar, None, ALU.mult)
                        else:
                            ins = nc.vector.scalar_tensor_tensor(acc[:, cnd, :], ada[half][:, k, :], scalar,
                                                                 acc[:, cnd, :], ALU.mult, ALU.add)
                    ins.then_inc(s_mac, 1)

            def ada_sum(p, s):
                at = p - PAIRS_FIRST - rows_before[s]
                dve.wait_ge(s_adaT, at + 1)
                nc.vector.reduce_sum(asum[:, :], ps[7][:, :].rearrange("p (a q) -> p a q", a=4), AX).then_inc(s_asum, 1)
                dve.wait_ge(s_asum, at + 1)
                add_bias(p, 1, asum[:, :].rearrange("p (c a) -> p a c", c=2))

            def copy_rows(s, i):
                at = rows_before[s] + i
                dve.wait_ge(s_rows, at + 1)
                if at:
                    dve.wait_ge(s_rowT, at)
                nc.vector.tensor_copy(acc[0:2, 0, :], ps[7][0:2, 0:256]).then_inc(s_rowc, 1)

            def add_rows(s, i):
                dve.wait_ge(s_rowT, rows_before[s] + i + 1)
                add_bias(pair_at[s] + i, 1, ps[6][:, 0:4].rearrange("p (a b) -> p a b", b=2))

            def ada_step(s, i):
                if i < n_pairs[s]:
                    add_rows(s, i)
                if i + 1 < n_pairs[s]:
                    copy_rows(s, i + 1)

            dve.wait_ge(s_vT, 1)
            nc.vector.tensor_copy(vt[:, 0:V_END], ps[6][:, 0:V_END]).then_inc(s_vt, 1)
            dve.wait_ge(s_vt, 1)
            lg = vt[:, V_LB:V_LB + 4 * HG_HEADS].rearrange("p (l e) -> p l e", l=2)
            link(nc.vector.tensor_tensor(lb[:, 0, :], lg[:, 0, :], lg[:, 1, :], ALU.max))
            link(nc.vector.memset(lb[:, 5, 0:1], EPS))
            link(nc.vector.tensor_tensor(lb[:, 1, :], lg[:, 0, :], lb[:, 0, :], ALU.subtract))
            nc.vector.tensor_tensor(lb[:, 2, :], lg[:, 1, :], lb[:, 0, :], ALU.subtract).then_inc(s_mod, 1)
            for k in range(KT):
                dve.wait_ge(s_xT, k + 1)
                nc.vector.tensor_copy(x[:, k, :], ps[k % 4][:, 0:T]).then_inc(s_x, 1)
            for i in range(2):
                split_lo(i, i, chunk_size(i))
            dve.wait_ge(s_lbe, 1)
            link(nc.vector.tensor_tensor(lb[:, 0, :], lb[:, 1, :], lb[:, 2, :], ALU.add))
            link(nc.vector.reciprocal(lb[:, 0, :], lb[:, 0, :]))
            link(nc.vector.tensor_tensor(lb[:, 1, :], lb[:, 1, :], lb[:, 0, :], ALU.mult))
            link(nc.vector.tensor_tensor(lb[:, 2, :], lb[:, 2, :], lb[:, 0, :], ALU.mult))
            link(nc.vector.tensor_tensor(lb[:, 3, :], lb[:, 1, :], lb[:, 2, :], ALU.add))
            link(nc.vector.tensor_tensor(lb[:, 3, :], lb[:, 3, :], lb[:, 1, :], ALU.subtract))
            link(nc.vector.tensor_scalar(lb[:, 4, :], lb[:, 3, :], -1.0, 1.0, ALU.mult, ALU.add))
            for q in range(QUADS):
                dve.wait_ge(s_adaP, q + 1)
                nc.vector.tensor_copy(first_rows[:, 512 * q:512 * q + 512], ps[4 + q][0:2, :]).then_inc(s_adaR, 1)
            dve.wait_ge(s_adaP, QUADS + 1)
            add_bias(0, PAIRS_FIRST, ps[4][:, 0:4 * PAIRS_FIRST].rearrange("p (a b) -> p a b", b=2))

            def sum_squares(m):
                for k in range(1, 6):
                    dve.wait_ge(s_sq, 8 * m + k + 1)
                    ins = nc.vector.tensor_tensor(xf[:, 0, :], xf[:, 0, :], xf[:, k, :], ALU.add)
                    if k < 5:
                        link(ins)
                ins.then_inc(s_sqs, 1)

            def norm(m):
                if m == 0:
                    sum_squares(0)
                mixer = m < n_stages and STAGES[m][0] != "ffn"
                if mixer:
                    ada_sum(pair_at[m] - 1, m - 1)
                if m < n_stages:
                    dve.wait_ge(s_ada, norm_pairs[m])
                    sc = prm_tile(m, 1)
                    ng = vt[:, norm_col[m]:norm_col[m] + KT].unsqueeze(2).broadcast_to([P, KT, 2])
                    nc.vector.scalar_tensor_tensor(mod_a[:, :, :], prm[:, sc:sc + KT, :], 1.0, ng,
                                                   ALU.add, ALU.mult).then_inc(s_mod, 1)
                    dve.wait_ge(s_mod, m + 2)
                dve.wait_ge(s_rs, m + 1)
                link(nc.vector.reciprocal(rr[:, :], rr[:, :]))

                if m == n_stages:
                    for k in range(KT):
                        nc.vector.scalar_tensor_tensor(xf[:, k, :], x[:, k, :], vt[:, V_NF + k:V_NF + k + 1],
                                                       rr[:, :], ALU.mult, ALU.mult).then_inc(s_xr, 1)
                    return
                def scaled(k):
                    for cnd, a, b in GROUPS:
                        last = nc.vector.scalar_tensor_tensor(xf[:, k, a:b], x[:, k, a:b], mod_a[:, k, cnd:cnd + 1],
                                                              rr[:, a:b], ALU.mult, ALU.mult)
                    last.then_inc(s_xr, 1)

                def low(k):
                    dve.wait_ge(s_xh, 8 * m + k + 1)
                    for cnd, a, b in GROUPS:
                        last = nc.vector.scalar_tensor_tensor(xl[:, k, a:b], xf[:, k, a:b],
                                                              prm[:, prm_tile(m, 0) + k, cnd:cnd + 1],
                                                              xh[:, k, a:b].bitcast(F32), ALU.add, ALU.subtract)
                    last.then_inc(s_xl, 1)

                scaled(0)
                scaled(1)
                for k in range(KT):
                    if k + 2 < KT:
                        scaled(k + 2)
                    low(k)
                if m:
                    n = BASE[m] + 1
                    split_lo(n, n % 2, chunk_size(n))

            def gates(s):
                dve.wait_ge(s_ada, norm_pairs[s] + 4)
                g = prm_tile(s, 2)
                link(nc.vector.tensor_scalar(hgate[:, :, :], prm[:, g:g + KT, :],
                                             0.5 if STAGES[s][0] == "ffn" else 1.0, None, ALU.mult))

            def residual(k, bank):
                for cnd, a, b in GROUPS:
                    last = nc.vector.scalar_tensor_tensor(
                        x[:, bass.ds(k, 1), a:b].rearrange("p a t -> p (a t)"), bank[:, a:b],
                        hgate[:, bass.ds(k, 1), cnd], x[:, bass.ds(k, 1), a:b].rearrange("p a t -> p (a t)"),
                        ALU.mult, ALU.add)
                last.then_inc(s_x, 1)

            def ffn(s):
                n0, g0 = BASE[s], gh0[s]
                pa = pair_at[s]
                n_w1 = min(n_pairs[s], FT // 2)

                def w1_tile(cc, slot, size, p, last=0):
                    n = n0 + cc
                    split_lo(n + 2, slot, size)
                    dve.wait_ge(s_sa, g0 + cc + 1)
                    nc.vector.tensor_tensor(g_raw[slot][:, :], silu_a[slot][:, :], ps[2 * slot + 1][:, 0:T],
                                            ALU.mult).then_inc(s_gm, 1)
                    def ada_part():
                        if p is not None:
                            if slot == 0 and last is not None:
                                ada_sum(p - 1, last)
                            ada_half(p, slot, s, isinstance(p, int) and p == PAIRS_FIRST)

                    if size == KT * 256:
                        ada_part()
                    dve.wait_ge(s_gh, g0 + cc + 1)
                    nc.vector.tensor_tensor(gg[:, bass.ds(cc, 1), 1, :].rearrange("p a t -> p (a t)"),
                                            g_raw[slot][:, :],
                                            gg[:, bass.ds(cc, 1), 0, :].rearrange("p a t -> p (a t)").bitcast(F32),
                                            ALU.subtract).then_inc(s_gl, 1)
                    if size != KT * 256:
                        ada_part()

                for slot in range(2):
                    w1_tile(slot, slot, KT * 256, pa, s - 1 if pending[s] else None)
                with dve.Fori(1, min(n_w1, FT // 2 - 1)) as i:
                    for slot in range(2):
                        w1_tile(2 * i + slot, slot, KT * 256, pa + i, s)
                if n_w1 < FT // 2 - 1:
                    ada_sum(n_all - 1, s)
                    with dve.Fori(n_w1, FT // 2 - 1) as i:
                        for slot in range(2):
                            w1_tile(2 * i + slot, slot, KT * 256, None)
                for slot in range(2):
                    w1_tile(FT - 2 + slot, slot, HALF * P, pa + n_w1 - 1 if n_w1 == FT // 2 else None, s)
                gates(s)

                def w2_tile(d, e, size, p, last=False):
                    n = n0 + FT + 2 * d

                    def ada_part():
                        if p is not None:
                            if e == 0:
                                ada_sum(p - 1, s)
                            ada_half(p, e, s)

                    if size:
                        split_lo(n + 2, 0, size)
                    if last:
                        ada_part()
                        sum_squares(s + 1)
                    else:
                        split_lo(n + 3, 1, size)
                    dve.wait_ge(s_used, n + 2)
                    residual(d, ps[4 + e])
                    if not last:
                        ada_part()

                looped = n_pairs[s] > n_w1
                with dve.Fori(0, KT // 2 - 1) as i:
                    for e in range(2):
                        w2_tile(2 * i + e, e, HALF * P, pa + n_w1 + i if looped else None)
                for e in range(2):
                    w2_tile(KT - 2 + e, e, chunk_size(BASE[s + 1]) if e else HALF * P,
                            pa + n_w1 + KT // 2 - 1 if looped else None, e == 1)

            def next_lo(n):
                if n + 1 not in BASE:
                    split_lo(n + 2, n % 2, chunk_size(n + 2))

            def out_projection(s, n, pair):
                gates(s)
                for i in range(4):
                    next_lo(n + i)
                    if i == 3:
                        sum_squares(s + 1)
                    dve.wait_ge(s_used, n + i + 1)
                    for e in range(2):
                        residual(2 * i + e, ps[2 * (i % 2) + e])
                    ada_step(s, pair + i)

            def mix0(s):
                n0 = BASE[s]
                copy_rows(s, 0)
                for i in range(8):
                    next_lo(n0 + i)
                    ada_step(s, i)
                dve.wait_ge(s_ckT, 1)
                nc.vector.tensor_copy(ckT[:, :, :].rearrange("p a t -> p (a t)"), ps[6][:, :]).then_inc(s_ckv, 1)
                dve.wait_ge(s_nkT, 1)
                nc.vector.tensor_copy(nk[:, :], ps[6][:, :]).then_inc(s_nk, 1)
                for f in range(6):
                    dve.wait_ge(s_fo, f + 1)
                    tb, gp = f // 2, f % 2
                    nc.vector.tensor_copy(ab[:, tb, 2 * gp:2 * gp + 2, :],
                                          ps[f % 4][:, :].rearrange("p (g c) -> p g c", g=2)).then_inc(s_foe, 1)
                for g in range(4):
                    dve.wait_ge(s_foh, g + 1)
                    nc.vector.tensor_tensor(gg[:, 4 + g, 1, :], ps[(6 + g) % 4][:, 0:T],
                                            gg[:, 4 + g, 0, :].bitcast(F32), ALU.subtract).then_inc(s_foe, 1)

                def maxes(u):
                    width = NP_ if units[u][2] == 0 else T
                    dve.wait_ge(s_sc, u + 1)
                    link(nc.vector.reduce_max(smax[:, u:u + 1], score_bank(u)[:, 0:width], AX))
                    nc.vector.tensor_scalar(smax[:, u:u + 1], smax[:, u:u + 1], -1.0, None, ALU.mult).then_inc(s_mx, 1)

                def attn_lo(pair):
                    dve.wait_ge(s_ath, pair + 1)
                    nc.vector.tensor_tensor(gg[:, pair, 1, :], ps[4 + pair % 2][:, 0:T],
                                            gg[:, pair, 0, :].bitcast(F32), ALU.subtract).then_inc(s_at, 1)

                maxes(0)
                maxes(1)
                for u in range(24):
                    width = NP_ if units[u][2] == 0 else T
                    dve.wait_ge(s_exp, u + 1)
                    link(nc.vector.reciprocal(srec[:, u:u + 1], ssum[:, u:u + 1]))
                    nc.vector.tensor_scalar(prob[u % 3][:, 0:width], prob[u % 3][:, 0:width],
                                            srec[:, u:u + 1], None, ALU.mult).then_inc(s_pn, 1)
                    if u + 2 < 24:
                        maxes(u + 2)
                    if u % 6 == 2 and u > 6:
                        attn_lo(u // 6 - 1)
                attn_lo(3)
                out_projection(s, n0 + 8, 8)

            def mix1(s):
                n0 = BASE[s]

                def level(u, lv):
                    pair, h2, d = u // 4, u // 2 % 2, u % 2
                    if lv == 0 and u >= 2:
                        dve.wait_ge(s_ud, u - 1)
                    tq, ks, b = 1 - d, d, pair % 2
                    q, pr, k, r, m = (blk(a, lv) for a in (hq[b][:, h2, :], hp_[b][d][:, h2, :], hk[b][d][:, h2, :],
                                                           hr[u % 2][:, :], hm[u % 2][:, lv, :]))
                    w = 1 << lv
                    end = w - 1 if d == 0 else 0
                    nc.vector.tensor_tensor(m[:, :, tq, :], q[:, :, tq, :], pr[:, :, tq, :], ALU.mult)
                    whole = [P, T // (2 * w), w]
                    if lv == 0:
                        nc.vector.tensor_copy(m[:, :, ks, :], k[:, :, ks, :])
                        nc.vector.memset(r[:, :, tq, :], 1.0)
                        link(nc.vector.tensor_copy(r[:, :, ks, :], pr[:, :, tq, :]))
                    else:
                        nc.vector.tensor_tensor(m[:, :, ks, :], k[:, :, ks, :], r[:, :, ks, :], ALU.mult)
                        link(nc.vector.tensor_tensor(r[:, :, ks, :], r[:, :, ks, :],
                                                     pr[:, :, tq, end:end + 1].broadcast_to(whole), ALU.mult))
                    link(nc.vector.tensor_tensor(pr[:, :, tq, :], pr[:, :, tq, :],
                                                 pr[:, :, ks, end:end + 1].broadcast_to(whole), ALU.mult))
                    if lv == LEVELS - 1:
                        nc.vector.tensor_tensor(qi[u % 2], hq[b][:, h2, :], hp_[b][d][:, h2, :], ALU.mult)
                        nc.vector.tensor_tensor(ki[u % 2], hk[b][d][:, h2, :], hr[u % 2][:, :],
                                                ALU.mult).then_inc(s_un, 1)

                def evac(u, kind):
                    pair, h2, d = u // 4, u // 2 % 2, u % 2
                    g = fill_no[u, kind]
                    bank = fill_bank(g)
                    dve.wait_ge(s_gb, g + 1)
                    if kind == "diag":
                        nc.vector.tensor_tensor(gd[:, :].rearrange("p (c t) -> p c t", c=3),
                                                bank[:, 0:T].rearrange("p (c t) -> p c t", c=3),
                                                ident.unsqueeze(1).broadcast_to([P, 3, P]), ALU.mult).then_inc(s_ge, 1)
                    elif kind[:5] == "level":
                        mask = cst[:, C_MASK + d * LEVELS * 64:C_MASK + (d + 1) * LEVELS * 64]
                        nc.vector.tensor_tensor(gm[int(kind[5])][:, :], bank[:, 0:LEVELS * 64], mask, ALU.mult).then_inc(s_ge, 1)
                    elif kind == "turn":
                        nc.vector.tensor_copy(ktok[:, :, :], bank[:, 0:256].rearrange("p (a k) -> p a k", a=2)).then_inc(s_ge, 1)
                    elif kind == "state":
                        first = 1 if d == 0 else 2
                        col = first * P + (P - 1 if d == 0 else 0)
                        if pair:
                            dve.wait_ge(s_sfo[2 * h2 + d], 16 * pair)
                        nc.vector.tensor_copy(sfin[:, 2 * h2 + d, :], bank[:, 0:P]).then_inc(s_sf, 1)
                        dve.wait_ge(s_st0[pair % 2], 32 * (pair // 2 + 1))
                        nc.vector.scalar_tensor_tensor(st1[:, :], st0[pair % 2][:, d, h2, :],
                                                       hp_[pair % 2][d][:, h2, col:col + 1],
                                                       bank[:, P:2 * P], ALU.mult, ALU.add).then_inc(s_ge, 1)
                    else:
                        nc.vector.tensor_scalar(orr[:, :], bank[:, 0:T], EPS, None, ALU.add).then_inc(s_ge, 1)

                def finish(head):
                    evac(2 * head + 2, "mean")
                    nc.vector.scalar_tensor_tensor(y_all[:, head, :], ps[6][:, 0:T], vt[:, V_HG:V_HG + 1],
                                                   sg[head // 2 % 2][:, head % 2, :], ALU.mult, ALU.mult).then_inc(s_yo, 1)

                def scale_y(head):
                    y = y_all[:, head, :]
                    dve.wait_ge(s_yo, head + 1)
                    dve.wait_ge(s_ort, head + 1)
                    link(nc.vector.reciprocal(orr[:, :], orr[:, :]))
                    nc.vector.tensor_tensor(y, y, orr[:, :], ALU.mult).then_inc(s_oy, 1)

                def y_lo(head):
                    dve.wait_ge(s_oh, head + 1)
                    nc.vector.tensor_tensor(xl[:, head, :], y_all[:, head, :], xh[:, head, :].bitcast(F32),
                                            ALU.subtract).then_inc(s_ol, 1)

                def decays(pair, d):
                    dve.wait_ge(s_pj, pj0[s] + 5 * pair + d + 2)
                    for h2 in range(2):
                        cc = d * HG_HEADS + 2 * pair + h2
                        f, k = hp_[pair % 2][d][:, h2, :], hk[pair % 2][d][:, h2, :]
                        nc.vector.tensor_scalar(f, f, lb[:, 4, cc:cc + 1], lb[:, 3, cc:cc + 1], ALU.mult, ALU.add)
                        last = nc.vector.tensor_scalar(k, k, lb[:, 4, cc:cc + 1], None, ALU.mult)
                    last.then_inc(s_dec, 1)
                    dve.wait_ge(s_dec, 2 * pair + d + 1)

                copy_rows(s, 0)
                for i, (pair, part) in enumerate(hg_steps):
                    u, nxt = unit_at(i), unit_at(i + 2) if part == 2 else None if part == 3 else unit_at(i + 1)
                    if u is not None:
                        for kind in unit_kinds(u):
                            evac(u, kind)
                    if 0 < i < 20:
                        next_lo(n0 + i - 1)
                    if u and u % 2 == 0:
                        finish(u // 2 - 1)
                    if pair < 4 and part in (2, 3):
                        decays(pair, part - 2)
                    if nxt is not None:
                        for lv in range(LEVELS):
                            level(nxt, lv)
                    if u and u % 2 == 0:
                        scale_y(u // 2 - 1)
                    if i == 19:
                        next_lo(n0 + i)
                    elif i == 20:
                        for head in range(6):
                            y_lo(head)
                    elif i == 22:
                        y_lo(6)
                    if pair == 0:
                        ada_step(s, part)
                finish(7)
                scale_y(7)
                y_lo(7)
                out_projection(s, n0 + 20, n_pairs[s])

            for s, (kind, _, _) in enumerate(STAGES):
                norm(s)
                {"ffn": ffn, "mix0": mix0, "mix1": mix1}[kind](s)
            norm(n_stages)
            for f in range(2 * TB):
                tb, half = f // 2, f % 2
                dve.wait_ge(s_yT, f + 1)
                nc.vector.tensor_copy(y_stage(tb)[:, half * 512:half * 512 + 512], ps[f % 2][:, :]).then_inc(s_yo2, 1)

        @block.tensor
        def _(pe):
            def mm3(out, a, b, first, last):
                (ah, al), (bh, bl) = a, b
                nc.tensor.matmul(out, ah, bh, start=first, stop=False)
                nc.tensor.matmul(out, ah, bl, start=False, stop=False)
                return nc.tensor.matmul(out, al, bh, start=False, stop=last)

            def hidden(k, a=0, b=T):
                return gg[:, k, 0, a:b], gg[:, k, 1, a:b]

            def normed(k, a=0, b=T):
                return xh[:, k, a:b], xl[:, k, a:b]

            def wtile(slot, k, width, a, b):
                return (w_hi[slot][:, k * width + a:k * width + b], w_lo[slot][:, k * width + a:k * width + b])

            def ada_turn(p, s):
                pe.wait_ge(s_mac, 8 * (p - PAIRS_FIRST - rows_before[s]) + 8)
                pe.wait_ge(s_ada, p)
                for e in range(4):
                    last = nc.tensor.transpose(ps[7][:, e * P:(e + 1) * P],
                                               acc[:, e // 2, e % 2 * P:(e % 2 + 1) * P], ident)
                last.then_inc(s_adaT, 1)

            def ada_rows(s, i):
                if i == 0:
                    pe.wait_ge(s_ada, pair_at[s])
                for k in range(KT):
                    if k % 4 == 0:
                        pe.wait_ge(s_adaw[k // 4], 16 * (pair_at[s] + i - PAIRS_FIRST) + 16)
                    last = nc.tensor.matmul(ps[7][0:2, 0:256], cond[:, k, :], ada[k // 4][:, k % 4, :],
                                            start=(k == 0), stop=(k == KT - 1))
                last.then_inc(s_rows, 1)

            def ada_step(s, i):
                if i < n_pairs[s]:
                    pe.wait_ge(s_rowc, rows_before[s] + i + 1)
                    pe.wait_ge(s_ada, pair_at[s] + i)
                    for e in range(2):
                        last = nc.tensor.transpose(ps[6][:, 2 * e:2 * e + 2], acc[0:2, 0, e * P:(e + 1) * P],
                                                   cst[0:2, C_ID:C_ID + 2])
                    last.then_inc(s_rowT, 1)
                if i + 1 < n_pairs[s]:
                    ada_rows(s, i + 1)

            pe.wait_ge(s_cst, 16)
            pe.wait_ge(s_vrow, 16 * 8)
            nc.tensor.transpose(ps[6][:, 0:P], vrow[:, 0, :], ident)
            nc.tensor.transpose(ps[6][:, P:V_END], vrow[0:V_END - P, 1, :],
                                cst[0:V_END - P, C_ID:C_ID + V_END - P]).then_inc(s_vT, 1)
            pe.wait_ge(s_xin, 32)
            xin = xf[:, :, :].rearrange("p k t -> p (k t)").rearrange("p (b d) -> p b d", b=TB)
            for k in range(KT):
                if k >= 4:
                    pe.wait_ge(s_x, k - 3)
                for tb in range(TB):
                    last = nc.tensor.transpose(ps[k % 4][:, tb * P:(tb + 1) * P], xin[:, tb, k * P:(k + 1) * P], ident)
                last.then_inc(s_xT, 1)
            pe.wait_ge(s_cond, 1)
            for q in range(QUADS):
                pe.wait_ge(s_first[q], 32)
                for k in range(KT):
                    last = nc.tensor.matmul(ps[4 + q][0:2, :], cond[:, k, :], first_ada[q][:, k, :],
                                            start=(k == 0), stop=(k == KT - 1))
                last.then_inc(s_adaP, 1)
            pe.wait_ge(s_adaR, QUADS)
            for e in range(2 * PAIRS_FIRST):
                last = nc.tensor.transpose(ps[4][:, 2 * e:2 * e + 2], first_rows[:, e * P:(e + 1) * P],
                                           cst[0:2, C_ID:C_ID + 2])
            last.then_inc(s_adaP, 1)

            def norm(m):
                if 0 < m < n_stages and not pending[m]:
                    pe.wait_ge(s_ada, pair_at[m])
                pe.wait_ge(s_sqs, m + 1)
                for k in (0, 6, 7):
                    if k:
                        pe.wait_ge(s_sq, 8 * m + k + 1)
                    last = nc.tensor.matmul(ps[6][:, 0:T], cst[:, C_MEAN:C_MEAN + P], xf[:, k, :],
                                            start=(k == 0), stop=(k == KT - 1))
                last.then_inc(s_ms, 1)
                if m < n_stages and STAGES[m][0] != "ffn":
                    ada_turn(pair_at[m] - 1, m - 1)
                    ada_rows(m, 0)

            def first_products(m, outs, ws):
                for k in range(KT):
                    pe.wait_ge(s_xh, 8 * m + k + 1)
                    for e, out in enumerate(outs):
                        for w in ws[2 * k + e]:
                            nc.tensor.matmul(out, w, xh[:, k, :], start=(k == 0 and w is ws[e][0]), stop=False)
                for k in range(KT):
                    pe.wait_ge(s_xl, 8 * m + k + 1)
                    for e, out in enumerate(outs):
                        last = nc.tensor.matmul(out, ws[2 * k + e][0], xl[:, k, :], start=False, stop=(k == KT - 1))
                return last

            def features(m, n, slot, first):
                pe.wait_ge(s_lo, n + 1)
                outs = [ps[2 * slot + e][:, 0:T] for e in range(2)]
                ws = [wtile(slot, k, 256, e * P, (e + 1) * P) for k in range(KT) for e in range(2)]
                if first:
                    last = first_products(m, outs, ws)
                else:
                    for k in range(KT):
                        for e in range(2):
                            last = mm3(outs[e], ws[2 * k + e], normed(k), k == 0, k == KT - 1)
                last.then_inc(s_used, 1)

            def tokens(n, slot):
                pe.wait_ge(s_lo, n + 1)
                for tb in range(TB):
                    out = ps[2 * slot + tb // 2][:, tb % 2 * 256:tb % 2 * 256 + 256]
                    for k in range(KT):
                        last = mm3(out, normed(k, tb * P, (tb + 1) * P), wtile(slot, k, 256, 0, 256),
                                   k == 0, k == KT - 1)
                last.then_inc(s_used, 1)

            def out_products(i, parts, k0, k1):
                slot = i % 2
                for k in range(k0, k1):
                    for e in range(2):
                        last = mm3(ps[2 * slot + e][:, 0:T], wtile(slot, k, 256, e * P, (e + 1) * P), parts(k),
                                   k == 0, k == KT - 1)
                if k1 == KT:
                    last.then_inc(s_used, 1)

            def out_projection(s, n, parts, pair, ahead=0):
                for i in range(4):
                    pe.wait_ge(s_lo, n + i + 1)
                    if i >= 2:
                        pe.wait_ge(s_x, 8 * (s + 1) + 2 * (i - 1))
                    out_products(i, parts, ahead if i < 2 else 0, KT)
                    ada_step(s, pair + i)

            def ffn(s):
                n0, g0 = BASE[s], gh0[s]
                pa = pair_at[s]
                n_w1 = min(n_pairs[s], FT // 2)

                def w1_tile(cc, slot, first, guard, turn=None):
                    if guard:
                        pe.wait_ge(s_gm, g0 + cc - 1)
                    pe.wait_ge(s_lo, n0 + cc + 1)
                    outs = [ps[2 * slot + e][:, 0:T] for e in range(2)]
                    ws = [[(w[slot][:, (e * KT + k) * P:(e * KT + k + 1) * P]) for w in (w_hi, w_lo)]
                          for k in range(KT) for e in range(2)]
                    if first:
                        last = first_products(s, outs, ws)
                    else:
                        for k in range(KT):
                            if turn and k == 2:
                                ada_turn(*turn)
                            for e in range(2):
                                last = mm3(outs[e], ws[2 * k + e], normed(k), k == 0, k == KT - 1)
                    last.then_inc(s_used, 1)

                w1_tile(0, 0, True, False)
                w1_tile(1, 1, False, False, (pa - 1, s - 1) if pending[s] else None)
                with pe.Fori(1, n_w1) as i:
                    w1_tile(2 * i, 0, False, True)
                    w1_tile(2 * i + 1, 1, False, True, (pa + i - 1, s))
                if n_w1 < FT // 2:
                    w1_tile(2 * n_w1, 0, False, True)
                    w1_tile(2 * n_w1 + 1, 1, False, True, (n_all - 1, s))
                    with pe.Fori(n_w1 + 1, FT // 2) as i:
                        for slot in range(2):
                            w1_tile(2 * i + slot, slot, False, True)

                def w2_tile(d, bank, guard, turn=None):
                    if guard:
                        pe.wait_ge(s_x, 8 * (s + 1) + d - 1)
                    for half in range(2):
                        pe.wait_ge(s_lo, n0 + FT + 2 * d + half + 1)
                        pe.wait_ge(s_gl, g0 + HALF * (half + 1))
                        for kk in range(HALF):
                            if turn and half == 0 and kk == 4:
                                ada_turn(*turn)
                            last = mm3(bank[:, 0:T], wtile(half, kk, P, 0, P), hidden(half * HALF + kk),
                                       half == 0 and kk == 0, half == 1 and kk == HALF - 1)
                        last.then_inc(s_used, 1)

                looped = n_pairs[s] > n_w1
                w2_tile(0, ps[4], False)
                w2_tile(1, ps[5], False, (pa + n_w1 - 1, s) if looped else None)
                with pe.Fori(1, KT // 2) as i:
                    w2_tile(2 * i, ps[4], True)
                    w2_tile(2 * i + 1, ps[5], True, (pa + n_w1 + i - 1, s) if looped else None)

            def mix0(s):
                n0 = BASE[s]
                for i in range(8):
                    slot = i % 2
                    if i >= 2:
                        pe.wait_ge(s_pj, pj0[s] + i - 1)
                    if i // 2 == 2:
                        tokens(n0 + i, slot)
                    else:
                        features(s, n0 + i, slot, i == 0)
                    ada_step(s, i)
                pe.wait_ge(s_kv, 48)
                pe.wait_ge(s_ada, pair_at[s] + 8)
                for e in range(4):
                    last = nc.tensor.transpose(ps[6][:, e * P:(e + 1) * P], ck[:, e * P:(e + 1) * P], ident)
                last.then_inc(s_ckT, 1)
                pe.wait_ge(s_pj, pj0[s] + 8)
                pe.wait_ge(s_ckv, 1)
                for e in range(4):
                    last = nc.tensor.transpose(ps[6][:, e * P:(e + 1) * P], kT[:, e, 0:P], ident)
                last.then_inc(s_nkT, 1)
                for f in range(6):
                    tb, gp = f // 2, f % 2
                    if f >= 4:
                        pe.wait_ge(s_foe, f - 3)
                    for e in range(2):
                        g = 2 * gp + e
                        last = nc.tensor.matmul(ps[f % 4][:, e * 256:e * 256 + 256], fT[:, g, tb * P:(tb + 1) * P],
                                                dft[:, 0:2 * P], start=True, stop=True)
                    last.then_inc(s_fo, 1)
                pe.wait_ge(s_foe, 6)
                for g in range(4):
                    if g >= 2:
                        pe.wait_ge(s_foe, 6 + g - 1)
                    bank = ps[(6 + g) % 4]
                    for e in range(2):
                        nc.tensor.matmul(bank[:, 0:P], ab[:, 0, g, e * P:(e + 1) * P],
                                         dft[:, C_DT128 - C_KEEP + e * P:C_DT128 - C_KEEP + (e + 1) * P],
                                         start=(e == 0), stop=(e == 1))
                    for tt in range(2):
                        for e in range(2):
                            at_ = C_DT256 - C_KEEP + (2 * tt + e) * NS_
                            last = nc.tensor.matmul(bank[:, NP_:T], ab[:, 1 + tt, g, e * P:(e + 1) * P],
                                                    dft[:, at_:at_ + NS_], start=(tt == 0 and e == 0),
                                                    stop=(tt == 1 and e == 1))
                    last.then_inc(s_fo, 1)
                pe.wait_ge(s_foe, 10)
                pe.wait_ge(s_bias, 4)

                def scores(u):
                    pair, h2, what = units[u]
                    rows = slice(HD * h2, HD * h2 + HD)
                    bank = score_bank(u)
                    if u >= 3:
                        pe.wait_ge(s_exp, u - 2)
                    if what == 0:
                        nc.tensor.matmul(bank[:, 0:P], qT[rows, pair, 0:P], kT[rows, pair, 0:P],
                                         start=True, stop=True).then_inc(s_sc, 1)
                        return
                    b = what - 1
                    q = qT[rows, pair, NP_ + b * P:NP_ + (b + 1) * P]
                    nc.tensor.matmul(bank[:, 0:NS_], q, kT[rows, pair, NP_:T], start=True, stop=False)
                    tab = bias[:, 2 * pair + h2, 2 - 2 * b:6 - 2 * b, :].rearrange("p r c -> p (r c)")
                    nc.tensor.matmul(bank[:, 0:NS_], anti, tab, start=False, stop=True)
                    nc.tensor.matmul(bank[:, NS_:T], q, ckT[rows, pair, :], start=True, stop=True).then_inc(s_sc, 1)

                def turn(u):
                    n = 1 if units[u][2] == 0 else 3
                    pe.wait_ge(s_pn, u + 1)
                    if u >= 2:
                        pe.wait_ge(s_pt, u - 1)
                    for e in range(n):
                        last = nc.tensor.transpose(ps[2 + u % 2][:, e * P:(e + 1) * P], prob[u % 3][:, e * P:(e + 1) * P], ident)
                    last.then_inc(s_tr, 1)

                def values(u):
                    pair, h2, what = units[u]
                    head = 2 * pair + h2
                    cols = slice(head * HD, head * HD + HD)
                    if u % 6 == 0 and pair >= 2:
                        pe.wait_ge(s_at, pair - 1)
                    pe.wait_ge(s_pt, u + 1)
                    out = ps[4 + pair % 2][HD * h2:HD * h2 + HD, what * P:(what + 1) * P]
                    vals = [vtok[:, 0, cols]] if what == 0 else [vtok[:, 1, cols], vtok[:, 2, cols], cv[:, cols]]
                    for e, v in enumerate(vals):
                        last = nc.tensor.matmul(out, v, probT[u % 2][:, e * P:(e + 1) * P],
                                                start=(e == 0), stop=(e == len(vals) - 1))
                    last.then_inc(s_pv, 1)

                for u in range(3):
                    scores(u)
                for u in range(24):
                    turn(u)
                    if u + 3 < 24:
                        scores(u + 3)
                    if u:
                        values(u - 1)
                values(23)
                pe.wait_ge(s_at, 4)
                out_projection(s, n0 + 8, hidden, 8)

            def mix1(s):
                n0 = BASE[s]

                def next_bank(u, kind):
                    g = fill_no[u, kind]
                    if g >= 3:
                        pe.wait_ge(s_ge, g - 2)
                    return fill_bank(g)

                def mean(head):
                    bank = next_bank(2 * head + 2, "mean")
                    pe.wait_ge(s_osq, head + 1)
                    nc.tensor.matmul(bank[:, 0:T], cst[:, C_MEANH:C_MEANH + P], osq[:, :],
                                     start=True, stop=True).then_inc(s_gb, 1)

                def unit_first(u):
                    h2, d, b = u // 2 % 2, u % 2, u // 4 % 2
                    vcols = slice(h2 * P, (h2 + 1) * P)
                    m = hm[u % 2]
                    pe.wait_ge(s_un, u + 1)
                    if d == 0:
                        bank = next_bank(u, "diag")
                        pe.wait_ge(s_dec, 2 * (u // 4) + 2)
                        for cc in range(3):
                            for e in range(2):
                                last = nc.tensor.matmul(bank[:, cc * P:(cc + 1) * P], hk[b][e][:, h2, cc * P:(cc + 1) * P],
                                                        hq[b][:, h2, cc * P:(cc + 1) * P], start=(e == 0), stop=(e == 1))
                        last.then_inc(s_gb, 1)
                    first = 1 if d == 0 else 2
                    bank = next_bank(u, "turn")
                    nc.tensor.transpose(bank[:, 0:P], ki[u % 2][:, 0:P], ident)
                    nc.tensor.transpose(bank[:, P:2 * P], ki[u % 2][:, first * P:(first + 1) * P], ident).then_inc(s_gb, 1)
                    for cc in range(3):
                        bank = next_bank(u, f"level{cc}")
                        for lv in range(LEVELS):
                            rhs = blk(m[:, lv, cc * P:(cc + 1) * P], lv)[:, :, 1 - d, :]
                            last = nc.tensor.matmul(bank[:, lv * 64:(lv + 1) * 64], m[:, lv, cc * P:(cc + 1) * P],
                                                    rhs, start=True, stop=True)
                        last.then_inc(s_gb, 1)
                    bank = next_bank(u, "state")
                    pe.wait_ge(s_ge, fill_no[u, "turn"] + 1)
                    if u % 4 == 0:
                        pe.wait_ge(s_pj, pj0[s] + 5 * (u // 4) + 4)
                    nc.tensor.matmul(bank[:, 0:P], ktok[:, 0, :], hv[b][:, 0, vcols], start=True, stop=True)
                    nc.tensor.matmul(bank[:, P:2 * P], ktok[:, 1, :], hv[b][:, first, vcols],
                                     start=True, stop=True).then_inc(s_gb, 1)

                def unit_second(u):
                    pair, h2, d, b = u // 4, u // 2 % 2, u % 2, u // 4 % 2
                    head = 2 * pair + h2
                    o = ps[6]
                    vcols = slice(h2 * P, (h2 + 1) * P)
                    first = 1 if d == 0 else 2
                    second = 3 - first
                    if d == 0:
                        if head:
                            pe.wait_ge(s_yo, head)
                        for cc in range(3):
                            nc.tensor.matmul(o[:, cc * P:(cc + 1) * P], hv[b][:, cc, vcols], gd[:, cc * P:(cc + 1) * P],
                                             start=(cc == 0), stop=False, skip_group_check=True)
                    for cc in range(3):
                        pe.wait_ge(s_ge, fill_no[u, f"level{cc}"] + 1)
                        for lv in range(LEVELS):
                            out = blk(o[:, cc * P:(cc + 1) * P], lv)[:, :, 1 - d, :]
                            masked = gm[cc][:, lv * 64:(lv + 1) * 64].rearrange("p (b w) -> p b w", w=1 << lv)
                            nc.tensor.matmul(out, hv[b][:, cc, vcols], masked,
                                             start=False, stop=False, skip_group_check=True)
                    pe.wait_ge(s_st0[b], 32 * (pair // 2 + 1))
                    nc.tensor.matmul(o[:, first * P:(first + 1) * P], st0[b][:, d, h2, :],
                                     qi[u % 2][:, first * P:(first + 1) * P], start=False, stop=False, skip_group_check=True)
                    pe.wait_ge(s_ge, fill_no[u, "state"] + 1)
                    nc.tensor.matmul(o[:, second * P:(second + 1) * P], st1[:, :],
                                     qi[u % 2][:, second * P:(second + 1) * P], start=False, stop=True,
                                     skip_group_check=True).then_inc(s_ud, 1)

                for i, (pair, part) in enumerate(hg_steps):
                    u = unit_at(i)
                    if u is not None:
                        if u == 0:
                            pe.wait_ge(s_ada, pair_at[s] + n_pairs[s])
                        unit_first(u)
                        if u and u % 2 == 0:
                            mean(u // 2 - 1)
                    if pair < 4:
                        if i >= 2:
                            pe.wait_ge(s_pj, pj0[s] + i - 1)
                        if part == 3:
                            tokens(n0 + i, i % 2)
                        else:
                            features(s, n0 + i, i % 2, i == 0)
                    elif part:
                        if part == 1:
                            pe.wait_ge(s_pj, pj0[s] + 20)
                            pe.wait_ge(s_ol, 6)
                        pe.wait_ge(s_lo, n0 + 20 + part)
                        out_products(part - 1, normed, 0, 6)
                    if u is not None:
                        unit_second(u)
                    if pair == 0:
                        ada_step(s, part)
                pe.wait_ge(s_ol, 7)
                for i in range(2):
                    out_products(i, normed, 6, 7)
                mean(7)
                pe.wait_ge(s_ol, HG_HEADS)
                out_projection(s, n0 + 20, normed, n_pairs[s], 7)

            for s, (kind, _, _) in enumerate(STAGES):
                norm(s)
                {"ffn": ffn, "mix0": mix0, "mix1": mix1}[kind](s)
            norm(n_stages)
            for f in range(2 * TB):
                tb, half = f // 2, f % 2
                pe.wait_ge(s_xr, 8 * n_stages + 8)
                if f >= 2:
                    pe.wait_ge(s_yo2, f - 1)
                for e in range(4):
                    last = nc.tensor.transpose(ps[f % 2][:, e * P:(e + 1) * P],
                                               xf[:, 4 * half + e, tb * P:(tb + 1) * P], ident)
                last.then_inc(s_yT, 1)


_INS = ['x_prompt', 'x_sample', 'cache_k', 'cache_v', 'state_hgrn', 'c', 'c_ctx', 'ada_w', 'ada_b', 'norm_g',
        'ffn_w1', 'ffn_w2', 'mix0_w_in', 'mix0_w_out', 'na_rpb', 'mix1_w_in', 'mix1_w_out',
        'hg_lb_logits', 'hg_norm_g', 'norm_f']
_OUTS = [(1, NP_, D), (1, NS_, D), (1, 1, NP_, HEADS, HD), (1, 1, NP_, HEADS, HD), (1, 1, 2, HG_HEADS, P, P)]


def kernel(**inputs):
    import concourse.bacc as bacc
    from concourse.bass_utils import run_bass_kernel_spmd as run

    nc = bacc.Bacc("TRN2", target_bir_lowering=False, num_devices=1)
    arrays, args = {}, []
    given = {name: np.ascontiguousarray(inputs[name]) for name in _INS}
    given["consts"] = shape_constants()
    for name, a in given.items():
        arrays[f"in_{name}"] = a
        args.append(nc.dram_tensor(f"in_{name}", a.shape, mybir.dt.from_np(a.dtype), kind="ExternalInput").ap())
    for i, shape in enumerate(_OUTS):
        args.append(nc.dram_tensor(f"out_{i}", shape, F32, kind="ExternalOutput").ap())
    build(nc, *args)
    r = run(nc, [arrays], core_ids=[0])
    return tuple(r.results[0][f"out_{i}"] for i in range(len(_OUTS)))
```
